# Optimizing a Trainium2 kernel written in Bass

```python
import math
import jax, jax.numpy as jnp
from jax import lax
import numpy as np

D_MODEL = 1024
BATCH = 1
SEQ = 256
DEPTH = 2

GRID_W = 64
CTX_LEN = 256
N_MIXERS = 3
D_FF = 2816
N_MOD = 9
EPS = 1e-6

SSD_D_INNER = 2 * D_MODEL
SSD_HEAD_DIM = 64
SSD_N_HEADS = SSD_D_INNER // SSD_HEAD_DIM
SSD_N_GROUPS = 4
SSD_D_STATE = 128
SSD_CONV_W = 5
SSD_CHUNK = 128
SSD_GN = SSD_N_GROUPS * SSD_D_STATE
SSD_CONV_DIM = SSD_D_INNER + 2 * SSD_GN
SSD_IN_DIM = SSD_D_INNER + SSD_CONV_DIM + 2 * SSD_N_HEADS

POOL_WINDOWS = (2, 4, 8, 16)
POOL_GROUPS = 4
POOL_GROUP_DIM = D_MODEL // POOL_GROUPS

HY_ORDER = 2
HY_SHORT_W = 3
HY_EMB_DIM = 33
HY_BANDS = (HY_EMB_DIM - 1) // 2
HY_FILTER_HIDDEN = 64
HY_MAX_DECAY = math.log(1e-2) / 0.3
HY_MIN_DECAY = math.log(1e-2) / 1.5


def rmsnorm(x, g):
    xf = x.astype(jnp.float32)
    y = xf * lax.rsqrt(jnp.mean(xf * xf, axis=-1, keepdims=True) + EPS)
    return (y * g.astype(jnp.float32)).astype(x.dtype)

def modulate(x, g, shift, scale):
    return rmsnorm(x, g) * (1 + scale) + shift

def swiglu(u, wg, wu, wd):
    return (jax.nn.silu(u @ wg) * (u @ wu)) @ wd

def dwconv_centred(u, w, b):
    K = w.shape[0]
    P = K // 2
    L = u.shape[1]
    up = jnp.pad(u, ((0, 0), (P, P), (0, 0)))
    out = b
    for k in range(K):
        out = out + w[k] * up[:, k:k + L]
    return out

def ssd_scan(x, dt, A, B, C, h0, with_output):
    b, l, H, P = x.shape
    G, N = B.shape[2], B.shape[3]
    E = H // G
    Q = SSD_CHUNK
    nc = l // Q
    xdt = (x.astype(jnp.float32) * dt[..., None]).reshape(b, nc, Q, G, E, P)
    Bc = B.astype(jnp.float32).reshape(b, nc, Q, G, N)
    Cc = C.astype(jnp.float32).reshape(b, nc, Q, G, N)
    a_cum = jnp.cumsum((dt * A).reshape(b, nc, Q, G, E), axis=2)
    a_last = a_cum[:, :, -1]
    decay_to_end = jnp.exp(a_last[:, :, None] - a_cum)
    states = jnp.einsum('bcsgn,bcsge,bcsgep->bcgepn', Bc, decay_to_end, xdt)

    def step(h, inp):
        st, al = inp
        return h * jnp.exp(al)[..., None, None] + st, h

    h_final, h_in = lax.scan(step, h0, (jnp.moveaxis(states, 1, 0), jnp.moveaxis(a_last, 1, 0)))
    if not with_output:
        return None, h_final
    h_in = jnp.moveaxis(h_in, 0, 1)
    seg = a_cum[:, :, :, None] - a_cum[:, :, None, :]
    mask = jnp.tril(jnp.ones((Q, Q), dtype=bool))[:, :, None, None]
    Lmat = jnp.exp(jnp.where(mask, seg, -jnp.inf))
    cb = jnp.einsum('bclgn,bcsgn->bclsg', Cc, Bc)
    y_diag = jnp.einsum('bclsg,bclsge,bcsgep->bclgep', cb, Lmat, xdt)
    y_off = jnp.einsum('bclgn,bcgepn,bclge->bclgep', Cc, h_in, jnp.exp(a_cum))
    y = (y_diag + y_off).reshape(b, l, H, P)
    return y.astype(x.dtype), h_final

def ssd_mixer(u_lat, u_ctx, w_in, conv_w, conv_b, a_log, dt_bias, d_skip, norm_g, w_out, need_ctx_out):
    H, P, G, N = SSD_N_HEADS, SSD_HEAD_DIM, SSD_N_GROUPS, SSD_D_STATE
    A = -jnp.exp(a_log.astype(jnp.float32))

    def project(u):
        b, l, _ = u.shape
        zxbcdt = u @ w_in
        z = zxbcdt[..., :SSD_D_INNER]
        xbc = jax.nn.silu(dwconv_centred(zxbcdt[..., SSD_D_INNER:SSD_D_INNER + SSD_CONV_DIM], conv_w, conv_b))
        dt_raw = zxbcdt[..., SSD_D_INNER + SSD_CONV_DIM:]
        xs = xbc[..., :SSD_D_INNER].reshape(b, l, H, P)
        Bm = xbc[..., SSD_D_INNER:SSD_D_INNER + SSD_GN].reshape(b, l, G, N)
        Cm = xbc[..., SSD_D_INNER + SSD_GN:].reshape(b, l, G, N)
        dt = jax.nn.softplus(dt_raw.reshape(b, l, 2, H).astype(jnp.float32) + dt_bias.astype(jnp.float32))
        return z, xs, Bm, Cm, dt

    def flip(t, d):
        return t[:, ::-1] if d == 1 else t

    zc, xc, Bc, Cc, dtc = project(u_ctx)
    zl, xl, Bl, Cl, dtl = project(u_lat)
    b = u_lat.shape[0]
    h0 = jnp.zeros((b, G, H // G, P, N), jnp.float32)
    y_lat = d_skip[:, None] * xl
    y_ctx = d_skip[:, None] * xc if need_ctx_out else None
    for d in range(2):
        yc, hc = ssd_scan(flip(xc, d), flip(dtc[:, :, d], d), A[d], flip(Bc, d), flip(Cc, d), h0, need_ctx_out)
        yl, _ = ssd_scan(flip(xl, d), flip(dtl[:, :, d], d), A[d], flip(Bl, d), flip(Cl, d), hc, True)
        y_lat = y_lat + flip(yl, d)
        if need_ctx_out:
            y_ctx = y_ctx + flip(yc, d)

    def gate_norm_out(y, z):
        b_, l_ = y.shape[:2]
        gy = (y.reshape(b_, l_, SSD_D_INNER) * jax.nn.silu(z)).reshape(b_, l_, G, SSD_D_INNER // G)
        gy = rmsnorm(gy, norm_g.reshape(G, SSD_D_INNER // G))
        return gy.reshape(b_, l_, SSD_D_INNER) @ w_out

    out_lat = gate_norm_out(y_lat, zl)
    out_ctx = gate_norm_out(y_ctx, zc) if need_ctx_out else None
    return out_lat, out_ctx

def box_sum(v, w, axis):
    L = v.shape[axis]
    cs = jnp.cumsum(v, axis=axis)
    pad = [(0, 0)] * v.ndim
    pad[axis] = (1, 0)
    cs = jnp.pad(cs, pad)
    pos = jnp.arange(L)
    hi = jnp.minimum(pos + (w - w // 2), L)
    lo = jnp.maximum(pos - w // 2, 0)
    s = jnp.take(cs, hi, axis=axis) - jnp.take(cs, lo, axis=axis)
    return s, (hi - lo).astype(jnp.float32)

def pool_grid(v, w):
    b, l, C = v.shape
    rows = l // GRID_W
    v4 = v.astype(jnp.float32).reshape(b, rows, GRID_W, C)
    s, cnt_c = box_sum(v4, w, 2)
    s, cnt_r = box_sum(s, w, 1)
    mean = s / (cnt_r[:, None, None] * cnt_c[None, :, None])
    return mean.reshape(b, l, C).astype(v.dtype) - v

def pool_seq(v, w):
    s, cnt = box_sum(v.astype(jnp.float32), w, 1)
    return (s / cnt[None, :, None]).astype(v.dtype) - v

def pool_mixer(u_lat, u_ctx, w, bias, scale, need_ctx_out):
    def mix(u, pool_fn):
        b, l, _ = u.shape
        grp = u.reshape(b, l, POOL_GROUPS, POOL_GROUP_DIM)
        pooled = jnp.stack([pool_fn(grp[:, :, g], POOL_WINDOWS[g]) for g in range(POOL_GROUPS)], axis=2)
        y = jnp.einsum('blgc,gcd->blgd', pooled, w) + bias
        return y.reshape(b, l, D_MODEL) * scale

    out_lat = mix(u_lat, pool_grid)
    out_ctx = mix(u_ctx, pool_seq) if need_ctx_out else None
    return out_lat, out_ctx

def hyena_filter_fft(L, fw1, fb1, fw2, fb2, fw3, ffreq):
    f32 = jnp.float32
    pos = jnp.arange(L, dtype=f32)
    t = jnp.linspace(0.0, 1.0, L, dtype=f32)
    wpos = 2.0 * math.pi * pos / L
    f = jnp.linspace(1e-4, HY_BANDS - 1, HY_BANDS, dtype=f32)
    ang = wpos[:, None] * f[None, :]
    z = jnp.concatenate([t[:, None], jnp.cos(ang), -jnp.sin(ang)], axis=-1)
    h = jnp.sin(ffreq[0].astype(f32) * (z @ fw1.astype(f32) + fb1.astype(f32)))
    h = jnp.sin(ffreq[1].astype(f32) * (h @ fw2.astype(f32) + fb2.astype(f32)))
    h = (h @ fw3.astype(f32)).reshape(L, HY_ORDER, 2, D_MODEL)
    deltas = jnp.abs(jnp.linspace(HY_MIN_DECAY, HY_MAX_DECAY, D_MODEL, dtype=f32))
    h = h * jnp.exp(-t[:, None, None, None] * deltas)
    h = h * lax.rsqrt(jnp.sum(h * h, axis=(0, 2), keepdims=True) + EPS)
    kern = jnp.concatenate([h[:, :, 0], jnp.zeros((1, HY_ORDER, D_MODEL), f32), h[:0:-1, :, 1]], axis=0)
    return jnp.fft.rfft(kern, axis=0)

def fftconv(u, kf, bias):
    L = u.shape[1]
    uf = u.astype(jnp.float32)
    y = jnp.fft.irfft(jnp.fft.rfft(uf, n=2 * L, axis=1) * kf, n=2 * L, axis=1)[:, :L]
    return (y + uf * bias.astype(jnp.float32)).astype(u.dtype)

def hyena_mixer(u_lat, u_ctx, w_in, conv_w, conv_b, fw1, fb1, fw2, fb2, fw3, ffreq, hbias, w_out, need_ctx_out):
    def run(u):
        kf = hyena_filter_fft(u.shape[1], fw1, fb1, fw2, fb2, fw3, ffreq)
        p = dwconv_centred(u @ w_in, conv_w, conv_b)
        v, x1, x2 = jnp.split(p, 3, axis=-1)
        z = x1 * fftconv(v, kf[:, 0], hbias[0])
        y = x2 * fftconv(z, kf[:, 1], hbias[1])
        return y @ w_out

    out_lat = run(u_lat)
    out_ctx = run(u_ctx) if need_ctx_out else None
    return out_lat, out_ctx

def n_layers_of(kind):
    return len(range(kind, DEPTH, N_MIXERS))

def first_inputs(seed: int = 0) -> dict:
    key = jax.random.key(seed)
    ks = jax.random.split(key, 32)
    f32 = jnp.float32

    def nrm(k, shape, scale):
        return jax.random.normal(k, shape, f32) * scale

    nA, nB, nC = n_layers_of(0), n_layers_of(1), n_layers_of(2)
    D, F = D_MODEL, D_FF
    H = SSD_N_HEADS
    dt0 = jnp.exp(jax.random.uniform(ks[12], (nA, 2, H), f32, math.log(1e-3), math.log(1e-1)))
    return {
        "x": nrm(ks[0], (BATCH, SEQ, D), 1.0),
        "c": nrm(ks[1], (BATCH, D), 1.0),
        "ctx": nrm(ks[2], (BATCH, CTX_LEN, D), 1.0),
        "c_ctx": nrm(ks[3], (D,), 1.0),
        "ada_w": nrm(ks[4], (DEPTH, D, N_MOD * D), 0.5 * D ** -0.5),
        "ada_b": nrm(ks[5], (DEPTH, N_MOD * D), 0.02),
        "norm_g": 1.0 + nrm(ks[6], (DEPTH, 3, D), 0.05),
        "ffn_w_gate": nrm(ks[7], (DEPTH, 2, D, F), D ** -0.5),
        "ffn_w_up": nrm(ks[8], (DEPTH, 2, D, F), D ** -0.5),
        "ffn_w_down": nrm(ks[9], (DEPTH, 2, F, D), F ** -0.5),
        "ssd_w_in": nrm(ks[10], (nA, D, SSD_IN_DIM), D ** -0.5),
        "ssd_conv_w": nrm(ks[11], (nA, SSD_CONV_W, SSD_CONV_DIM), SSD_CONV_W ** -0.5),
        "ssd_conv_b": nrm(ks[13], (nA, SSD_CONV_DIM), 0.02),
        "ssd_a_log": jnp.log(jax.random.uniform(ks[14], (nA, 2, H), f32, 1.0, 16.0)),
        "ssd_dt_bias": dt0 + jnp.log(-jnp.expm1(-dt0)),
        "ssd_d": 1.0 + nrm(ks[15], (nA, H), 0.1),
        "ssd_norm_g": 1.0 + nrm(ks[16], (nA, SSD_D_INNER), 0.05),
        "ssd_w_out": nrm(ks[17], (nA, SSD_D_INNER, D), SSD_D_INNER ** -0.5),
        "pool_w": nrm(ks[18], (nB, POOL_GROUPS, POOL_GROUP_DIM, POOL_GROUP_DIM), POOL_GROUP_DIM ** -0.5),
        "pool_b": nrm(ks[19], (nB, POOL_GROUPS, POOL_GROUP_DIM), 0.02),
        "pool_scale": 1.0 + nrm(ks[20], (nB, D), 0.1),
        "hy_w_in": nrm(ks[21], (nC, D, 3 * D), D ** -0.5),
        "hy_conv_w": nrm(ks[22], (nC, HY_SHORT_W, 3 * D), HY_SHORT_W ** -0.5),
        "hy_conv_b": nrm(ks[23], (nC, 3 * D), 0.02),
        "hy_filt_w1": nrm(ks[24], (nC, HY_EMB_DIM, HY_FILTER_HIDDEN), HY_EMB_DIM ** -0.5),
        "hy_filt_b1": nrm(ks[25], (nC, HY_FILTER_HIDDEN), 0.1),
        "hy_filt_w2": nrm(ks[26], (nC, HY_FILTER_HIDDEN, HY_FILTER_HIDDEN), HY_FILTER_HIDDEN ** -0.5),
        "hy_filt_b2": nrm(ks[27], (nC, HY_FILTER_HIDDEN), 0.1),
        "hy_filt_w3": nrm(ks[28], (nC, HY_FILTER_HIDDEN, HY_ORDER * 2 * D), HY_FILTER_HIDDEN ** -0.5),
        "hy_filt_freq": 1.0 + nrm(ks[29], (nC, 2, HY_FILTER_HIDDEN), 0.1),
        "hy_bias": nrm(ks[30], (nC, HY_ORDER, D), 0.1),
        "hy_w_out": nrm(ks[31], (nC, D, D), D ** -0.5),
        "final_g": 1.0 + nrm(jax.random.fold_in(key, 99), (D,), 0.05),
    }

def first_block(x, c, ctx, c_ctx, ada_w, ada_b, norm_g, ffn_w_gate, ffn_w_up, ffn_w_down,
              ssd_w_in, ssd_conv_w, ssd_conv_b, ssd_a_log, ssd_dt_bias, ssd_d, ssd_norm_g, ssd_w_out,
              pool_w, pool_b, pool_scale,
              hy_w_in, hy_conv_w, hy_conv_b, hy_filt_w1, hy_filt_b1, hy_filt_w2, hy_filt_b2, hy_filt_w3,
              hy_filt_freq, hy_bias, hy_w_out, final_g):
    h = ctx
    sc = jax.nn.silu(c)
    scc = jax.nn.silu(c_ctx)
    for i in range(DEPTH):
        kind = i % N_MIXERS
        j = i // N_MIXERS
        last = i == DEPTH - 1
        ctx_in_needed = (not last) or kind == 0
        m = (sc @ ada_w[i] + ada_b[i]).reshape(-1, N_MOD, D_MODEL)[:, :, None, :]
        mc = (scc @ ada_w[i] + ada_b[i]).reshape(N_MOD, D_MODEL)[:, None, None, :]

        x = x + 0.5 * m[:, 2] * swiglu(modulate(x, norm_g[i, 0], m[:, 0], m[:, 1]),
                                       ffn_w_gate[i, 0], ffn_w_up[i, 0], ffn_w_down[i, 0])
        if ctx_in_needed:
            h = h + 0.5 * mc[2] * swiglu(modulate(h, norm_g[i, 0], mc[0], mc[1]),
                                         ffn_w_gate[i, 0], ffn_w_up[i, 0], ffn_w_down[i, 0])

        u = modulate(x, norm_g[i, 1], m[:, 3], m[:, 4])
        uc = modulate(h, norm_g[i, 1], mc[3], mc[4]) if ctx_in_needed else None
        if kind == 0:
            y, yc = ssd_mixer(u, uc, ssd_w_in[j], ssd_conv_w[j], ssd_conv_b[j], ssd_a_log[j], ssd_dt_bias[j],
                              ssd_d[j], ssd_norm_g[j], ssd_w_out[j], not last)
        elif kind == 1:
            y, yc = pool_mixer(u, uc, pool_w[j], pool_b[j], pool_scale[j], not last)
        else:
            y, yc = hyena_mixer(u, uc, hy_w_in[j], hy_conv_w[j], hy_conv_b[j], hy_filt_w1[j], hy_filt_b1[j],
                                hy_filt_w2[j], hy_filt_b2[j], hy_filt_w3[j], hy_filt_freq[j], hy_bias[j],
                                hy_w_out[j], not last)
        x = x + m[:, 5] * y
        if not last:
            h = h + mc[5] * yc

        x = x + 0.5 * m[:, 8] * swiglu(modulate(x, norm_g[i, 2], m[:, 6], m[:, 7]),
                                       ffn_w_gate[i, 1], ffn_w_up[i, 1], ffn_w_down[i, 1])
        if not last:
            h = h + 0.5 * mc[8] * swiglu(modulate(h, norm_g[i, 2], mc[6], mc[7]),
                                         ffn_w_gate[i, 1], ffn_w_up[i, 1], ffn_w_down[i, 1])
    return rmsnorm(x, final_g)


D_MIX = D_MODEL
HEAD_DIM = 64
N_Q_HEADS = 8
N_KV_HEADS = 2
GQA_GROUP = N_Q_HEADS // N_KV_HEADS
D_ATTN = N_Q_HEADS * HEAD_DIM
D_KV = N_KV_HEADS * HEAD_DIM
WINDOW = 128
ATT_BLOCK = 128
N_BUCKETS = 32
MAX_DISTANCE = 128
D_CONV = D_MIX // 4
CONV_WIDTH = 3
D_SGU = D_MIX // 4
SGU_GROUPS = 4
SGU_GROUP_DIM = D_SGU // SGU_GROUPS
SGU_CHUNK = 128
IN_SPLITS = (D_ATTN, D_KV, D_KV, D_CONV, D_CONV, D_CONV, D_SGU, D_SGU)
D_IN = D_ATTN + 2 * D_KV + 3 * D_CONV + 2 * D_SGU
PEER_HEADS = 8
PEER_TOPK = 16
N_KEYS = 128
N_EXPERTS = N_KEYS * N_KEYS
PEER_QDIM = 256
PEER_HALF = PEER_QDIM // 2
PEER_TOKEN_BLOCK = 128
NEG_INF = -1e30


def rms_norm(x, g):
    xf = x.astype(jnp.float32)
    y = xf * lax.rsqrt(jnp.mean(xf * xf, axis=-1, keepdims=True) + EPS)
    return (y * g.astype(jnp.float32)).astype(x.dtype)

def t5_causal_bucket(dist):
    max_exact = N_BUCKETS // 2
    d = jnp.maximum(dist, 0)
    log_ratio = jnp.log(jnp.maximum(d, 1).astype(jnp.float32) / max_exact) / math.log(MAX_DISTANCE / max_exact)
    large = max_exact + (log_ratio * (N_BUCKETS - max_exact)).astype(jnp.int32)
    large = jnp.minimum(large, N_BUCKETS - 1)
    return jnp.where(d < max_exact, d, large)

def sliding_window_attention(q, k, v, sink, rel_bias):
    B, S = q.shape[0], q.shape[1]
    nb = S // ATT_BLOCK
    qb = q.reshape(B, nb, ATT_BLOCK, N_KV_HEADS, GQA_GROUP, HEAD_DIM)
    kb = k.reshape(B, nb, ATT_BLOCK, N_KV_HEADS, HEAD_DIM)
    vb = v.reshape(B, nb, ATT_BLOCK, N_KV_HEADS, HEAD_DIM)

    def with_prev(t):
        prev = jnp.pad(t[:, :-1], ((0, 0), (1, 0), (0, 0), (0, 0), (0, 0)))
        return jnp.concatenate([prev, t], axis=2)

    kw, vw = with_prev(kb), with_prev(vb)
    logits = jnp.einsum('bnqkgd,bnskd->bnkgqs', qb, kw,
                        preferred_element_type=jnp.float32) * (HEAD_DIM ** -0.5)
    q_idx = jnp.arange(ATT_BLOCK)[:, None]
    s_idx = jnp.arange(2 * ATT_BLOCK)[None, :]
    dist = q_idx + ATT_BLOCK - s_idx
    in_window = (dist >= 0) & (dist < WINDOW)
    blk = jnp.arange(nb)[:, None, None]
    key_exists = (blk * ATT_BLOCK + s_idx[None] - ATT_BLOCK) >= 0
    mask = in_window[None] & key_exists
    bias = rel_bias.astype(jnp.float32)[t5_causal_bucket(dist)]
    bias = bias.transpose(2, 0, 1).reshape(N_KV_HEADS, GQA_GROUP, ATT_BLOCK, 2 * ATT_BLOCK)
    logits = jnp.where(mask[None, :, None, None], logits + bias, NEG_INF)
    sink_l = sink.astype(jnp.float32).reshape(1, 1, N_KV_HEADS, GQA_GROUP, 1, 1)
    m = jnp.maximum(jnp.max(logits, axis=-1, keepdims=True), sink_l)
    p = jnp.exp(logits - m)
    p = p / (jnp.sum(p, axis=-1, keepdims=True) + jnp.exp(sink_l - m))
    out = jnp.einsum('bnkgqs,bnskd->bnqkgd', p.astype(v.dtype), vw)
    return out.reshape(B, S, D_ATTN)

def short_conv_mixer(b_gate, c_gate, h, conv_w):
    S = h.shape[1]
    z = c_gate * h
    zp = jnp.pad(z, ((0, 0), (CONV_WIDTH - 1, 0), (0, 0)))
    conv = zp[:, 0:S] * conv_w[0]
    for j in range(1, CONV_WIDTH):
        conv = conv + zp[:, j:j + S] * conv_w[j]
    return b_gate * conv

def chunked_spatial_gating(u, v, w_s, b_s):
    B, S = u.shape[0], u.shape[1]
    nc = S // SGU_CHUNK
    vf = v.astype(jnp.float32).reshape(B, S, SGU_GROUPS, SGU_GROUP_DIM)
    mu = jnp.mean(vf, axis=-1, keepdims=True)
    var = jnp.mean(jnp.square(vf - mu), axis=-1, keepdims=True)
    vn = ((vf - mu) * lax.rsqrt(var + EPS)).astype(v.dtype)
    vn = vn.reshape(B, nc, SGU_CHUNK, SGU_GROUPS, SGU_GROUP_DIM)
    causal = jnp.tril(jnp.ones((SGU_CHUNK, SGU_CHUNK), dtype=w_s.dtype))
    w = w_s * causal[None]
    mixed = jnp.einsum('gts,bnsgc->bntgc', w, vn) + b_s.T[None, None, :, :, None]
    return u * mixed.reshape(B, S, D_SGU)

def peer_ffn(h, w_pq, sub_keys, expert_down, expert_up):
    B, S, D = h.shape
    tokens = h.reshape(-1, PEER_TOKEN_BLOCK, D)

    def block(t):
        T = t.shape[0]
        q = (t @ w_pq).reshape(T, PEER_HEADS, 2, PEER_HALF)
        s = jnp.einsum('thpk,hpnk->thpn', q, sub_keys, preferred_element_type=jnp.float32)
        top_s, top_i = lax.top_k(s, PEER_TOPK)
        cand_s = top_s[:, :, 0, :, None] + top_s[:, :, 1, None, :]
        cand_i = top_i[:, :, 0, :, None] * N_KEYS + top_i[:, :, 1, None, :]
        best_s, best_pos = lax.top_k(cand_s.reshape(T, PEER_HEADS, PEER_TOPK * PEER_TOPK), PEER_TOPK)
        experts = jnp.take_along_axis(cand_i.reshape(T, PEER_HEADS, PEER_TOPK * PEER_TOPK), best_pos, axis=-1)
        gate = jax.nn.softmax(best_s, axis=-1)
        u = expert_down[experts]
        act = jax.nn.gelu(jnp.einsum('td,thkd->thk', t, u, preferred_element_type=jnp.float32),
                          approximate=False)
        wgt = (gate * act).astype(t.dtype)
        vv = expert_up[experts]
        return jnp.einsum('thk,thkd->td', wgt, vv)

    return lax.map(block, tokens).reshape(B, S, D)

def hybrid_layer(x, c_act, rel_bias, w_ada, b_ada, norm1_g, norm2_g, w_in, q_norm_g, k_norm_g,
                 attn_sink, conv_w, sgu_w, sgu_b, out_norm_g, w_out, peer_wq, peer_sub_keys,
                 peer_down, peer_up):
    B, S = x.shape[0], x.shape[1]
    mod = (c_act @ w_ada + b_ada)[:, None, :]
    sh1, sc1, g1, sh2, sc2, g2 = jnp.split(mod, 6, axis=-1)
    h = rms_norm(x, norm1_g) * (1 + sc1) + sh1
    proj = h @ w_in
    split_pts = [int(i) for i in np.cumsum(IN_SPLITS)[:-1]]
    q, k, v, cb, cc, ch, su, sv = jnp.split(proj, split_pts, axis=-1)
    q = rms_norm(q.reshape(B, S, N_Q_HEADS, HEAD_DIM), q_norm_g)
    k = rms_norm(k.reshape(B, S, N_KV_HEADS, HEAD_DIM), k_norm_g)
    v = v.reshape(B, S, N_KV_HEADS, HEAD_DIM)
    y_attn = sliding_window_attention(q, k, v, attn_sink, rel_bias)
    y_conv = short_conv_mixer(cb, cc, ch, conv_w)
    y_sgu = chunked_spatial_gating(su, sv, sgu_w, sgu_b)
    ga, gc, gs = jnp.split(out_norm_g, [D_ATTN, D_ATTN + D_CONV])
    merged = jnp.concatenate([rms_norm(y_attn, ga), rms_norm(y_conv, gc), rms_norm(y_sgu, gs)], axis=-1)
    x = x + g1 * (merged @ w_out)
    h2 = rms_norm(x, norm2_g) * (1 + sc2) + sh2
    x = x + g2 * peer_ffn(h2, peer_wq, peer_sub_keys, peer_down, peer_up)
    return x

def second_inputs(seed: int = 0) -> dict:
    key = jax.random.key(seed)
    ks = jax.random.split(key, 20)
    f32 = jnp.float32
    nrm = lambda k, shape, s: jax.random.normal(k, shape, f32) * s
    return {
        "x": nrm(ks[0], (BATCH, SEQ, D_MODEL), 1.0),
        "c": nrm(ks[1], (BATCH, D_MODEL), 1.0),
        "rel_bias": nrm(ks[2], (N_BUCKETS, N_Q_HEADS), 0.5),
        "w_ada": nrm(ks[3], (DEPTH, D_MODEL, 6 * D_MODEL), 0.5 * D_MODEL ** -0.5),
        "b_ada": nrm(ks[4], (DEPTH, 6 * D_MODEL), 0.02),
        "norm1_g": 1.0 + nrm(ks[5], (DEPTH, D_MODEL), 0.02),
        "norm2_g": 1.0 + nrm(ks[6], (DEPTH, D_MODEL), 0.02),
        "w_in": nrm(ks[7], (DEPTH, D_MODEL, D_IN), D_MODEL ** -0.5),
        "q_norm_g": 1.0 + nrm(ks[8], (DEPTH, HEAD_DIM), 0.02),
        "k_norm_g": 1.0 + nrm(ks[9], (DEPTH, HEAD_DIM), 0.02),
        "attn_sink": nrm(ks[10], (DEPTH, N_Q_HEADS), 0.5),
        "conv_w": nrm(ks[11], (DEPTH, CONV_WIDTH, D_CONV), CONV_WIDTH ** -0.5),
        "sgu_w": nrm(ks[12], (DEPTH, SGU_GROUPS, SGU_CHUNK, SGU_CHUNK), SGU_CHUNK ** -0.5),
        "sgu_b": 1.0 + nrm(ks[13], (DEPTH, SGU_GROUPS, SGU_CHUNK), 0.02),
        "out_norm_g": 1.0 + nrm(ks[14], (DEPTH, D_MIX), 0.02),
        "w_out": nrm(ks[15], (DEPTH, D_MIX, D_MODEL), D_MIX ** -0.5),
        "peer_wq": nrm(ks[16], (DEPTH, D_MODEL, PEER_HEADS * PEER_QDIM), D_MODEL ** -0.5),
        "peer_sub_keys": nrm(ks[17], (DEPTH, PEER_HEADS, 2, N_KEYS, PEER_HALF), PEER_HALF ** -0.5),
        "peer_down": nrm(ks[18], (DEPTH, N_EXPERTS, D_MODEL), D_MODEL ** -0.5),
        "peer_up": nrm(ks[19], (DEPTH, N_EXPERTS, D_MODEL), 0.5 * PEER_HEADS ** -0.5),
    }

def second_block(x, c, rel_bias, w_ada, b_ada, norm1_g, norm2_g, w_in, q_norm_g, k_norm_g, attn_sink,
              conv_w, sgu_w, sgu_b, out_norm_g, w_out, peer_wq, peer_sub_keys, peer_down, peer_up):
    c_act = jax.nn.silu(c)
    for l in range(DEPTH):
        x = hybrid_layer(x, c_act, rel_bias, w_ada[l], b_ada[l], norm1_g[l], norm2_g[l], w_in[l],
                         q_norm_g[l], k_norm_g[l], attn_sink[l], conv_w[l], sgu_w[l], sgu_b[l],
                         out_norm_g[l], w_out[l], peer_wq[l], peer_sub_keys[l], peer_down[l], peer_up[l])
    return x


def setup_inputs(seed=0):
    out = dict(first_inputs(seed))
    for name, value in second_inputs(seed + 1).items():
        if name != "x":
            out[name + "_2"] = value
    return out


def reference(
    x, c, ctx, c_ctx, ada_w, ada_b, norm_g, ffn_w_gate, ffn_w_up, ffn_w_down, ssd_w_in,
    ssd_conv_w, ssd_conv_b, ssd_a_log, ssd_dt_bias, ssd_d, ssd_norm_g, ssd_w_out, pool_w,
    pool_b, pool_scale, hy_w_in, hy_conv_w, hy_conv_b, hy_filt_w1, hy_filt_b1, hy_filt_w2,
    hy_filt_b2, hy_filt_w3, hy_filt_freq, hy_bias, hy_w_out, final_g, c_2, rel_bias_2, w_ada_2,
    b_ada_2, norm1_g_2, norm2_g_2, w_in_2, q_norm_g_2, k_norm_g_2, attn_sink_2, conv_w_2,
    sgu_w_2, sgu_b_2, out_norm_g_2, w_out_2, peer_wq_2, peer_sub_keys_2, peer_down_2, peer_up_2,
):
    x = first_block(
        x, c, ctx, c_ctx, ada_w, ada_b, norm_g, ffn_w_gate, ffn_w_up, ffn_w_down, ssd_w_in,
        ssd_conv_w, ssd_conv_b, ssd_a_log, ssd_dt_bias, ssd_d, ssd_norm_g, ssd_w_out, pool_w,
        pool_b, pool_scale, hy_w_in, hy_conv_w, hy_conv_b, hy_filt_w1, hy_filt_b1, hy_filt_w2,
        hy_filt_b2, hy_filt_w3, hy_filt_freq, hy_bias, hy_w_out, final_g,
    )
    return second_block(
        x, c_2, rel_bias_2, w_ada_2, b_ada_2, norm1_g_2, norm2_g_2, w_in_2, q_norm_g_2,
        k_norm_g_2, attn_sink_2, conv_w_2, sgu_w_2, sgu_b_2, out_norm_g_2, w_out_2, peer_wq_2,
        peer_sub_keys_2, peer_down_2, peer_up_2,
    )


_drawn_inputs = setup_inputs


def setup_inputs(seed=0):
    import zlib

    import numpy as np

    out = dict(_drawn_inputs(seed))
    spreads = {}
    factors = {'ctx': 3.204,
     'ssd_conv_b': 5.695,
     'ssd_d': 4.73,
     'ssd_norm_g': 3.448,
     'pool_b': 6.861,
     'norm1_g_2': 5.423,
     'norm2_g_2': 8.0,
     'q_norm_g_2': 8.0,
     'k_norm_g_2': 8.0,
     'attn_sink_2': 7.869,
     'sgu_b_2': 8.0,
     'out_norm_g_2': 6.158}
    for name, (base, spread) in spreads.items():
        noise = np.random.default_rng([zlib.crc32(name.encode()), seed]).standard_normal(out[name].shape)
        drawn = base * np.exp(spread * noise) if base else spread * noise
        out[name] = __import__('jax').numpy.asarray(drawn.astype(out[name].dtype))
    for name, factor in factors.items():
        out[name] = (out[name] * factor).astype(out[name].dtype)
    return out
```

```python
from contextlib import ExitStack

import concourse.bass as bass
from concourse import mybir

F32 = mybir.dt.float32
U32 = mybir.dt.uint32
ACT = mybir.ActivationFunctionType
ALU = mybir.AluOpType
AX_X = mybir.AxisListType.X

P = 128
D = 1024
KB = D // P
T = 256
TT = T // P
F = 2816
EPS = 1e-6
FFN_ITERS = F // 256
RING = 6
TILE = 2048

H, HD, G, N = 32, 64, 4, 128
D_INNER = H * HD
XB = D_INNER // P
CONV_W = 5
Q = 128
NCH = T // Q

HEADS, DH, KV = 8, 64, 2
BUCKETS, MAX_DIST, WINDOW = 32, 128, 128
NEG = -1e30
PH, TOPK, KEYS = 8, 16, 128
PICKS = PH * TOPK
SLOTS = 16

STAGES = [("ada0", 12), ("ffn0", 33), ("ffn1", 33), ("proj_ctx", 11), ("proj_lat", 21), ("ssd_out", 8), ("ffn2", 33), ("ffn3", 33), ("pool", 1), ("ffn4", 33)]
for _l in range(2):
    STAGES += [(f"w_in{_l}", 8), (f"w_out{_l}", 4), (f"wq{_l}", 8), (f"keys{_l}", 1)]
BASE, _n = {}, 0
for _name, _count in STAGES:
    BASE[_name] = _n
    _n += _count


def consumed(stage, i):
    return BASE[stage] + i + 1


ADA = [("ada_w", 0, 3, 6, 0, 2), ("ada_w", 1, 0, 6, 0, 0), ("ada_w", 1, 6, 3, 0, 0), ("w_ada2", 0, 0, 6, 2, 0), ("w_ada2", 1, 0, 6, 2, 0)]
ADA_RING = 6
ADA_STEPS = [2 * (count + also) for _, _, _, count, _, also in ADA]
ADA_FREE = max(ADA_STEPS)
ADA_TURNS = 4
ADA_BASE = [ADA_FREE + ADA_TURNS * sum(ADA_STEPS[:n]) for n in range(len(ADA) + 1)]


def ada_last(n, j):
    return sum(2 * (1 + (t < ADA[n][5])) for t in range(j + 1))


COLS = {}
_at = 0
for _name, _count in [("c", 8), ("c_ctx", 8), ("c2", 8), ("ada_b0", 72), ("ada_b1", 72), ("norm_g", 48),
                      ("conv_w", 120), ("conv_b", 24), ("ssd_ng", 16), ("ssd_d", 16), ("dt_bias", 1), ("a_log", 1),
                      ("pool_b", 8), ("pool_scale", 8), ("final_g", 8), ("ada_b2_0", 48), ("ada_b2_1", 48),
                      ("n1g", 16), ("n2g", 16), ("qg", 2), ("kg", 2), ("conv_w2", 12), ("out_g", 16)]:
    COLS[_name] = (_at, _count)
    _at += _count
N_COLS = _at

BSTEP = 384


def program(nc, A, stop=None):
    ctx = ExitStack()
    with ctx:
        def sb(name, shape, dt=F32):
            return ctx.enter_context(nc.sbuf_tensor(name, shape, dt))

        def sem(name):
            return ctx.enter_context(nc.semaphore(name))

        xT = sb("xT", [P, KB, T])
        hT = sb("hT", [P, KB, T])
        u = sb("u", [P, KB, T])
        sq = sb("sq", [P, KB, T])
        std = sb("std", [P, T])
        rstd = sb("rstd", [P, T])
        wring = sb("wring", [P, RING, TILE])
        cols = sb("cols", [P, N_COLS])
        ident = sb("ident", [P, P])
        ones = sb("ones", [P, P])
        bones = sb("bones", [P, P])
        tri = sb("tri", [P, P])
        trisuf = sb("trisuf", [P, P])
        flip = sb("flip", [P, P])
        eps = sb("eps", [P, 1])
        silu_c = sb("silu_c", [P, KB, 3])
        cpair = sb("cpair", [P, 2, 3])
        mod0 = sb("mod0", [P, 72])
        mod0c = sb("mod0c", [P, 72])
        mod1 = sb("mod1", [P, 72])
        mod2 = sb("mod2", [P, 2, 48])
        gscale = sb("gscale", [P, 16, KB])
        hgate = sb("hgate", [P, 5, KB])
        rowp = sb("rowp", [1, 2, 4, P])
        sink = sb("sink", [P, 2, HEADS])
        thr = sb("thr", [P, 2, TOPK])
        gate_in = sb("gate_in", [1, 1])
        gate_out = sb("gate_out", [1, 1])
        AREA = 27930
        arena = sb("arena", [P, AREA])
        psum = ctx.enter_context(nc.psum_tensor("psum", [P, 8, 512], F32))

        def at(off, *dims):
            n = 1
            for d in dims:
                n *= d
            assert off + n <= AREA, (off, dims)
            v = arena[:, off:off + n]
            if len(dims) == 1:
                return v
            names = "abcde"[:len(dims)]
            return v.rearrange(f"p ({' '.join(names)}) -> p {' '.join(names)}",
                               **{k: d for k, d in zip(names, dims)})

        def col(name, i, n=1):
            return cols[:, COLS[name][0] + i:COLS[name][0] + i + n]

        sg = at(0, 2, 512)
        hid = at(1024, 2, 512)
        aring = at(2048, ADA_RING, 2, D)
        asum = at(14336, 8, D)
        asum2 = at(22528, 3, D)
        arow = at(14336, 3, D)[0:2]
        xbc = at(0, 24, T)
        z = at(6144, XB, T)
        xtok = at(10240, NCH, D_INNER)
        btok = at(14336, NCH, G * N)
        xw = at(15360, 2, D_INNER)
        h_first = at(19456, 2, D_INNER)
        h_second = u[:, :, :].rearrange("p a b -> p (a b)")
        h_second_b = sq[:, :, :].rearrange("p a b -> p (a b)")
        raw = at(23552, 3, 2, T + CONV_W - 1)
        decay = at(23552, 3, 512)
        hflat = hT[:, :, :].rearrange("p a b -> p (a b)")
        eoff = hflat[:, 0:1536].rearrange("p (a b) -> p a b", a=3)
        dt64 = hflat[0:64, 1024:2048].rearrange("p (a b) -> p a b", a=4)
        da_tok = at(27160, 4, 64)
        acum = at(27416, NCH, 64)
        diff = at(27544, NCH, 64)
        eal = at(27672, NCH, 64)
        wdt = at(27800, NCH, 64)
        dtw = at(25112, 3, T)[0:64]
        exp_a = sb("exp_a", [64, 1])
        cbm = at(25112, NCH, 2, 512)
        grstd = xw[:, 0, 0:1024].rearrange("p (a b) -> p a b", a=4)
        vpad = at(0, 8, 80)
        pa = at(640, 8, 80)
        pb = at(1280, 8, 80)
        prow = at(1920, 2, 4, 64)
        psum2 = at(2432, 2, 4, 64)
        pooled = at(3072, 8, T)
        rcnt = at(5120, 4, T)
        bias_t = at(0, HEADS, T)
        sgw = at(2048, 2, 4, P)
        boh = at(3072, BSTEP)
        brow = at(3456, BSTEP)
        relx = at(3840, HEADS)
        AO = 3072
        proj = at(AO, 16, T)
        merged = at(AO + 4096, 8, T)
        kd = at(AO + 6144, KV, T)
        rs5 = at(AO + 6656, 5, T)
        vtok = at(AO + 7936, TT, P)
        prob = at(AO + 8192, HEADS, T)
        probT = at(AO + 10240, HEADS, 2, P)
        small = at(AO + 12288, 8, HEADS)
        zpad = at(AO + 12352, 2, T + 2)
        cacc = at(AO + 12868, 2, T)
        vc = at(AO + 13380, 2, T)
        vrs = at(AO + 13892, 2, T)
        vntok = at(AO + 14404, TT, T)
        ors = at(AO + 14916, 3, T)
        gq8 = at(AO + 15684, 1)
        vsq = at(AO + 15700, 2, T)
        rows = at(AO, SLOTS, D)
        qT = at(AO, 16, T)
        score = [at(AO + 4096, 16, KEYS), u[:, :, :].rearrange("p a b -> p (a b)").rearrange("p (a b) -> p a b", a=16)]
        rep = sq[:, :, :].rearrange("p a b -> p (a b)").rearrange("p (a b) -> p a b", a=16)
        rep2 = sq[:, :, :]
        cand = hT[:, :, :].rearrange("p h (a b) -> p h a b", a=TOPK)
        h2tok = at(AO + 16384, TT, D)
        yacc = at(AO + 18432, 2, D)
        ytok = h2tok
        PO = AO + 20480
        topv = at(PO, 16, TOPK)
        topf = at(PO + 256, 16, TOPK)
        dtop = at(PO + 512, 16, TOPK)
        bestv = at(PO + 768, PH, TOPK)
        posf = at(PO + 896, PICKS)
        isum = at(PO + 1024, PICKS)
        jrem = at(PO + 1152, PICKS)
        e1 = at(PO + 1280, PICKS)
        e2 = at(PO + 1408, PICKS)
        gate = at(PO + 1536, TT, PICKS)
        dots = at(PO + 1792, TT, PICKS)
        wexp = at(PO + 2048, TT, PICKS)
        dots16 = at(PO + 2304, TOPK)
        w16 = at(PO + 2320, TOPK)
        gsum = at(PO + 2336, 2, PH)
        gsub = at(PO + 2352, PH, TOPK)
        topi = sb("topi", [P, 16, TOPK], U32)
        posi = sb("posi", [P, PICKS], U32)
        eidx = sb("eidx", [P, TT, PICKS], U32)
        istage = sb("istage", [P, 2, TOPK], U32)
        ge = sq[:, :, :].rearrange("p a b -> p (a b)")
        tmp = hT[:, :, :].rearrange("p a b -> p (a b)")

        cols_in = sem("cols_in")
        x_in = sem("x_in")
        h_in_sem = sem("h_in")
        rows_in = sem("rows_in")
        weights_in = [sem(f"weights_in{i}") for i in range(RING)]
        weights_consumed = sem("weights_consumed")
        eps_set = sem("eps_set")
        bones_set = sem("bones_set")
        pool_step = sem("pool_step")
        act_step = sem("act_step")
        dve_step = sem("dve_step")
        silu_c_ready = sem("silu_c_ready")
        ada_in = [sem(f"ada_in{i}") for i in range(ADA_RING)]
        ada_step = sem("ada_step")
        cpair_set = sem("cpair_set")
        ada_summed = sem("ada_summed")
        arow_ready = sem("arow_ready")
        arow_turned = sem("arow_turned")
        mods_ready = sem("mods_ready")
        x_ready = sem("x_ready")
        h_ready = sem("h_ready")
        sq_ready = sem("sq_ready")
        ms_ready = sem("ms_ready")
        std_ready = sem("std_ready")
        un_ready = sem("un_ready")
        u_ready = sem("u_ready")
        silu_ready = sem("silu_ready")
        hid_ready = sem("hid_ready")
        proj_evicted = sem("proj_evicted")
        conv_done = sem("conv_done")
        xbc_ready = sem("xbc_ready")
        z_ready = sem("z_ready")
        tok_done = sem("tok_done")
        tok_evicted = sem("tok_evicted")
        negabs_ready = sem("negabs_ready")
        expabs_ready = sem("expabs_ready")
        dt_ready = sem("dt_ready")
        da_done = sem("da_done")
        da_evicted = sem("da_evicted")
        cum_done = sem("cum_done")
        diff_ready = sem("diff_ready")
        decay_ready = sem("decay_ready")
        xw_ready = sem("xw_ready")
        state_done = sem("state_done")
        state_added = sem("state_added")
        cb_done = sem("cb_done")
        cbm_ready = sem("cbm_ready")
        xdt_ready = sem("xdt_ready")
        bc_done = sem("bc_done")
        seg_ready = sem("seg_ready")
        expseg_ready = sem("expseg_ready")
        expbc_ready = sem("expbc_ready")
        m_ready = sem("m_ready")
        eoff_ready = sem("eoff_ready")
        y_done = sem("y_done")
        y_evicted = sem("y_evicted")
        gated_ready = sem("gated_ready")
        gsq_ready = sem("gsq_ready")
        gms_ready = sem("gms_ready")
        gstd_ready = sem("gstd_ready")
        gnorm_ready = sem("gnorm_ready")
        so_evicted = sem("so_evicted")
        pooled_ready = sem("pooled_ready")
        rcnt_in = sem("rcnt_in")
        sgw_in = sem("sgw_in")
        boh_in = sem("boh_in")
        relx_in = sem("relx_in")
        brow_done = sem("brow_done")
        brow_ready = sem("brow_ready")
        brow_out = sem("brow_out")
        bias_in = sem("bias_in")
        sgw_ready = sem("sgw_ready")
        win_evicted = sem("win_evicted")
        qksq_ready = sem("qksq_ready")
        qkms_ready = sem("qkms_ready")
        qkstd_ready = sem("qkstd_ready")
        qk_ready = sem("qk_ready")
        vt_done = sem("vt_done")
        vtok_ready = sem("vtok_ready")
        vsum_done = sem("vsum_done")
        vc_ready = sem("vc_ready")
        vsq_ready = sem("vsq_ready")
        vvar_done = sem("vvar_done")
        vstd_ready = sem("vstd_ready")
        vn_ready = sem("vn_ready")
        vnt_done = sem("vnt_done")
        vntok_ready = sem("vntok_ready")
        mix_done = sem("mix_done")
        logits_done = sem("logits_done")
        nmax_ready = sem("nmax_ready")
        pexp_ready = sem("pexp_ready")
        prob_ready = sem("prob_ready")
        probT_done = sem("probT_done")
        probT_ready = sem("probT_ready")
        pv_done = sem("pv_done")
        pv_evicted = sem("pv_evicted")
        heads_ready = sem("heads_ready")
        osq_ready = sem("osq_ready")
        oms_ready = sem("oms_ready")
        ostd_ready = sem("ostd_ready")
        merged_ready = sem("merged_ready")
        wq_evicted = sem("wq_evicted")
        h2t_done = sem("h2t_done")
        h2t_ready = sem("h2t_ready")
        keys_done = sem("keys_done")
        score_ready = sem("score_ready")
        gsub_ready = sem("gsub_ready")
        gexp_ready = sem("gexp_ready")
        eidx_ready = sem("eidx_ready")
        stage_set = sem("stage_set")
        gate_passed = sem("gate_passed")
        row_in = [sem(f"row_in{i}") for i in range(SLOTS)]
        rows_free = sem("rows_free")
        dots_saved = sem("dots_saved")
        dots_ready = sem("dots_ready")
        gelu_ready = sem("gelu_ready")
        ytok_ready = sem("ytok_ready")
        yt_done = sem("yt_done")
        out_stored = sem("out_stored")

        def modcol(m, i):
            return m[:, 8 * i:8 * i + 8]

        NORMS = [
            (xT, col("norm_g", 0, 8), modcol(mod0, 0), modcol(mod0, 1), (x_in, 16), 1),
            (hT, col("norm_g", 0, 8), modcol(mod0c, 0), modcol(mod0c, 1), (h_in_sem, 16), 1),
            (hT, col("norm_g", 8, 8), modcol(mod0c, 3), modcol(mod0c, 4), (h_ready, 1), 3),
            (xT, col("norm_g", 8, 8), modcol(mod0, 3), modcol(mod0, 4), (x_ready, 1), 3),
            (xT, col("norm_g", 16, 8), modcol(mod0, 6), modcol(mod0, 7), (x_ready, 2), 3),
            (xT, col("norm_g", 24, 8), modcol(mod1, 0), modcol(mod1, 1), (x_ready, 3), 4),
            (xT, col("norm_g", 32, 8), modcol(mod1, 3), modcol(mod1, 4), (x_ready, 4), 4),
            (xT, col("norm_g", 40, 8), modcol(mod1, 6), modcol(mod1, 7), (x_ready, 5), 5),
            (xT, None, None, None, (x_ready, 6), 0),
        ]
        for l in range(2):
            m2 = mod2[:, l, :]
            NORMS += [(xT, col("n1g", 8 * l, 8), m2[:, 0:8], m2[:, 8:16], (x_ready, 7 + 2 * l), 6 + l),
                      (xT, col("n2g", 8 * l, 8), m2[:, 24:32], m2[:, 32:40], (x_ready, 8 + 2 * l), 6 + l)]
        FINAL = 8
        FFN_NORM = [0, 1, 4, 5, 7]
        FFN_GATE = [modcol(mod0, 2), modcol(mod0c, 2), modcol(mod0, 8), modcol(mod1, 2), modcol(mod1, 8)]
        FFN_DST = [xT, hT, xT, xT, xT]

        def u_done(n):
            return 8 * (n if n <= FINAL else n - 1)

        def place(h):
            return (h % 2) * (HEADS // 2) + h // 2

        def bank(b, off=0, n=512):
            return psum[:, b, off:off + n]

        def h_state(d, second):
            if not second:
                return h_first[:, d, :]
            return h_second if d == 0 else h_second_b

        def first_chunk(d):
            return 0 if d == 0 else 1

        def xdt(c, d):
            return xw[:, d, :] if c == 0 else xtok[:, d, :]

        ADA_BANK = (5, 5, 5, 6, 7)
        BC_BANK = (0, 1, 4)

        block = ctx.enter_context(nc.Block())

        @block.sync
        def _(sp):
            loaded = [0]

            def load(src, a, b):
                n = loaded[0]
                loaded[0] += 1
                if n >= RING:
                    sp.wait_ge(weights_consumed, n - RING + 1)
                sp.dma_start(wring[:, n % RING, 0:a * b].rearrange("p (a b) -> p a b", a=a), src) \
                    .then_inc(weights_in[n % RING], 16)

            def rows_of(w):
                return w.rearrange("(k p) n -> p k n", p=P)

            def load_columns(w, count, width=256):
                v = rows_of(w)
                for i in range(count):
                    load(v[:, :, i * width:(i + 1) * width], v.shape[1], width)

            def load_ffn(n, l, f):
                gate_w, up_w, down_w = (rows_of(A[k][l, f]) for k in ("ffn_w_gate", "ffn_w_up", "ffn_w_down"))
                load(gate_w[:, :, 0:256], KB, 256)
                load(up_w[:, :, 0:256], KB, 256)
                load(gate_w[:, :, 256:512], KB, 256)
                load(up_w[:, :, 256:512], KB, 256)
                load(down_w[:, 0:2, :], 2, D)
                load(gate_w[:, :, 512:768], KB, 256)
                load(up_w[:, :, 512:768], KB, 256)
                load(down_w[:, 2:4, :], 2, D)
                name, layer, group, count, _, _ = ADA[n]
                ada = rows_of(A[name][layer])
                if n == 2:
                    sp.wait_ge(weights_consumed, consumed("ssd_out", 7))
                if n == 4:
                    sp.wait_ge(x_ready, 5)
                sp.wait_ge(ada_step, ADA_BASE[n])
                first = loaded[0]
                with sp.Fori(0, (FFN_ITERS - 3) // 2, 1) as it:
                    for j in range(6):
                        slot = (first + j) % RING
                        sp.wait_ge(weights_consumed, it * 6 + (first + j - RING + 1))
                        if j % 3 < 2:
                            src = (gate_w, up_w)[j % 3][:, :, bass.ds(it * 512 + 256 * (3 + j // 3), 256)]
                            dst = wring[:, slot, :].rearrange("p (a b) -> p a b", a=KB)
                        else:
                            src = down_w[:, bass.ds(it * 4 + 2 * (2 + j // 3), 2), :]
                            dst = wring[:, slot, :].rearrange("p (a b) -> p a b", a=2)
                        sp.dma_start(dst, src).then_inc(weights_in[slot], 16)
                        if j < count:
                            sp.wait_ge(ada_step, it * ADA_STEPS[n] + (ADA_BASE[n] - ADA_STEPS[n] + ada_last(n, j)))
                            sp.dma_start(aring[:, j], ada[:, bass.ds(it * 2, 2), (group + j) * D:(group + j + 1) * D]) \
                                .then_inc(ada_in[j], 16)
                loaded[0] += 6 * ((FFN_ITERS - 3) // 2)
                load(down_w[:, 2 * FFN_ITERS - 2:2 * FFN_ITERS, :], 2, D)

            sp.dma_start(cols[:], A["cols"]).then_inc(cols_in, 16)
            for group in range(3):
                for i in range(4):
                    load(rows_of(A["ada_w"][0])[:, 2 * i:2 * i + 2, group * D:(group + 1) * D], 2, D)
            load_ffn(0, 0, 0)
            load_ffn(1, 0, 0)
            w_ssd = rows_of(A["ssd_w_in"])
            for lat in range(2):
                load(w_ssd[:, :, 5120:5184], KB, 64)
                for i in range(12 if lat else 10):
                    load(w_ssd[:, :, 2048 + 256 * i:2304 + 256 * i], KB, 256)
                for i in range(8 if lat else 0):
                    load(w_ssd[:, :, 256 * i:256 * i + 256], KB, 256)
            load_columns(A["ssd_w_out"], 8, 128)
            load_ffn(2, 0, 1)
            load_ffn(3, 1, 0)
            load(A["pool_w"].rearrange("g (k p) n -> p (g k) n", p=P), 8, 256)
            load_ffn(4, 1, 1)
            for l in range(2):
                load_columns(A["w_in2"][l], 8)
                load_columns(A["w_out2"][l], 4)
                load_columns(A["peer_wq"][l], 8)
                load(A[f"keys{l}"], 16, KEYS)
            sp.wait_ge(x_ready, stop or 11)
            sp.dma_start(A["out"], xT[:]).then_inc(out_stored, 16)
            sp.wait_ge(out_stored, 16)

        @block.tensor
        def _(pe):
            taken = [0]

            def tile():
                n = taken[0]
                taken[0] += 1
                pe.wait_ge(weights_in[n % RING], 16 * (n // RING + 1))
                return wring[:, n % RING, :]

            def mm(out, lhsT, rhs, start, stop, shared=False):
                return nc.tensor.matmul(out, lhsT, rhs, start=start, stop=stop, skip_group_check=shared)

            def transpose(out, in_):
                return nc.tensor.transpose(out, in_, ident[0:in_.shape[0], 0:in_.shape[0]])

            def ada_rows(groups):
                for g in groups:
                    for i in range(4):
                        w = tile().rearrange("p (k n) -> p k n", k=2)
                        for k in range(2):
                            for half in range(2):
                                ins = mm(psum[0:2, 2 * g + half, :], silu_c[:, 2 * i + k, 0:2], w[:, k, half * 512:(half + 1) * 512],
                                         i == 0 and k == 0, i == 3 and k == 1)
                        ins.then_inc(weights_consumed, 1)
                pe.wait_ge(arow_ready, groups[-1] + 1)
                for g in groups:
                    for b in range(KB):
                        ins = transpose(bank(6, (KB * g + b) * 2, 2), arow[:, g, b * P:(b + 1) * P])
                ins.then_inc(arow_turned, 1)

            def ada_sums(n):
                count = ADA[n][3] + ADA[n][5]
                pe.wait_ge(ada_step, ADA_BASE[n + 1])
                for a in range(count):
                    for b in range(KB):
                        ins = mm(bank(ADA_BANK[n], KB * a + b, 1), (asum2 if n == 2 else asum)[:, a, b * P:(b + 1) * P], ones[:, 0:1], True, True)
                ins.then_inc(ada_summed, 1)

            def norm_sums(n):
                pe.wait_ge(sq_ready, n + 1)
                if n == 9:
                    pe.wait_ge(mods_ready, 7)
                for k in range(KB):
                    ins = mm(bank(7, 0, T), ones[:], sq[:, k, :], k == 0, k == KB - 1)
                ins.then_inc(ms_ready, 1)

            def ffn(n):
                base = n * FFN_ITERS
                src = u

                def half(w, out):
                    w = w.rearrange("p (k n) -> p k n", k=KB)
                    for b in range(2):
                        for k in range(KB):
                            ins = mm(out[:, b * T:(b + 1) * T], w[:, k, b * P:(b + 1) * P], src[:, k, :], k == 0, k == KB - 1)
                    ins.then_inc(weights_consumed, 1)

                def down(w, s, first, last):
                    w = w.rearrange("p (f n) -> p f n", f=2)
                    for f in range(2):
                        for d in range(KB):
                            ins = mm(bank(d // 2, (d % 2) * T, T), w[:, f, d * P:(d + 1) * P],
                                     hid[:, s, f * T:(f + 1) * T], first and f == 0 and d % 2 == 0, last and f == 1, True)
                    ins.then_inc(weights_consumed, 1)

                def slot(i):
                    return wring[:, i % RING, :]

                pe.wait_ge(u_ready, u_done(FFN_NORM[n] + 1))
                half(tile(), bank(4))
                half(tile(), bank(6))
                if n in (1, 4):
                    pe.wait_ge(mods_ready, {1: 3, 4: 6}[n])
                half(tile(), bank(5))
                half(tile(), bank(7))
                pe.wait_ge(hid_ready, base + 1)
                down(tile(), 0, True, False)
                half(tile(), bank(4))
                half(tile(), bank(6))
                pe.wait_ge(hid_ready, base + 2)
                down(tile(), 1, False, False)
                w0 = taken[0]
                with pe.Fori(0, (FFN_ITERS - 3) // 2, 1) as it:
                    for j in range(2):
                        for k in range(3):
                            i = w0 + 3 * j + k
                            if k == 2:
                                pe.wait_ge(hid_ready, it * 2 + (base + 3 + j))
                            pe.wait_ge(weights_in[i % RING], it * 16 + 16 * (i // RING + 1))
                            if k < 2:
                                half(slot(i), bank(4 + 2 * k + (1 - j)))
                            else:
                                down(slot(i), j, False, False)
                taken[0] += 6 * ((FFN_ITERS - 3) // 2)
                pe.wait_ge(hid_ready, base + FFN_ITERS)
                down(tile(), 0, False, True)

            def project(stage, i, count, evicted, before, src, kb, width):
                w = tile()[:, 0:kb * width].rearrange("p (k n) -> p k n", k=kb)
                if i >= 4:
                    pe.wait_ge(evicted, before + i - 3)
                for b in range((width + P - 1) // P):
                    m = min(P, width - b * P)
                    for k in range(kb):
                        ins = mm(psum[0:m, i % 4, b * T:(b + 1) * T], w[:, k, b * P:b * P + m], src[:, k, :],
                                 k == 0, k == kb - 1)
                ins.then_inc(weights_consumed, 1)

            pe.wait_ge(pool_step, 9)
            pe.wait_ge(bones_set, 1)
            pe.wait_ge(silu_c_ready, 3)
            ada_rows((0, 1))
            norm_sums(0)
            ada_rows((2,))
            pe.wait_ge(mods_ready, 2)
            ffn(0)
            norm_sums(1)
            ada_sums(0)
            ffn(1)

            def ssd_project(lat):
                stage = "proj_lat" if lat else "proj_ctx"
                pe.wait_ge(u_ready, u_done(4 if lat else 3))
                n = 21 if lat else 11
                for i in range(n):
                    if lat and i < 4:
                        pe.wait_ge(state_added, 4)
                    project(stage, i, n, proj_evicted, 11 * lat, u, KB, 64 if i == 0 else 256)

            def ssd_tokens(lat):
                pe.wait_ge(dt_ready, lat + 1)
                if lat:
                    pe.wait_ge(decay_ready, 2)
                for i in range(4):
                    ins = transpose(bank(6, 64 * i, 64), dt64[:, 1 + i // 2, (i % 2) * P:(i % 2) * P + P])
                ins.then_inc(da_done, 1)
                pe.wait_ge(da_evicted, lat + 1)
                for c in range(NCH):
                    for d, m in enumerate((tri, trisuf)):
                        mm(bank(6, 256 + 64 * c + 32 * d, 32), m[:], da_tok[:, 2 + c, 32 * d:32 * d + 32], True, True)
                ins = mm(bank(6, 384, 128), ones[:], da_tok[:, 2:4, :], True, True)
                ins.then_inc(cum_done, 1)
                for i in range(10):
                    g, c = i // 2, i % 2
                    pe.wait_ge(xbc_ready, (12 if lat else 0) * 1 - (2 if lat else 0) + 2 * g + 2)
                    if 10 * lat + i >= 2:
                        pe.wait_ge(tok_evicted, 10 * lat + i - 1)
                    for b in range(4):
                        ins = transpose(bank(4 + i % 2, b * P, P), xbc[:, 4 * g + b, c * P:c * P + P])
                    ins.then_inc(tok_done, 1)

            def ssd_states(k, c):
                pe.wait_ge(xw_ready, k + 1)
                if k == 0:
                    pe.wait_ge(proj_evicted, 11)
                elif k == 4:
                    pe.wait_ge(proj_evicted, 32)
                else:
                    pe.wait_ge(state_added, k)
                if k in (0, 4):
                    pe.wait_ge(tok_evicted, 10 if k == 0 else 20)
                for g in range(G):
                    ins = mm(bank(g), btok[:, c, g * N:(g + 1) * N], xw[:, k % 2, g * 512:(g + 1) * 512], True, True)
                ins.then_inc(state_done, 1)

            norm_sums(2)
            ada_sums(1)
            ssd_project(0)
            pe.wait_ge(mods_ready, 4)
            ssd_tokens(0)
            for k in range(4):
                d, i = k // 2, k % 2
                ssd_states(k, first_chunk(d) if i == 0 else 1 - first_chunk(d))
            norm_sums(3)
            ssd_project(1)
            ssd_tokens(1)
            for d in range(2):
                ssd_states(4 + d, first_chunk(d))
            pe.wait_ge(xbc_ready, 22)
            for c in range(NCH):
                for g in range(G):
                    ins = mm(bank(4 + c, g * P, P), xbc[:, 16 + g, c * P:c * P + P], xbc[:, 20 + g, c * P:c * P + P],
                             True, True)
            ins.then_inc(cb_done, 1)

            BATCHES = [(c, jb, d) for c in range(NCH) for jb in range(H // 4) for d in range(2)]

            def running_sums(b):
                c, jb, d = BATCHES[b]
                if b < 3:
                    pe.wait_ge(state_added, 6)
                    if b == 2:
                        pe.wait_ge(cbm_ready, 2)
                else:
                    pe.wait_ge(seg_ready, b - 2)
                    pe.wait_ge(expbc_ready, b - 2)
                for i in range(4):
                    h = 32 * d + 4 * jb + i
                    ins = mm(bank(BC_BANK[b % 3], i * P, P), da_tok[:, 2 + c, h:h + 1].to_broadcast([P, P]),
                             (tri, trisuf)[d][:], True, True)
                ins.then_inc(bc_done, 1)

            def outputs(b):
                c, jb, d = BATCHES[b]
                pe.wait_ge(m_ready, b + 1)
                pe.wait_ge(eoff_ready, b + 1)
                pe.wait_ge(xdt_ready, 2 * c + d + 1)
                t = c * 8 + jb
                if d == 0 and t >= 2:
                    pe.wait_ge(y_evicted, t - 1)
                state = h_state(d, c != first_chunk(d))
                for i in range(4):
                    h = 4 * jb + i
                    out = psum[64 * (h % 2):64 * (h % 2) + 64, 2 + t % 2, (i // 2) * P:(i // 2 + 1) * P]
                    mm(out, xdt(c, d)[:, h * HD:(h + 1) * HD], decay[:, b % 3, i * P:(i + 1) * P], d == 0 and i < 2, False, True)
                    ins = mm(out, state[:, h * HD:(h + 1) * HD], eoff[:, b % 3, i * P:(i + 1) * P], False, d == 1, True)
                ins.then_inc(y_done, 1)

            running_sums(0)
            running_sums(1)
            for b in range(len(BATCHES)):
                if b + 2 < len(BATCHES):
                    running_sums(b + 2)
                outputs(b)
            pe.wait_ge(y_evicted, 16)
            pe.wait_ge(gsq_ready, 1)
            for g in range(G):
                for k in range(4):
                    ins = mm(bank(g // 2, (g % 2) * T, T), ones[:], z[:, 4 * g + k, :], k == 0, k == 3)
            ins.then_inc(gms_ready, 1)
            pe.wait_ge(gnorm_ready, 1)
            pe.wait_ge(gstd_ready, 1)
            for i in range(8):
                project("ssd_out", i, 8, so_evicted, 0, xbc, 16, 128)
            norm_sums(4)
            ffn(2)
            norm_sums(5)
            ffn(3)

            norm_sums(6)
            ada_sums(2)
            ada_sums(3)
            w = tile().rearrange("p (g k n) -> p g k n", g=4, k=2)
            pe.wait_ge(pooled_ready, 4)
            for g in range(4):
                for b in range(2):
                    for k in range(2):
                        ins = mm(bank(g, b * T, T), w[:, g, k, b * P:(b + 1) * P], pooled[:, 2 * g + k, :], k == 0, k == 1)
            ins.then_inc(weights_consumed, 1)
            norm_sums(7)
            ffn(4)
            norm_sums(FINAL)
            pe.wait_ge(std_ready, FINAL + 1)
            ada_sums(4)

            pe.wait_ge(boh_in, 16)
            pe.wait_ge(relx_in, 16)
            mm(psum[0:HEADS, 6, 0:BSTEP], relx[0:BUCKETS + 1, :], boh[0:BUCKETS + 1, :], True, True) \
                .then_inc(brow_done, 1)

            for l in range(2):
                norm_sums(9 + 2 * l)
                pe.wait_ge(u_ready, u_done(10 + 2 * l))
                for i in range(8):
                    project("w_in", i, 8, win_evicted, 8 * l, u, KB, 256)
                pe.wait_ge(qksq_ready, l + 1)
                for b in range(5):
                    ins = mm(bank(4 + b // 2, (b % 2) * T, T), bones[:], sq[:, b, :], True, True)
                ins.then_inc(qkms_ready, 1)
                pe.wait_ge(win_evicted, 8 * l + 8)
                for t in range(TT):
                    ins = transpose(bank(1, t * P, P), proj[:, 5, t * P:(t + 1) * P])
                ins.then_inc(vt_done, 1)
                for b in range(2):
                    ins = mm(bank(7, b * T, T), bones[:], proj[:, 14 + b, :], True, True)
                ins.then_inc(vsum_done, 1)
                pe.wait_ge(vsq_ready, l + 1)
                for b in range(2):
                    ins = mm(bank(0, b * T, T), bones[:], vsq[:, b, :], True, True)
                ins.then_inc(vvar_done, 1)
                pe.wait_ge(vn_ready, l + 1)
                for t in range(TT):
                    for b in range(2):
                        ins = transpose(bank(7, t * T + b * P, P), vc[:, b, t * P:(t + 1) * P])
                ins.then_inc(vnt_done, 1)
                pe.wait_ge(vntok_ready, l + 1)
                pe.wait_ge(sgw_ready, 1)
                pe.wait_ge(rows_in, 32)
                pe.wait_ge(vstd_ready, l + 1)
                for t in range(TT):
                    for g in range(4):
                        out = psum[64 * (g % 2):64 * (g % 2) + 64, 0, t * T + (g // 2) * P:t * T + (g // 2 + 1) * P]
                        mm(out, vntok[:, t, g * DH:(g + 1) * DH], sgw[:, l, g, :], True, False)
                        ins = mm(out, ones[0:1, 0:DH], rowp[0:1, l, g, :], False, True)
                ins.then_inc(mix_done, 1)
                pe.wait_ge(qk_ready, l + 1)
                pe.wait_ge(bias_in, 16)
                pe.wait_ge(heads_ready, 2 * l + 1)
                pe.wait_ge(vtok_ready, l + 1)
                for n in range(TT):
                    r = 2 * l + n
                    if n:
                        pe.wait_ge(pexp_ready, r)
                    lo = P if n == 0 else 0
                    for h in range(HEADS):
                        out = bank(place(h) // 2, (place(h) % 2) * T + lo, T - lo)
                        part = slice(64 * (h % 2), 64 * (h % 2) + 64)
                        mm(out, flip[:], bias_t[:, h, lo:T], True, False)
                        ins = mm(out, proj[part, h // 2, n * P:(n + 1) * P],
                                 kd[part, h // 4, (n - 1) * P + lo:(n + 1) * P], False, True)
                    ins.then_inc(logits_done, 1)
                    pe.wait_ge(prob_ready, r + 1)
                    if n:
                        pe.wait_ge(pv_evicted, r)
                    for h in range(HEADS):
                        for s in range(lo // P, 2):
                            ins = transpose(bank(4 + h // 2, (h % 2) * T + s * P, P), prob[:, h, s * P:(s + 1) * P])
                    ins.then_inc(probT_done, 1)
                    pe.wait_ge(probT_ready, r + 1)
                    for h in range(HEADS):
                        out = psum[64 * (h % 2):64 * (h % 2) + 64, 4, (h // 2) * P:(h // 2 + 1) * P]
                        for s in range(lo // P, 2):
                            ins = mm(out, vtok[:, n - 1 + s, (h // 4) * DH:(h // 4 + 1) * DH], probT[:, place(h), s, :],
                                     s == lo // P, s == 1)
                    ins.then_inc(pv_done, 1)
                pe.wait_ge(osq_ready, l + 1)
                pe.wait_ge(pv_evicted, 2 * l + 2)
                for k in range(8):
                    g = 0 if k < 4 else 1 + (k - 4) // 2
                    ins = mm(bank(5 + g // 2, (g % 2) * T, T), ones[:], sq[:, k, :], k in (0, 4, 6), k in (3, 5, 7))
                ins.then_inc(oms_ready, 1)
                pe.wait_ge(merged_ready, l + 1)
                for i in range(4):
                    project("w_out", i, 4, None, 0, merged, KB, 256)
                norm_sums(10 + 2 * l)
                pe.wait_ge(u_ready, u_done(11 + 2 * l))
                for i in range(8):
                    project("wq", i, 8, wq_evicted, 8 * l, u, KB, 256)
                for t in range(TT):
                    for k in range(KB):
                        ins = transpose(bank(4 + 2 * t + k // 4, (k % 4) * P, P), u[:, k, t * P:(t + 1) * P])
                ins.then_inc(h2t_done, 1)
                w = tile().rearrange("p (a b) -> p a b", a=16)
                pe.wait_ge(wq_evicted, 8 * l + 8)
                pe.wait_ge(h2t_ready, l + 1)
                for t in range(TT):
                    for a in range(16):
                        ins = mm(bank(4 * t + a // 4, (a % 4) * P, P), qT[:, a, t * P:(t + 1) * P], w[:, a, :], True, True)
                    if t == 0:
                        ins.then_inc(keys_done, 1)
                ins.then_inc(weights_consumed, 1)
                pe.wait_ge(score_ready, 2 * l + 2)
                for t in range(TT):
                    pe.wait_ge(ytok_ready, 2 * l + t + 1)
                    for k in range(KB):
                        ins = transpose(bank(2 * t + k // 4, (k % 4) * P, P), ytok[:, t, k * P:(k + 1) * P])
                    ins.then_inc(yt_done, 1)

        @block.scalar
        def _(act):
            def f(out, in_, fn, **kw):
                return nc.scalar.activation(out, in_, fn, **kw)

            act.dma_start(xT[:], A["xT"]).then_inc(x_in, 16)
            act.dma_start(hT[:], A["hT"]).then_inc(h_in_sem, 16)
            act.dma_start(rowp[:], A["sgu_b"]).then_inc(rows_in, 16)
            act.dma_start(sink[:], A["sink"].unsqueeze(0).to_broadcast([P, 2, HEADS])).then_inc(rows_in, 16)
            act.wait_ge(cols_in, 16)
            f(silu_c[:, :, 0], col("c", 0, 8), ACT.Silu).then_inc(silu_c_ready, 1)
            f(silu_c[:, :, 1], col("c_ctx", 0, 8), ACT.Silu).then_inc(silu_c_ready, 1)
            f(silu_c[:, :, 2], col("c2", 0, 8), ACT.Silu).then_inc(silu_c_ready, 1)
            f(exp_a[:], cols[0:64, COLS["a_log"][0]:COLS["a_log"][0] + 1], ACT.Exp).then_inc(act_step, 1)

            def norm(n):
                src, _, shift, _, (ready, value), _ = NORMS[n]
                act.wait_ge(ready, value)
                if n:
                    act.wait_ge(ms_ready, n)
                f(sq[:], src[:], ACT.Square).then_inc(sq_ready, 1)
                act.wait_ge(ms_ready, n + 1)
                f(std[:], bank(7, 0, T), ACT.Sqrt, scale=1.0 / D, bias=eps[:, 0:1]).then_inc(std_ready, 1)
                if n == FINAL:
                    return
                for k in range(KB):
                    act.wait_ge(un_ready, u_done(n) + k + 1)
                    f(u[:, k, :], u[:, k, :], ACT.Identity, bias=shift[:, k:k + 1]).then_inc(u_ready, 1)

            def ffn(n):
                base = n * FFN_ITERS
                name = f"ffn{n}"

                def silu(i, wait_tile, wait_hid):
                    act.wait_ge(weights_consumed, wait_tile)
                    if wait_hid is not None:
                        act.wait_ge(hid_ready, wait_hid)
                    f(sg[:, i % 2, :], bank(4 + i % 2), ACT.Silu).then_inc(silu_ready, 1)

                silu(0, consumed(name, 0), None)
                silu(1, consumed(name, 2), None)
                silu(2, consumed(name, 5), base + 1)
                with act.Fori(0, (FFN_ITERS - 3) // 2, 1) as it:
                    for j in range(2):
                        silu(3 + j, it * 6 + consumed(name, 8 + 3 * j), it * 2 + (base + 2 + j))

            act.wait_ge(eps_set, 1)
            norm(0)
            ffn(0)
            norm(1)
            ffn(1)

            def ssd_project(lat):
                name = "proj_lat" if lat else "proj_ctx"
                act.wait_ge(weights_consumed, consumed(name, 0))
                if lat:
                    act.wait_ge(da_evicted, 1)
                    act.wait_ge(da_done, 1)
                f(dt64[:, 0, :], psum[0:64, 0, 0:T], ACT.Identity, bias=cols[0:64, COLS["dt_bias"][0]:COLS["dt_bias"][0] + 1]) \
                    .then_inc(proj_evicted, 1)
                nconv = 12 if lat else 10

                def silu_conv(i):
                    act.wait_ge(conv_done, 10 * lat + i + 1)
                    f(xbc[:, 2 * i:2 * i + 2, :], xbc[:, 2 * i:2 * i + 2, :], ACT.Silu).then_inc(xbc_ready, 1)

                for i in range(nconv):
                    t = 10 * lat + i
                    act.wait_ge(weights_consumed, consumed(name, 1 + i))
                    if t >= 3:
                        act.wait_ge(conv_done, t - 2)
                    f(raw[:, t % 3, :, 2:2 + T], bank((1 + i) % 4).rearrange("p (a b) -> p a b", a=2), ACT.Identity) \
                        .then_inc(proj_evicted, 1)
                    if i == 0:
                        act.wait_ge(negabs_ready, lat + 1)
                        f(dtw[:, 0, :], dtw[:, 0, :], ACT.Exp).then_inc(expabs_ready, 1)
                    if i:
                        silu_conv(i - 1)
                silu_conv(nconv - 1)
                for i in range(8 if lat else 0):
                    act.wait_ge(weights_consumed, consumed(name, 13 + i))
                    f(z[:, 2 * i:2 * i + 2, :], bank((13 + i) % 4).rearrange("p (a b) -> p a b", a=2), ACT.Silu) \
                        .then_inc(proj_evicted, 1)
                act.wait_ge(diff_ready, lat + 1)
                f(diff[:], diff[:], ACT.Exp).then_inc(decay_ready, 1)
                f(eal[:], bank(6, 384, 128).rearrange("p (a b) -> p a b", a=NCH), ACT.Exp).then_inc(decay_ready, 1)

            norm(2)
            ssd_project(0)
            norm(3)
            ssd_project(1)
            for b in range(NCH * (H // 4) * 2):
                act.wait_ge(bc_done, b + 1)
                if b >= 3:
                    act.wait_ge(y_done, b - 2)
                act.wait_ge(seg_ready, b + 1)
                f(eoff[:, b % 3, :], bank(BC_BANK[b % 3]), ACT.Exp).then_inc(expbc_ready, 1)
                f(decay[:, b % 3, :], decay[:, b % 3, :], ACT.Exp).then_inc(expseg_ready, 1)
            act.wait_ge(gated_ready, 2)
            f(z[:], xbc[:, 0:XB, :], ACT.Square).then_inc(gsq_ready, 1)
            act.wait_ge(gms_ready, 1)
            f(grstd, psum[:, 0:2, :].rearrange("p a (b c) -> p (a b) c", b=2), ACT.Sqrt, scale=1.0 / 512, bias=eps[:, 0:1]) \
                .then_inc(gstd_ready, 1)
            norm(4)
            ffn(2)
            norm(5)
            ffn(3)
            norm(6)
            norm(7)
            ffn(4)
            norm(FINAL)
            act.wait_ge(bias_in, 16)
            for l in range(2):
                norm(9 + 2 * l)
                for i in range(8):
                    act.wait_ge(weights_consumed, consumed(f"w_in{l}", i))
                    f(proj[:, 2 * i:2 * i + 2, :], bank(i % 4).rearrange("p (a b) -> p a b", a=2), ACT.Identity) \
                        .then_inc(win_evicted, 1)
                    if i == 2:
                        act.wait_ge(win_evicted, 8 * l + 3)
                        f(sq[:, 0:5, :], proj[:, 0:5, :], ACT.Square).then_inc(qksq_ready, 1)
                act.wait_ge(qkms_ready, l + 1)
                f(rs5.rearrange("p a b -> p (a b)"), psum[:, 4:7, :].rearrange("p a b -> p (a b)")[:, 0:5 * T], ACT.Sqrt,
                  scale=1.0 / DH, bias=eps[:, 0:1]).then_inc(qkstd_ready, 1)
                act.wait_ge(vc_ready, l + 1)
                f(vsq, vc, ACT.Square).then_inc(vsq_ready, 1)
                act.wait_ge(vvar_done, l + 1)
                f(vrs, bank(0).rearrange("p (a b) -> p a b", a=2), ACT.Sqrt, scale=1.0 / DH, bias=eps[:, 0:1]) \
                    .then_inc(vstd_ready, 1)
                for n in range(TT):
                    r = 2 * l + n
                    lo = P if n == 0 else 0
                    act.wait_ge(nmax_ready, r + 1)
                    if n:
                        act.wait_ge(probT_done, r)
                    for h in range(HEADS):
                        f(prob[:, h, lo:T], bank(h // 2, (h % 2) * T + lo, T - lo), ACT.Exp,
                          bias=small[:, 1, h:h + 1], accum_out=small[:, 2, h:h + 1])
                    f(small[:, 3, :], small[:, 3, :], ACT.Exp).then_inc(pexp_ready, 1)
                act.wait_ge(heads_ready, 2 * l + 2)
                act.wait_ge(pv_evicted, 2 * l + 2)
                f(sq[:], merged, ACT.Square).then_inc(osq_ready, 1)
                act.wait_ge(oms_ready, l + 1)
                f(ors[:, 0, :], bank(5, 0, T), ACT.Sqrt, scale=1.0 / 512, bias=eps[:, 0:1])
                f(ors[:, 1, :], bank(5, T, T), ACT.Sqrt, scale=1.0 / 256, bias=eps[:, 0:1])
                f(ors[:, 2, :], bank(6, 0, T), ACT.Sqrt, scale=1.0 / 256, bias=eps[:, 0:1]).then_inc(ostd_ready, 1)
                norm(10 + 2 * l)
                for i in range(8):
                    act.wait_ge(weights_consumed, consumed(f"wq{l}", i))
                    f(qT[:, 2 * i:2 * i + 2, :], bank(i % 4).rearrange("p (a b) -> p a b", a=2), ACT.Identity) \
                        .then_inc(wq_evicted, 1)
                for t in range(TT):
                    if t == 0:
                        act.wait_ge(keys_done, l + 1)
                    else:
                        act.wait_ge(weights_consumed, consumed(f"keys{l}", 0))
                    f(score[t].rearrange("p a b -> p (a b)"),
                      psum[:, 4 * t:4 * t + 4, :].rearrange("p a b -> p (a b)"), ACT.Identity).then_inc(score_ready, 1)
                for t in range(TT):
                    act.wait_ge(gsub_ready, 2 * l + t + 1)
                    f(gsub, gsub, ACT.Exp).then_inc(gexp_ready, 1)
                for t in range(TT):
                    act.wait_ge(dots_ready, 2 * l + t + 1)
                    f(wexp[:, t, :], dots[:, t, :], ACT.Gelu).then_inc(gelu_ready, 1)

        @block.vector
        def _(dve):
            steps = [0]
            v = nc.vector

            def tick(ins):
                ins.then_inc(dve_step, 1)
                steps[0] += 1
                return ins

            def settle():
                dve.wait_ge(dve_step, steps[0])

            def tt(out, a, b, op):
                return v.tensor_tensor(out, a, b, op)

            def stt(out, a, s, b, op0, op1):
                return v.scalar_tensor_tensor(out=out, in0=a, scalar=s, in1=b, op0=op0, op1=op1)

            def ts(out, a, s1, s2=None, op0=ALU.mult, op1=None):
                return v.tensor_scalar(out, a, s1, s2, op0, op1) if op1 is not None else v.tensor_scalar(out, a, s1, None, op0)

            v.memset(eps[:], EPS).then_inc(eps_set, 1)
            tick(v.memset(bones[:], 0.0))
            settle()
            tick(v.memset(bones[0:64, 0:64], 1.0))
            v.memset(bones[64:P, 64:P], 1.0).then_inc(bones_set, 1)
            v.memset(gsum[0:1, 0, 0:1], 0.0).then_inc(rows_free, SLOTS)
            v.memset(gsum[0:1, 0, 1:2], 0.0).then_inc(ada_step, ADA_FREE)

            def mods_first(groups, n):
                for g in groups:
                    dve.wait_ge(weights_consumed, consumed("ada0", 4 * g + 3))
                    v.tensor_copy(arow[:, g, :], psum[0:2, 2 * g:2 * g + 2, :].rearrange("p a b -> p (a b)")).then_inc(arow_ready, 1)
                dve.wait_ge(arow_turned, n)
                lo, hi = KB * groups[0], KB * (groups[-1] + 1)
                ps = bank(6, 0, 48).rearrange("p (a b) -> p a b", b=2)
                tick(tt(mod0[:, lo:hi], ps[:, lo:hi, 0], col("ada_b0", lo, hi - lo), ALU.add))
                tt(mod0c[:, lo:hi], ps[:, lo:hi, 1], col("ada_b0", lo, hi - lo), ALU.add).then_inc(mods_ready, 1)

            def mods(n):
                name, layer, group, count, _, also = ADA[n]
                out, b = {"ada_w": ((mod0, mod1)[layer][:], f"ada_b{layer}"), "w_ada2": (mod2[:, layer, :], f"ada_b2_{layer}")}[name]
                dve.wait_ge(ada_summed, n + 1)
                if also:
                    tick(tt(mod0c[:, KB * group:KB * (group + also)], bank(ADA_BANK[n], KB * count, KB * also), col(b, KB * group, KB * also), ALU.add))
                tt(out[:, KB * group:KB * (group + count)], bank(ADA_BANK[n], 0, KB * count), col(b, KB * group, KB * count), ALU.add) \
                    .then_inc(mods_ready, 1)

            def norm(n):
                src, g, _, scale, (ready, value), mods_count = NORMS[n]
                dve.wait_ge(ready, value)
                if n == FINAL:
                    dve.wait_ge(std_ready, n + 1)
                    dve.wait_ge(ms_ready, n + 1)
                    tick(v.reciprocal(rstd[:], std[:]))
                    settle()
                    for k in range(KB):
                        ins = stt(xT[:, k, :], xT[:, k, :], col("final_g", k), rstd[:], ALU.mult, ALU.mult)
                    ins.then_inc(x_ready, 1)
                    return
                dve.wait_ge(mods_ready, mods_count)
                tick(stt(gscale[:, n, :], scale, 1.0, g, ALU.add, ALU.mult))
                dve.wait_ge(std_ready, n + 1)
                tick(v.reciprocal(rstd[:], std[:]))
                settle()
                if n == 3:
                    dve.wait_ge(weights_consumed, consumed("proj_ctx", 10))
                for k in range(KB):
                    stt(u[:, k, :], src[:, k, :], gscale[:, n, k:k + 1], rstd[:], ALU.mult, ALU.mult).then_inc(un_ready, 1)

            def ffn(n):
                base = n * FFN_ITERS
                name = f"ffn{n}"

                def product(i, wait_tile, wait_silu, wait_down):
                    dve.wait_ge(weights_consumed, wait_tile)
                    dve.wait_ge(silu_ready, wait_silu)
                    tt(hid[:, i % 2, :], sg[:, i % 2, :], bank(6 + i % 2), ALU.mult).then_inc(hid_ready, 1)

                if n == 0:
                    dve.wait_ge(mods_ready, 2)
                tick(ts(hgate[:, n, :], FFN_GATE[n], 0.5))
                _, _, _, count, vec, also = ADA[n]
                sums = asum2 if n == 2 else asum
                tick(v.memset(sums[:, 0:count + also, :], 0.0))
                product(0, consumed(name, 1), base + 1, None)
                product(1, consumed(name, 3), base + 2, None)
                product(2, consumed(name, 6), base + 3, None)
                settle()
                if n == 0:
                    dve.wait_ge(silu_c_ready, 3)
                slot_uses = [ADA_TURNS * sum(ADA[m][3] > j for m in range(n)) for j in range(ADA_RING)]
                with dve.Fori(0, ADA_TURNS, 1) as it:
                    dve.wait_ge(ada_step, it * ADA_STEPS[n] + ADA_BASE[n])
                    v.tensor_copy(cpair[:], silu_c[:, bass.ds(it * 2, 2), :]).then_inc(cpair_set, 1)
                    dve.wait_ge(cpair_set, it + (ADA_TURNS * n + 1))
                    for j in range(2):
                        product(3 + j, it * 6 + consumed(name, 9 + 3 * j), it * 2 + (base + 4 + j), None)
                        for t in range(3 * j, min(3 * j + 3, count)):
                            dve.wait_ge(ada_in[t], it * 16 + 16 * (slot_uses[t] + 1))
                            for k in range(2):
                                for which in range(1 + (t < also)):
                                    if k and not which:
                                        dve.wait_ge(ada_step, it * ADA_STEPS[n] + (ADA_BASE[n] + ada_last(n, t) - 1 - (t < also)))
                                    dst = sums[:, count + t if which else t, :]
                                    stt(dst, aring[:, t, k, :], cpair[:, k, (1 if which else vec):(1 if which else vec) + 1], dst,
                                        ALU.mult, ALU.add).then_inc(ada_step, 1)
                dve.wait_ge(weights_consumed, consumed(name, 32))
                settle()
                dst = FFN_DST[n]
                for d in range(KB):
                    ins = stt(dst[:, d, :], bank(d // 2, (d % 2) * T, T), hgate[:, n, d:d + 1], dst[:, d, :], ALU.mult, ALU.add)
                ins.then_inc(h_ready if n == 1 else x_ready, 1)

            dve.wait_ge(cols_in, 16)
            mods_first((0, 1), 1)
            norm(0)
            mods_first((2,), 2)
            ffn(0)
            norm(1)
            mods(0)
            ffn(1)
            norm(2)
            mods(1)

            tick(v.memset(raw[:, :, :, 0:2], 0.0))
            tick(v.memset(raw[:, :, :, 2 + T:], 0.0))
            settle()

            def softplus(lat):
                val, dt, a = dt64[:, 0, :], dt64[:, 1, :], dt64[:, 2, :]
                e, r, s2 = dtw[:, 0, :], dtw[:, 1, :], dtw[:, 2, :]
                dve.wait_ge(proj_evicted, 11 * lat + 1)
                if lat:
                    dve.wait_ge(da_done, 1)
                stt(e, val, -1.0, val, ALU.mult, ALU.min).then_inc(negabs_ready, 1)
                yield
                dve.wait_ge(expabs_ready, lat + 1)
                tick(ts(r, e, 2.0, op0=ALU.add))
                settle()
                tick(v.reciprocal(r, r))
                settle()
                tick(tt(r, r, e, ALU.mult))
                settle()
                tick(tt(s2, r, r, ALU.mult))
                settle()
                tick(ts(e, s2, 1.0 / 15))
                settle()
                for odd in (13, 11, 9, 7, 5, 3):
                    tick(stt(e, e, 1.0 / odd, s2, ALU.add, ALU.mult))
                    settle()
                tick(stt(e, e, 1.0, r, ALU.add, ALU.mult))
                tick(ts(val, val, 0.0, op0=ALU.max))
                settle()
                tick(stt(dt, e, 2.0, val, ALU.mult, ALU.add))
                settle()
                dve.wait_ge(act_step, 1)
                ts(a, dt, exp_a[:, 0:1], -1.0, ALU.mult, ALU.mult).then_inc(dt_ready, 1)
                yield

            def ssd_conv(lat):
                name = "proj_lat" if lat else "proj_ctx"
                sp_steps = softplus(lat)
                next(sp_steps)
                for i in range(12 if lat else 10):
                    t = 10 * lat + i
                    dve.wait_ge(proj_evicted, 11 * lat + 2 + i)
                    if lat and i == 0:
                        dve.wait_ge(tok_done, 10)
                    for k in range(CONV_W):
                        for b in range(2):
                            blk = 2 * i + b
                            src = raw[:, t % 3, b, k:k + T]
                            w = col("conv_w", 24 * k + blk)
                            if k == 0:
                                ins = ts(xbc[:, blk, :], src, w, col("conv_b", blk), ALU.mult, ALU.add)
                            else:
                                ins = stt(xbc[:, blk, :], src, w, xbc[:, blk, :], ALU.mult, ALU.add)
                        if k < CONV_W - 1:
                            tick(ins)
                            settle()
                        else:
                            ins.then_inc(conv_done, 1)
                    if i == 1:
                        next(sp_steps)

            def sums(lat):
                dve.wait_ge(da_done, lat + 1)
                if lat:
                    settle()
                v.tensor_copy(da_tok.rearrange("p a b -> p (a b)"), bank(6, 0, 256)).then_inc(da_evicted, 1)
                dve.wait_ge(cum_done, lat + 1)
                cum = bank(6, 256, 128).rearrange("p (a b) -> p a b", a=NCH)
                tot = bank(6, 384, 128).rearrange("p (a b) -> p a b", a=NCH)
                tick(v.tensor_copy(acum, cum))
                settle()
                tt(diff, tot, acum, ALU.subtract).then_inc(diff_ready, 1)

            def tokens(lat):
                sums(lat)
                for i in range(10):
                    g, c = i // 2, i % 2
                    dve.wait_ge(tok_done, 10 * lat + i + 1)
                    dst = xtok[:, c, 512 * g:512 * g + 512] if g < 4 else btok[:, c, :]
                    v.tensor_copy(dst, bank(4 + i % 2)).then_inc(tok_evicted, 1)
                dve.wait_ge(decay_ready, 2 * lat + 2)
                dve.wait_ge(tok_evicted, 10 * lat + 10)
                dve.wait_ge(da_evicted, lat + 1)
                tick(tt(wdt, diff, da_tok[:, 0:2, :], ALU.mult))
                settle()

            def weigh(out, c, w):
                return tt(out.rearrange("p (h q) -> p h q", h=H), xtok[:, c, :].rearrange("p (h q) -> p h q", h=H),
                          w.unsqueeze(2).to_broadcast([P, H, HD]), ALU.mult)

            def heads3(a):
                return a.rearrange("p (h q) -> p h q", h=H)

            psum_state = psum[:, 0:4, :].rearrange("p a b -> p (a b)")

            def states(k, d, c, dst, src, first):
                if k >= 2:
                    dve.wait_ge(state_done, k - 1)
                weigh(xw[:, k % 2, :], c, wdt[:, c, 32 * d:32 * d + 32]).then_inc(xw_ready, 1)
                if not first:
                    tick(tt(heads3(dst), heads3(src), eal[:, c, 32 * d:32 * d + 32].unsqueeze(2).to_broadcast([P, H, HD]), ALU.mult))
                    settle()
                dve.wait_ge(state_done, k + 1)
                if first:
                    v.tensor_copy(dst, psum_state).then_inc(state_added, 1)
                else:
                    tt(dst, dst, psum_state, ALU.add).then_inc(state_added, 1)
                dve.wait_ge(state_added, k + 1)

            ssd_conv(0)
            tokens(0)
            for d in range(2):
                c0 = first_chunk(d)
                states(2 * d, d, c0, h_first[:, d, :], None, True)
                states(2 * d + 1, d, 1 - c0, h_first[:, d, :], h_first[:, d, :], False)
            norm(3)
            ssd_conv(1)
            tokens(1)
            for d in range(2):
                if d == 1:
                    dve.wait_ge(ms_ready, 4)
                states(4 + d, d, first_chunk(d), h_state(d, True), h_first[:, d, :], False)
            dve.wait_ge(cb_done, 1)
            for c in range(NCH):
                for d, m in enumerate((tri, trisuf)):
                    tt(cbm[:, c, d, :].rearrange("p (g l) -> p g l", g=G), bank(4 + c).rearrange("p (g l) -> p g l", g=G),
                       m[:, :].unsqueeze(1).to_broadcast([P, G, P]), ALU.mult).then_inc(cbm_ready, 1)
            dve.wait_ge(cbm_ready, 4)
            BATCHES = [(c, jb, d) for c in range(NCH) for jb in range(H // 4) for d in range(2)]

            def segments(b):
                c, jb, d = BATCHES[b]
                dve.wait_ge(bc_done, b + 1)
                if b >= 3:
                    dve.wait_ge(y_done, b - 2)
                for i in range(4):
                    h = 32 * d + 4 * jb + i
                    ins = ts(decay[:, b % 3, i * P:(i + 1) * P], bank(BC_BANK[b % 3], i * P, P), acum[:, c, h:h + 1], 0.0,
                             ALU.subtract, ALU.min)
                ins.then_inc(seg_ready, 1)

            def weights(b):
                c, jb, d = BATCHES[b]
                dve.wait_ge(expseg_ready, b + 1)
                g = jb // 2
                tt(decay[:, b % 3, :].rearrange("p (i l) -> p i l", i=4), decay[:, b % 3, :].rearrange("p (i l) -> p i l", i=4),
                   cbm[:, c, d, g * P:(g + 1) * P].unsqueeze(1).to_broadcast([P, 4, P]), ALU.mult).then_inc(m_ready, 1)

            def skip(b):
                c, jb, d = BATCHES[b]
                dve.wait_ge(y_done, b + 1)
                for j in range(2):
                    blk = 2 * jb + j
                    y = xbc[:, blk, c * P:(c + 1) * P]
                    ins = stt(y, y, col("ssd_d", blk), bank(2 + (c * 8 + jb) % 2, j * P, P), ALU.mult, ALU.add)
                ins.then_inc(y_evicted, 1)

            dve.wait_ge(state_done, 6)
            for c in range(NCH):
                for d in range(2):
                    if c:
                        dve.wait_ge(xdt_ready, 2 * c + d)
                    weigh(xdt(c, d), c, da_tok[:, c, 32 * d:32 * d + 32]).then_inc(xdt_ready, 1)
            for b in range(len(BATCHES)):
                segments(b)
                if b >= 3 and BATCHES[b - 3][2] == 1:
                    skip(b - 3)
                if b >= 1:
                    weights(b - 1)
            weights(31)
            skip(29)
            skip(31)
            dve.wait_ge(y_evicted, 16)
            tt(xbc[:, 0:8, :], xbc[:, 0:8, :], z[:, 0:8, :], ALU.mult).then_inc(gated_ready, 1)
            tt(xbc[:, 8:16, :], xbc[:, 8:16, :], z[:, 8:16, :], ALU.mult).then_inc(gated_ready, 1)
            dve.wait_ge(gstd_ready, 1)
            tick(v.reciprocal(grstd, grstd))
            settle()
            for k in range(XB):
                ins = stt(xbc[:, k, :], xbc[:, k, :], col("ssd_ng", k), grstd[:, k // 4, :], ALU.mult, ALU.mult)
            ins.then_inc(gnorm_ready, 1)
            for i in range(8):
                dve.wait_ge(weights_consumed, consumed("ssd_out", i))
                ins = stt(xT[:, i, :], bank(i % 4, 0, T), mod0[:, 40 + i:41 + i], xT[:, i, :], ALU.mult, ALU.add)
                if i < 7:
                    ins.then_inc(so_evicted, 1)
            ins.then_inc(x_ready, 1)
            norm(4)
            ffn(2)
            norm(5)
            ffn(3)
            norm(6)

            dve.wait_ge(u_ready, u_done(7))
            dve.wait_ge(rcnt_in, 16)
            tick(v.memset(vpad, 0.0))
            settle()
            for g in range(4):
                ug = u[:, 2 * g:2 * g + 2, :].rearrange("p a (r c) -> p (a r) c", r=4)
                tick(v.tensor_copy(vpad[:, :, 8:72], ug))
                settle()
                tick(tt(pa[:, :, 1:80], vpad[:, :, 0:79], vpad[:, :, 1:80], ALU.add))
                settle()
                cur, oth, lo, hi = pa, pb, 1, 80
                for s in (1, 2, 4)[:g]:
                    lo, hi = lo + s, hi - s
                    tick(tt(oth[:, :, lo:hi], cur[:, :, lo - s:hi - s], cur[:, :, lo + s:hi + s], ALU.add))
                    settle()
                    cur, oth = oth, cur
                cs = cur[:, :, 8:72].rearrange("p (a r) c -> p a r c", a=2)
                o = psum2
                if g == 0:
                    tick(v.tensor_copy(o[:, :, 0:1, :], cs[:, :, 0:1, :]))
                    for a in range(2):
                        tick(tt(o[:, a, 1:4, :], cs[:, a, 0:3, :], cs[:, a, 1:4, :], ALU.add))
                else:
                    for a in range(2):
                        tick(tt(prow[:, a, 0:3, :], cs[:, a, 0:3, :], cs[:, a, 1:4, :], ALU.add))
                    settle()
                    if g == 1:
                        tick(v.tensor_copy(o[:, :, 0, :], prow[:, :, 0, :]))
                        tick(tt(o[:, :, 1, :], prow[:, :, 0, :], cs[:, :, 2, :], ALU.add))
                        tick(tt(o[:, :, 2, :], prow[:, :, 0, :], prow[:, :, 2, :], ALU.add))
                        tick(tt(o[:, :, 3, :], prow[:, :, 2, :], cs[:, :, 1, :], ALU.add))
                    else:
                        for r in range(4):
                            tick(tt(o[:, :, r, :], prow[:, :, 0, :], prow[:, :, 2, :], ALU.add))
                settle()
                of = o.rearrange("p a r c -> p a (r c)")
                tick(tt(of, of, rcnt[:, g:g + 1, :].to_broadcast([P, 2, T]), ALU.mult))
                settle()
                tt(pooled[:, 2 * g:2 * g + 2, :], of, u[:, 2 * g:2 * g + 2, :], ALU.subtract).then_inc(pooled_ready, 1)
                dve.wait_ge(pooled_ready, g + 1)
            mods(2)
            mods(3)
            dve.wait_ge(weights_consumed, consumed("pool", 0))
            for k in range(KB):
                tick(ts(pooled[:, k, :], bank(k // 2, (k % 2) * T, T), col("pool_b", k), col("pool_scale", k), ALU.add, ALU.mult))
            settle()
            for k in range(KB):
                ins = stt(xT[:, k, :], pooled[:, k, :], mod1[:, 40 + k:41 + k], xT[:, k, :], ALU.mult, ALU.add)
            ins.then_inc(x_ready, 1)
            norm(7)
            ffn(4)
            norm(FINAL)
            mods(4)

            dve.wait_ge(brow_done, 1)
            v.tensor_copy(brow[0:HEADS, :], psum[0:HEADS, 6, 0:BSTEP]).then_inc(brow_ready, 1)
            dve.wait_ge(sgw_in, 16)
            tt(sgw.rearrange("p a g t -> p (a g) t"), sgw.rearrange("p a g t -> p (a g) t"),
               tri[:, :].unsqueeze(1).to_broadcast([P, 8, P]), ALU.mult).then_inc(sgw_ready, 1)

            def top16(vals, idx, src, spare, n):
                for i in range(n):
                    ins = v.max(out=vals[:, i, 0:8], in_=src[:, i, :])
                tick(ins)
                settle()
                for i in range(n):
                    v.max_index(out=idx[:, i, 0:8], in_max=vals[:, i, 0:8], in_values=src[:, i, :])
                    ins = v.match_replace(out=spare[:, i, :], in_to_replace=vals[:, i, 0:8], in_values=src[:, i, :], imm_value=-3.0e38)
                tick(ins)
                settle()
                for i in range(n):
                    ins = v.max(out=vals[:, i, 8:16], in_=spare[:, i, :])
                tick(ins)
                settle()
                for i in range(n):
                    ins = v.max_index(out=idx[:, i, 8:16], in_max=vals[:, i, 8:16], in_values=spare[:, i, :])
                tick(ins)
                settle()

            def attend(l):
                dve.wait_ge(cols_in, 16)
                tick(ts(gq8, col("qg", l), DH ** -0.5))
                dve.wait_ge(qkstd_ready, l + 1)
                tick(v.reciprocal(rs5, rs5))
                settle()
                dve.wait_ge(win_evicted, 8 * l + 8)
                for b in range(5):
                    ins = stt(proj[:, b, :], proj[:, b, :], gq8 if b < 4 else col("kg", l), rs5[:, b, :], ALU.mult, ALU.mult)
                tick(ins)
                settle()
                for kv in range(KV):
                    for half in range(2):
                        ins = v.tensor_copy(kd[64 * half:64 * half + 64, kv, :], proj[64 * kv:64 * kv + 64, 4, :])
                ins.then_inc(qk_ready, 1)
                dve.wait_ge(vt_done, l + 1)
                v.tensor_copy(vtok.rearrange("p a b -> p (a b)"), bank(1, 0, T)).then_inc(vtok_ready, 1)
                dve.wait_ge(vsum_done, l + 1)
                stt(vc, bank(7).rearrange("p (a b) -> p a b", a=2), -1.0 / DH, proj[:, 14:16, :], ALU.mult, ALU.add) \
                    .then_inc(vc_ready, 1)
                dve.wait_ge(vstd_ready, l + 1)
                tick(v.reciprocal(vrs, vrs))
                settle()
                tt(vc, vc, vrs, ALU.mult).then_inc(vn_ready, 1)
                tick(v.memset(zpad[:, :, 0:2], 0.0))
                tick(tt(zpad[:, :, 2:], proj[:, 8:10, :], proj[:, 10:12, :], ALU.mult))
                settle()
                for k in range(3):
                    for b in range(2):
                        w = col("conv_w2", 6 * l + 2 * k + b)
                        if k == 0:
                            ins = ts(cacc[:, b, :], zpad[:, b, 0:T], w)
                        else:
                            ins = stt(cacc[:, b, :], zpad[:, b, k:k + T], w, cacc[:, b, :], ALU.mult, ALU.add)
                    tick(ins)
                    settle()
                tick(tt(merged[:, 4:6, :], proj[:, 6:8, :], cacc, ALU.mult))
                dve.wait_ge(vnt_done, l + 1)
                v.tensor_copy(vntok.rearrange("p a b -> p (a b)"), bank(7)).then_inc(vntok_ready, 1)
                dve.wait_ge(mix_done, l + 1)
                for t in range(TT):
                    ins = tt(merged[:, 6:8, t * P:(t + 1) * P], proj[:, 12:14, t * P:(t + 1) * P],
                             bank(0, t * T, T).rearrange("p (a b) -> p a b", a=2), ALU.mult)
                ins.then_inc(heads_ready, 1)
                dve.wait_ge(rows_in, 32)
                mx, nm, rsum, es, den = (small[:, i, :] for i in range(5))
                for n in range(TT):
                    r = 2 * l + n
                    lo = P if n == 0 else 0
                    dve.wait_ge(logits_done, r + 1)
                    logits = psum[:, 0:4, :].rearrange("p a (b s) -> p (a b) s", b=2)[:, :, lo:T]
                    tick(v.tensor_reduce(mx, logits, AX_X, ALU.max))
                    settle()
                    tick(tt(mx, mx, sink[:, l, :], ALU.max))
                    settle()
                    tick(ts(nm, mx, -1.0))
                    settle()
                    tt(es, sink[:, l, :], nm, ALU.add).then_inc(nmax_ready, 1)
                    dve.wait_ge(pexp_ready, r + 1)
                    tick(tt(den, rsum, es, ALU.add))
                    settle()
                    tick(v.reciprocal(den, den))
                    settle()
                    tt(prob[:, :, lo:T], prob[:, :, lo:T], den.unsqueeze(2).to_broadcast([P, HEADS, T - lo]), ALU.mult) \
                        .then_inc(prob_ready, 1)
                    dve.wait_ge(probT_done, r + 1)
                    s0 = lo // P
                    v.tensor_copy(probT[:, :, s0:2, :].rearrange("p h s q -> p h (s q)"),
                                  psum[:, 4:8, :].rearrange("p a (b s) -> p (a b) s", b=2)[:, :, lo:T]).then_inc(probT_ready, 1)
                    dve.wait_ge(pv_done, r + 1)
                    v.tensor_copy(merged[:, 0:4, n * P:(n + 1) * P], bank(4).rearrange("p (a b) -> p a b", a=4)).then_inc(pv_evicted, 1)
                v.memset(gsum[:, 0, :], 0.0).then_inc(heads_ready, 1)
                dve.wait_ge(ostd_ready, l + 1)
                tick(v.reciprocal(ors, ors))
                settle()
                dve.wait_ge(pv_evicted, 2 * l + 2)
                for k in range(8):
                    g = 0 if k < 4 else 1 + (k - 4) // 2
                    ins = stt(merged[:, k, :], merged[:, k, :], col("out_g", 8 * l + k), ors[:, g, :], ALU.mult, ALU.mult)
                ins.then_inc(merged_ready, 1)
                for i in range(4):
                    dve.wait_ge(weights_consumed, consumed(f"w_out{l}", i))
                    for b in range(2):
                        k = 2 * i + b
                        ins = stt(xT[:, k, :], bank(i, b * T, T), mod2[:, l, 16 + k:17 + k], xT[:, k, :], ALU.mult, ALU.add)
                ins.then_inc(x_ready, 1)

            def candidates(l, t):
                dve.wait_ge(score_ready, 2 * l + t + 1)
                top16(topv, topi, score[t], rep, 16)
                tick(v.tensor_copy(topf, topi[:]))
                tv = topv.rearrange("p (h two) k -> p h two k", two=2)
                tick(tt(cand, tv[:, :, 0, :].unsqueeze(3).to_broadcast([P, PH, TOPK, TOPK]),
                        tv[:, :, 1, :].unsqueeze(2).to_broadcast([P, PH, TOPK, TOPK]), ALU.add))
                settle()
                tick(v.tensor_copy(dtop[:, :, 0:1], topf[:, :, 0:1]))
                tick(tt(dtop[:, :, 1:], topf[:, :, 1:], topf[:, :, 0:TOPK - 1], ALU.subtract))
                settle()

            def choose(l, t):
                top16(bestv, posi[:].rearrange("p (h k) -> p h k", h=PH), cand.rearrange("p h a b -> p h (a b)"), rep2, PH)
                tt(gsub, bestv, bestv[:, :, 0:1].to_broadcast([P, PH, TOPK]), ALU.subtract).then_inc(gsub_ready, 1)
                tick(v.tensor_copy(posf, posi[:]))
                settle()
                geb = ge.rearrange("p (a m) -> p a m", m=TOPK)
                ge4 = ge.rearrange("p (h k m) -> p h k m", h=PH, k=TOPK)
                tmpb = tmp.rearrange("p (a m) -> p a m", m=TOPK)
                tmp4 = tmp.rearrange("p (h k m) -> p h k m", h=PH, k=TOPK)
                dt4 = dtop.rearrange("p (h two) m -> p h two m", two=2)
                for half, (where, found) in enumerate(((posf, e1), (jrem, e2))):
                    tick(tt(geb, where.unsqueeze(2).to_broadcast([P, PICKS, TOPK]),
                            thr[:, half:half + 1, :].to_broadcast([P, PICKS, TOPK]), ALU.is_ge))
                    settle()
                    if half == 0:
                        tick(v.tensor_reduce(isum, geb, AX_X, ALU.add))
                    tick(tt(tmp4, ge4, dt4[:, :, half, :].unsqueeze(2).to_broadcast([P, PH, TOPK, TOPK]), ALU.mult))
                    settle()
                    tick(v.tensor_reduce(found, tmpb, AX_X, ALU.add))
                    if half == 0:
                        tick(stt(jrem, isum, -float(TOPK), posf, ALU.mult, ALU.add))
                    settle()
                tick(stt(e1, e1, float(KEYS), e2, ALU.mult, ALU.add))
                settle()
                v.tensor_copy(eidx[:, t, :], e1).then_inc(eidx_ready, 1)
                dve.wait_ge(gexp_ready, 2 * l + t + 1)
                tick(v.tensor_reduce(gsum[:, 0, :], gsub, AX_X, ALU.add))
                settle()
                tick(v.reciprocal(gsum[:, 1, :], gsum[:, 0, :]))
                settle()
                tick(tt(gate[:, t, :].rearrange("p (h k) -> p h k", h=PH), gsub,
                        gsum[:, 1, :].unsqueeze(2).to_broadcast([P, PH, TOPK]), ALU.mult))
                settle()

            def expert_dots(l, t, first, last):
                head0 = 32 * l + 8 * t + first
                with dve.Fori(0, last - first, 1) as it:
                    for j in range(TOPK):
                        dve.wait_ge(row_in[j], it * 16 + 16 * (head0 + 1))
                        v.tensor_tensor_reduce(out=rows[:, j, :], in0=rows[:, j, :], in1=h2tok[:, t, :], scale=1.0, scalar=0.0,
                                               op0=ALU.mult, op1=ALU.add, accum_out=dots16[:, j:j + 1]).then_inc(rows_free, 1)
                    dve.wait_ge(rows_free, it * TOPK + (SLOTS + TOPK * (head0 + 1)))
                    v.tensor_copy(dots[:, t, bass.ds(it * TOPK + first * TOPK, TOPK)], dots16).then_inc(dots_saved, 1)
                    dve.wait_ge(dots_saved, it + (head0 + 1))
                if last == PH:
                    v.memset(gsum[:, 0, :], 0.0).then_inc(dots_ready, 1)

            def expert_sum(l, t):
                head0 = 32 * l + 16 + 8 * t
                dve.wait_ge(gelu_ready, 2 * l + t + 1)
                tick(tt(wexp[:, t, :], wexp[:, t, :], gate[:, t, :], ALU.mult))
                tick(v.memset(yacc, 0.0))
                settle()
                with dve.Fori(0, PH, 1) as it:
                    v.tensor_copy(w16, wexp[:, t, bass.ds(it * TOPK, TOPK)]).then_inc(dots_saved, 1)
                    dve.wait_ge(dots_saved, it + (32 * l + 16 + 8 * t + 1))
                    for j in range(TOPK):
                        dve.wait_ge(row_in[j], it * 16 + 16 * (head0 + 1))
                        dve.wait_ge(rows_free, it * TOPK + (SLOTS + TOPK * head0 + j - 1))
                        stt(yacc[:, j % 2, :], rows[:, j, :], w16[:, j:j + 1], yacc[:, j % 2, :], ALU.mult, ALU.add) \
                            .then_inc(rows_free, 1)
                    dve.wait_ge(rows_free, it * TOPK + (SLOTS + TOPK * (head0 + 1)))
                tt(ytok[:, t, :], yacc[:, 0, :], yacc[:, 1, :], ALU.add).then_inc(ytok_ready, 1)
                dve.wait_ge(ytok_ready, 2 * l + t + 1)

            for l in range(2):
                norm(9 + 2 * l)
                attend(l)
                norm(10 + 2 * l)
                dve.wait_ge(h2t_done, l + 1)
                v.tensor_copy(h2tok.rearrange("p a b -> p (a b)"), psum[:, 4:8, :].rearrange("p a b -> p (a b)")).then_inc(h2t_ready, 1)
                candidates(l, 0)
                choose(l, 0)
                candidates(l, 1)
                expert_dots(l, 0, 0, PH // 2)
                choose(l, 1)
                expert_dots(l, 0, PH // 2, PH)
                expert_dots(l, 1, 0, PH)
                for t in range(TT):
                    expert_sum(l, t)
                for t in range(TT):
                    dve.wait_ge(yt_done, 2 * l + t + 1)
                    for k in range(KB):
                        ins = stt(xT[:, k, t * P:(t + 1) * P], bank(2 * t + k // 4, (k % 4) * P, P), mod2[:, l, 40 + k:41 + k],
                                  xT[:, k, t * P:(t + 1) * P], ALU.mult, ALU.add)
                ins.then_inc(x_ready, 1)

        @block.gpsimd
        def _(pool):
            g = nc.gpsimd
            done = [0]

            def each(ins):
                ins.then_inc(pool_step, 1)
                done[0] += 1
                pool.wait_ge(pool_step, done[0])

            each(g.memset(ones[:], 1.0))
            for m, start, op, base, step, mult in ((ident, 0.0, ALU.not_equal, 0, -1, 1), (flip, 0.0, ALU.not_equal, 1 - P, 1, 1),
                                                   (tri, 1.0, ALU.is_ge, 0, 1, -1), (trisuf, 1.0, ALU.is_ge, 0, -1, 1)):
                each(g.memset(m[:], start))
                each(g.affine_select(out=m[:], in_=m[:], compare_op=op, fill=1.0 - start, base=base, pattern=[[step, P]],
                                     channel_multiplier=mult))
            for i, (step, base) in enumerate(((TOPK, 0), (1, -TOPK))):
                each(g.iota(thr[:, i, :], pattern=[[step, TOPK]], base=base, channel_multiplier=0,
                            allow_small_or_imprecise_dtypes=True))
            each(g.memset(gate_in[:], 0.0))

            for b in range(NCH * (H // 4) * 2):
                c, jb = b // 16, (b // 2) % 8
                pool.wait_ge(expbc_ready, b + 1)
                e = eoff[:, b % 3, :].rearrange("p (i l) -> p i l", i=4)
                g.tensor_tensor(e, e, xbc[:, 20 + jb // 2, c * P:(c + 1) * P].unsqueeze(1).to_broadcast([P, 4, P]), ALU.mult) \
                    .then_inc(eoff_ready, 1)

            pool.wait_ge(x_ready, 4)
            pool.dma_start(rcnt, A["rcnt"].unsqueeze(0).to_broadcast([P, 4, T])).then_inc(rcnt_in, 16)
            pool.wait_ge(x_ready, 7)
            pool.dma_start(sgw, A["sgu_w"]).then_inc(sgw_in, 16)
            pool.dma_start(boh[0:BUCKETS + 1, :], A["bias_onehot"]).then_inc(boh_in, 16)
            pool.dma_start(relx[0:BUCKETS + 1, :], A["rel_bias"]).then_inc(relx_in, 16)
            pool.wait_ge(brow_ready, 1)
            pool.dma_start(A["bias_scratch"], brow[0:HEADS, :]).then_inc(brow_out, 16)
            pool.wait_ge(brow_out, 16)
            pool.dma_start(bias_t, bass.AP(A["bias_scratch"].tensor, 0, [[1, P], [BSTEP, HEADS], [1, T]])).then_inc(bias_in, 16)

            def gather(l, table, t, phase):
                head0 = 32 * l + 8 * phase
                pool.wait_ge(eidx_ready, 2 * l + t + 1)
                pool.wait_ge(weights_consumed, consumed(f"keys{l}", 0))
                with pool.Fori(0, PH // 2, 1) as it:
                    for hh in range(2):
                        g.tensor_copy(istage[:, hh, :], eidx[:, t, bass.ds(it * (2 * TOPK) + hh * TOPK, TOPK)]).then_inc(stage_set, 1)
                        for q in range(4):
                            n = head0 * 4 + hh * 4 + q
                            pool.wait_ge(gate_passed, it * 8 + (n + 1)) 
                            pool.wait_ge(stage_set, it * 2 + (head0 + hh + 1))
                            pool.wait_ge(rows_free, it * (2 * TOPK) + ((head0 + hh) * TOPK + 4 * q + 4))
                            g.tensor_tensor(gate_out[:], gate_in[:], gate_in[:], ALU.add).then_inc(gate_passed, 1)
                            for j in range(4 * q, 4 * q + 4):
                                pool.indirect_dma_start(out=rows[:, j, :], out_offset=None, in_=A[table],
                                                        in_offset=bass.IndirectOffsetOnAxis(ap=istage[:, hh, j:j + 1], axis=0)) \
                                    .then_inc(row_in[j], 16)

            g.tensor_tensor(gate_out[:], gate_in[:], gate_in[:], ALU.add).then_inc(gate_passed, 1)
            for l in range(2):
                for phase in range(4):
                    gather(l, f"peer_{'down' if phase < 2 else 'up'}{l}", phase % 2, phase)


def kernel(**inputs):
    import numpy as np
    import concourse.bacc as bacc
    from concourse.bass_utils import run_bass_kernel_spmd as run

    I = {k: np.asarray(v) for k, v in inputs.items()}

    def column(a):
        return np.ascontiguousarray(a).reshape(-1, P).T

    def pad64(a):
        return np.concatenate([a.reshape(64, 1), np.zeros((64, 1), np.float32)])

    parts = {
        "c": column(I["c"]), "c_ctx": column(I["c_ctx"]), "c2": column(I["c_2"]),
        "ada_b0": column(I["ada_b"][0]), "ada_b1": column(I["ada_b"][1]), "norm_g": column(I["norm_g"]),
        "conv_w": column(I["ssd_conv_w"][0]), "conv_b": column(I["ssd_conv_b"][0]), "ssd_ng": column(I["ssd_norm_g"][0]),
        "ssd_d": column(np.repeat(I["ssd_d"][0], HD)), "dt_bias": pad64(I["ssd_dt_bias"][0]), "a_log": pad64(I["ssd_a_log"][0]),
        "pool_b": column(I["pool_b"][0]), "pool_scale": column(I["pool_scale"][0]), "final_g": column(I["final_g"]),
        "ada_b2_0": column(I["b_ada_2"][0]), "ada_b2_1": column(I["b_ada_2"][1]),
        "n1g": column(I["norm1_g_2"]), "n2g": column(I["norm2_g_2"]),
        "qg": np.tile(I["q_norm_g_2"], (1, 2)).T, "kg": np.tile(I["k_norm_g_2"], (1, 2)).T,
        "conv_w2": column(I["conv_w_2"]), "out_g": column(I["out_norm_g_2"]),
    }
    cols = np.concatenate([parts[k] for k in COLS], axis=1)
    assert cols.shape == (P, N_COLS)

    def counts(n, w):
        pos = np.arange(n)
        return np.minimum(pos + (w - w // 2), n) - np.maximum(pos - w // 2, 0)

    rcnt = np.stack([1.0 / np.outer(counts(4, w), counts(64, w)).reshape(-1) for w in (2, 4, 8, 16)]).astype(np.float32)
    dist = 255 - np.arange(BSTEP)
    half = BUCKETS // 2
    dd = np.maximum(dist, 0)
    ratio = np.log(np.maximum(dd, 1).astype(np.float32) / np.float32(half)) / np.float32(np.log(MAX_DIST / half))
    large = np.minimum(half + (ratio * np.float32(BUCKETS - half)).astype(np.int32), BUCKETS - 1)
    bucket = np.where(dd < half, dd, large)
    ok = (dist >= 0) & (dist < WINDOW)
    onehot = np.zeros((BUCKETS + 1, BSTEP), np.float32)
    onehot[bucket[ok], np.arange(BSTEP)[ok]] = 1.0
    onehot[BUCKETS, ~ok] = NEG
    rel = np.concatenate([I["rel_bias_2"], np.ones((1, HEADS), np.float32)])

    def blocks(a):
        return np.ascontiguousarray(a[0].T.reshape(KB, P, T).transpose(1, 0, 2))

    arrays = {
        "xT": blocks(I["x"]), "hT": blocks(I["ctx"]), "cols": np.ascontiguousarray(cols),
        "ada_w": I["ada_w"], "ffn_w_gate": I["ffn_w_gate"], "ffn_w_up": I["ffn_w_up"], "ffn_w_down": I["ffn_w_down"],
        "ssd_w_in": I["ssd_w_in"][0], "ssd_w_out": I["ssd_w_out"][0], "pool_w": I["pool_w"][0],
        "w_ada2": I["w_ada_2"], "w_in2": I["w_in_2"], "w_out2": I["w_out_2"], "peer_wq": I["peer_wq_2"],
        "rcnt": rcnt, "bias_onehot": onehot, "rel_bias": rel, "sink": np.ascontiguousarray(I["attn_sink_2"].reshape(2, HEADS // 2, 2).transpose(0, 2, 1).reshape(2, HEADS)),
        "sgu_b": I["sgu_b_2"][None], "sgu_w": np.ascontiguousarray(I["sgu_w_2"].transpose(3, 0, 1, 2)),
    }
    for l in range(2):
        arrays[f"keys{l}"] = np.ascontiguousarray(I["peer_sub_keys_2"][l].reshape(16, KEYS, P).transpose(2, 0, 1))
        arrays[f"peer_down{l}"] = I["peer_down_2"][l]
        arrays[f"peer_up{l}"] = I["peer_up_2"][l]
    arrays = {k: np.ascontiguousarray(a) for k, a in arrays.items()}

    nc = bacc.Bacc("TRN2", target_bir_lowering=False, num_devices=1)
    A = {k: nc.dram_tensor(f"in_{k}", a.shape, F32, kind="ExternalInput").ap() for k, a in arrays.items()}
    A["bias_scratch"] = nc.dram_tensor("bias_scratch", (HEADS, BSTEP), F32, kind="Internal").ap()
    A["out"] = nc.dram_tensor("out", (P, KB, T), F32, kind="ExternalOutput").ap()
    program(nc, A)
    r = run(nc, [{f"in_{k}": a for k, a in arrays.items()}], core_ids=[0])
    out = np.asarray(r.results[0]["out"])
    return np.ascontiguousarray(out.transpose(1, 0, 2).reshape(D, T).T)[None]
```

```python
from contextlib import ExitStack

import concourse.bass as bass
from concourse import mybir

F32 = mybir.dt.float32
F32R = mybir.dt.float32r
U32 = mybir.dt.uint32
ACT = mybir.ActivationFunctionType
ALU = mybir.AluOpType
AX_X = mybir.AxisListType.X

P = 128
D = 1024
KB = D // P
T = 256
TT = T // P
F = 2816
EPS = 1e-6
FFN_ITERS = F // 256
FFN_TILES = 3 * FFN_ITERS
HIGH_RING = 3
RING = 6
TILE = 2048

H, HD, G, N = 32, 64, 4, 128
D_INNER = H * HD
XB = D_INNER // P
CONV_W = 5
Q = 128
NCH = T // Q

HEADS, DH, KV = 8, 64, 2
BUCKETS, MAX_DIST, WINDOW = 32, 128, 128
NEG = -1e30
PH, TOPK, KEYS = 8, 16, 128
PICKS = PH * TOPK
SLOTS = 16

STAGES = [("ada0", 12), ("ffn0", 33), ("ffn1", 33), ("proj_ctx", 11), ("proj_lat", 21), ("ssd_out", 8), ("ffn2", 33), ("ffn3", 33), ("pool", 1), ("ffn4", 33)]
for _l in range(2):
    STAGES += [(f"w_in{_l}", 8), (f"w_out{_l}", 4), (f"wq{_l}", 8)]
BASE, _n = {}, 0
for _name, _count in STAGES:
    BASE[_name] = _n
    _n += _count


def consumed(stage, i):
    return BASE[stage] + i + 1


ADA = [("ada_w", 0, 3, 6, 0, 2), ("ada_w", 1, 0, 6, 0, 0), ("ada_w", 1, 6, 3, 0, 0), ("w_ada2", 0, 0, 6, 2, 0), ("w_ada2", 1, 0, 6, 2, 0)]
ADA_RING = 3
ADA_STEPS = [2 * (count + also) for _, _, _, count, _, also in ADA]
ADA_FREE = max(ADA_STEPS)
ADA_TURNS = 4
ADA_BASE = [ADA_FREE + ADA_TURNS * sum(ADA_STEPS[:n]) for n in range(len(ADA) + 1)]


def ada_last(n, j):
    return sum(2 * (1 + (t < ADA[n][5])) for t in range(j + 1))


COLS = {}
_at = 0
for _name, _count in [("c", 8), ("c_ctx", 8), ("c2", 8), ("ada_b0", 72), ("ada_b1", 72), ("norm_g", 48),
                      ("conv_w", 120), ("conv_b", 24), ("ssd_ng", 16), ("ssd_d", 16), ("dt_bias", 1), ("a_log", 1),
                      ("pool_b", 8), ("pool_scale", 8), ("final_g", 8), ("ada_b2_0", 48), ("ada_b2_1", 48),
                      ("n1g", 16), ("n2g", 16), ("qg", 2), ("kg", 2), ("conv_w2", 12), ("out_g", 16)]:
    COLS[_name] = (_at, _count)
    _at += _count
N_COLS = _at

W_IN_ORDER = (0, 1, 2, 7, 6, 3, 4, 5)
BSTEP = 384


def program(nc, A, stop=None):
    ctx = ExitStack()
    with ctx:
        starts = {}

        def sb(name, shape, dt=F32):
            starts[name] = -(-nc.sbuf_base // 32) * 32
            return ctx.enter_context(nc.sbuf_tensor(name, shape, dt))

        def sem(name):
            return ctx.enter_context(nc.semaphore(name))

        xT = sb("xT", [P, KB, T])
        hT = sb("hT", [P, KB, T])
        u = sb("u", [P, KB, T])
        sq = sb("sq", [P, KB, T])
        std = sb("std", [P, T])
        rstd = sb("rstd", [P, T])
        wring = sb("wring", [P, RING, TILE])
        cols = sb("cols", [P, N_COLS])
        ident = sb("ident", [P, P])
        ones = sb("ones", [P, P])
        bones = sb("bones", [P, P])
        tri = sb("tri", [P, P])
        trisuf = sb("trisuf", [P, P])
        flip = sb("flip", [P, P])
        eps = sb("eps", [P, 1])
        silu_c = sb("silu_c", [P, KB, 3])
        cpair = sb("cpair", [P, 2, 3])
        mod0 = sb("mod0", [P, 72])
        mod0c = sb("mod0c", [P, 72])
        mod1 = sb("mod1", [P, 72])
        mod2 = sb("mod2", [P, 2, 48])
        gscale = sb("gscale", [P, 16, KB])
        hgate = sb("hgate", [P, 5, KB])
        rowp = sb("rowp", [1, 2, 4, P])
        sink = sb("sink", [P, 2, HEADS])
        thr = sb("thr", [P, 2, TOPK])
        gate_in = sb("gate_in", [1, 1])
        gate_out = sb("gate_out", [1, 1])
        AREA = 27930
        arena = sb("arena", [P, AREA])

        def rounded(name, shape, of, off=0):
            return nc.alloc_sbuf_tensor_at(name, shape, F32R, offset=starts[of] + 4 * off)

        wlow = rounded("wlow", [P, RING, TILE], "wring")
        whigh = rounded("whigh", [P, HIGH_RING, TILE], "arena", 8192)
        u_lo = rounded("u_lo", [P, KB, T], "u")
        u_hi = rounded("u_hi", [P, KB, T], "sq")
        hid_lo = rounded("hid_lo", [P, 2, 512], "arena", 1024)
        hid_hi = rounded("hid_hi", [P, 2, 512], "arena", 25600)
        psum = ctx.enter_context(nc.psum_tensor("psum", [P, 8, 512], F32))

        def at(off, *dims):
            n = 1
            for d in dims:
                n *= d
            assert off + n <= AREA, (off, dims)
            v = arena[:, off:off + n]
            if len(dims) == 1:
                return v
            names = "abcde"[:len(dims)]
            return v.rearrange(f"p ({' '.join(names)}) -> p {' '.join(names)}",
                               **{k: d for k, d in zip(names, dims)})

        def col(name, i, n=1):
            return cols[:, COLS[name][0] + i:COLS[name][0] + i + n]

        sg = at(0, 2, 512)
        hid = at(1024, 2, 512)
        aring = at(2048, ADA_RING, 2, D)
        asum = at(14336, 8, D)
        asum2 = at(22528, 3, D)
        arow = at(14336, 3, D)[0:2]
        xbc = at(0, 24, T)
        z = at(6144, XB, T)
        xtok = at(10240, NCH, D_INNER)
        btok = at(14336, NCH, G * N)
        xw = at(15360, 2, D_INNER)
        h_first = at(19456, 2, D_INNER)
        h_second = u[:, :, :].rearrange("p a b -> p (a b)")
        h_second_b = sq[:, :, :].rearrange("p a b -> p (a b)")
        raw = at(23552, 3, 2, T + CONV_W - 1)
        decay = at(23552, 3, 512)
        hflat = hT[:, :, :].rearrange("p a b -> p (a b)")
        eoff = hflat[:, 0:1536].rearrange("p (a b) -> p a b", a=3)
        dt64 = hflat[0:64, 1024:2048].rearrange("p (a b) -> p a b", a=4)
        da_tok = at(27160, 4, 64)
        acum = at(27416, NCH, 64)
        diff = at(27544, NCH, 64)
        eal = at(27672, NCH, 64)
        wdt = at(27800, NCH, 64)
        dtw = at(25112, 3, T)[0:64]
        exp_a = sb("exp_a", [64, 1])
        cbm = at(25112, NCH, 2, 512)
        grstd = xw[:, 0, 0:1024].rearrange("p (a b) -> p a b", a=4)
        vpad = at(0, 8, 80)
        pa = at(640, 8, 80)
        pb = at(1280, 8, 80)
        prow = at(1920, 2, 4, 64)
        psum2 = at(2432, 2, 4, 64)
        pooled = at(3072, 8, T)
        rcnt = at(5120, 4, T)
        bias_t = at(0, HEADS, T)
        sgw = at(2048, 2, 4, P)
        boh = at(3072, BSTEP)
        brow = at(3456, BSTEP)
        relx = at(3840, HEADS)
        AO = 3072
        proj = at(AO, 16, T)
        merged = at(AO + 4096, 8, T)
        kd = at(AO + 6144, KV, T)
        rs5 = at(AO + 6656, 5, T)
        vtok = at(AO + 7936, TT, P)
        prob = at(AO + 8192, HEADS, T)
        probT = at(AO + 10240, HEADS, 2, P)
        small = at(AO + 12288, 8, HEADS)
        zpad = at(AO + 12352, 2, T + 2)
        cacc = at(AO + 12868, 2, T)
        vc = at(AO + 13380, 2, T)
        vrs = at(AO + 13892, 2, T)
        vntok = at(AO + 14404, TT, T)
        ors = at(AO + 14916, 3, T)
        gq8 = at(AO + 15684, 1)
        vsq = at(AO + 15700, 2, T)
        rows = at(AO, SLOTS, D)
        qT = at(AO, 16, T)
        score = [at(AO + 4096, 16, KEYS), u[:, :, :].rearrange("p a b -> p (a b)").rearrange("p (a b) -> p a b", a=16)]
        rep = sq[:, :, :].rearrange("p a b -> p (a b)").rearrange("p (a b) -> p a b", a=16)
        rep2 = sq[:, :, :]
        cand = hT[:, :, :].rearrange("p h (a b) -> p h a b", a=TOPK)
        h2tok = at(AO + 16384, TT, D)
        yacc = at(AO + 18432, 2, D)
        keys = at(AO + 18432, 16, KEYS)
        ytok = h2tok
        PO = AO + 20480
        topv = at(PO, 16, TOPK)
        topf = at(PO + 256, 16, TOPK)
        dtop = at(PO + 512, 16, TOPK)
        bestv = at(PO + 768, PH, TOPK)
        posf = at(PO + 896, PICKS)
        isum = at(PO + 1024, PICKS)
        jrem = at(PO + 1152, PICKS)
        e1 = at(PO + 1280, PICKS)
        e2 = at(PO + 1408, PICKS)
        gate = at(PO + 1536, TT, PICKS)
        dots = at(PO + 1792, TT, PICKS)
        wexp = at(PO + 2048, TT, PICKS)
        dots16 = at(PO + 2304, TOPK)
        w16 = at(PO + 2320, TOPK)
        gsum = at(PO + 2336, 2, PH)
        gsub = at(PO + 2352, PH, TOPK)
        topi = sb("topi", [P, 16, TOPK], U32)
        posi = sb("posi", [P, PICKS], U32)
        eidx = sb("eidx", [P, TT, PICKS], U32)
        istage = sb("istage", [P, 2, TOPK], U32)
        ge = sq[:, :, :].rearrange("p a b -> p (a b)")
        tmp = hT[:, :, :].rearrange("p a b -> p (a b)")

        cols_in = sem("cols_in")
        x_in = sem("x_in")
        h_in_sem = sem("h_in")
        rows_in = sem("rows_in")
        weights_in = [sem(f"weights_in{i}") for i in range(RING)]
        weights_consumed = sem("weights_consumed")
        eps_set = sem("eps_set")
        bones_set = sem("bones_set")
        pool_step = sem("pool_step")
        act_step = sem("act_step")
        dve_step = sem("dve_step")
        silu_c_ready = sem("silu_c_ready")
        ada_in = [sem(f"ada_in{i}") for i in range(6)]
        w_high = sem("w_high")
        w_low = sem("w_low")
        u_high = sem("u_high")
        u_low = sem("u_low")
        hid_full = sem("hid_full")
        hid_high = sem("hid_high")
        ada_step = sem("ada_step")
        cpair_set = sem("cpair_set")
        ada_summed = sem("ada_summed")
        arow_ready = sem("arow_ready")
        arow_turned = sem("arow_turned")
        mods_ready = sem("mods_ready")
        x_ready = sem("x_ready")
        h_ready = sem("h_ready")
        sq_ready = sem("sq_ready")
        ms_ready = sem("ms_ready")
        std_ready = sem("std_ready")
        un_ready = sem("un_ready")
        u_ready = sem("u_ready")
        silu_ready = sem("silu_ready")
        hid_ready = sem("hid_ready")
        proj_evicted = sem("proj_evicted")
        conv_done = sem("conv_done")
        xbc_ready = sem("xbc_ready")
        z_ready = sem("z_ready")
        tok_done = sem("tok_done")
        tok_evicted = sem("tok_evicted")
        negabs_ready = sem("negabs_ready")
        expabs_ready = sem("expabs_ready")
        dt_ready = sem("dt_ready")
        da_done = sem("da_done")
        da_evicted = sem("da_evicted")
        cum_done = sem("cum_done")
        diff_ready = sem("diff_ready")
        decay_ready = sem("decay_ready")
        xw_ready = sem("xw_ready")
        state_done = sem("state_done")
        state_added = sem("state_added")
        cb_done = sem("cb_done")
        cbm_ready = sem("cbm_ready")
        xdt_ready = sem("xdt_ready")
        bc_done = sem("bc_done")
        seg_ready = sem("seg_ready")
        expseg_ready = sem("expseg_ready")
        expbc_ready = sem("expbc_ready")
        m_ready = sem("m_ready")
        eoff_ready = sem("eoff_ready")
        y_done = sem("y_done")
        y_evicted = sem("y_evicted")
        gated_ready = sem("gated_ready")
        gsq_ready = sem("gsq_ready")
        gms_ready = sem("gms_ready")
        gstd_ready = sem("gstd_ready")
        gnorm_ready = sem("gnorm_ready")
        so_evicted = sem("so_evicted")
        pooled_ready = sem("pooled_ready")
        rcnt_in = sem("rcnt_in")
        sgw_in = sem("sgw_in")
        boh_in = sem("boh_in")
        relx_in = sem("relx_in")
        brow_done = sem("brow_done")
        brow_ready = sem("brow_ready")
        brow_out = sem("brow_out")
        bias_in = sem("bias_in")
        sgw_ready = sem("sgw_ready")
        win_evicted = sem("win_evicted")
        qksq_ready = sem("qksq_ready")
        qkms_ready = sem("qkms_ready")
        qkstd_ready = sem("qkstd_ready")
        qk_ready = sem("qk_ready")
        vt_done = sem("vt_done")
        vtok_ready = sem("vtok_ready")
        vsum_done = sem("vsum_done")
        vc_ready = sem("vc_ready")
        vsq_ready = sem("vsq_ready")
        vvar_done = sem("vvar_done")
        vstd_ready = sem("vstd_ready")
        vn_ready = sem("vn_ready")
        vnt_done = sem("vnt_done")
        vntok_ready = sem("vntok_ready")
        mix_done = sem("mix_done")
        logits_done = sem("logits_done")
        nmax_ready = sem("nmax_ready")
        pexp_ready = sem("pexp_ready")
        prob_ready = sem("prob_ready")
        probT_done = sem("probT_done")
        probT_ready = sem("probT_ready")
        pv_done = sem("pv_done")
        pv_evicted = sem("pv_evicted")
        heads_ready = sem("heads_ready")
        osq_ready = sem("osq_ready")
        oms_ready = sem("oms_ready")
        ostd_ready = sem("ostd_ready")
        merged_ready = sem("merged_ready")
        wq_evicted = sem("wq_evicted")
        h2t_done = sem("h2t_done")
        h2t_ready = sem("h2t_ready")
        keys_in = sem("keys_in")
        keys_done = sem("keys_done")
        score_ready = sem("score_ready")
        gsub_ready = sem("gsub_ready")
        gexp_ready = sem("gexp_ready")
        eidx_ready = sem("eidx_ready")
        stage_set = sem("stage_set")
        gate_passed = sem("gate_passed")
        row_in = [sem(f"row_in{i}") for i in range(SLOTS)]
        rows_free = sem("rows_free")
        dots_saved = sem("dots_saved")
        dots_ready = sem("dots_ready")
        gelu_ready = sem("gelu_ready")
        ytok_ready = sem("ytok_ready")
        yt_done = sem("yt_done")
        out_stored = sem("out_stored")

        def modcol(m, i):
            return m[:, 8 * i:8 * i + 8]

        NORMS = [
            (xT, col("norm_g", 0, 8), modcol(mod0, 0), modcol(mod0, 1), (x_in, 16), 1),
            (hT, col("norm_g", 0, 8), modcol(mod0c, 0), modcol(mod0c, 1), (h_in_sem, 16), 1),
            (hT, col("norm_g", 8, 8), modcol(mod0c, 3), modcol(mod0c, 4), (h_ready, 1), 3),
            (xT, col("norm_g", 8, 8), modcol(mod0, 3), modcol(mod0, 4), (x_ready, 1), 3),
            (xT, col("norm_g", 16, 8), modcol(mod0, 6), modcol(mod0, 7), (x_ready, 2), 3),
            (xT, col("norm_g", 24, 8), modcol(mod1, 0), modcol(mod1, 1), (x_ready, 3), 4),
            (xT, col("norm_g", 32, 8), modcol(mod1, 3), modcol(mod1, 4), (x_ready, 4), 4),
            (xT, col("norm_g", 40, 8), modcol(mod1, 6), modcol(mod1, 7), (x_ready, 5), 5),
            (xT, None, None, None, (x_ready, 6), 0),
        ]
        for l in range(2):
            m2 = mod2[:, l, :]
            NORMS += [(xT, col("n1g", 8 * l, 8), m2[:, 0:8], m2[:, 8:16], (x_ready, 7 + 2 * l), 6 + l),
                      (xT, col("n2g", 8 * l, 8), m2[:, 24:32], m2[:, 32:40], (x_ready, 8 + 2 * l), 6 + l)]
        FINAL = 8
        FFN_NORM = [0, 1, 4, 5, 7]
        FFN_GATE = [modcol(mod0, 2), modcol(mod0c, 2), modcol(mod0, 8), modcol(mod1, 2), modcol(mod1, 8)]
        FFN_DST = [xT, hT, xT, xT, xT]

        def u_done(n):
            return 8 * (n if n <= FINAL else n - 1)

        def place(h):
            return (h % 2) * (HEADS // 2) + h // 2

        def bank(b, off=0, n=512):
            return psum[:, b, off:off + n]

        def h_state(d, second):
            if not second:
                return h_first[:, d, :]
            return h_second if d == 0 else h_second_b

        def first_chunk(d):
            return 0 if d == 0 else 1

        def xdt(c, d):
            return xw[:, d, :] if c == 0 else xtok[:, d, :]

        ADA_BANK = (5, 5, 5, 6, 7)
        BC_BANK = (0, 1, 4)

        block = ctx.enter_context(nc.Block())

        @block.sync
        def _(sp):
            loaded = [0]

            def load(src, a, b):
                n = loaded[0]
                loaded[0] += 1
                if n >= RING:
                    sp.wait_ge(weights_consumed, n - RING + 1)
                sp.dma_start(wring[:, n % RING, 0:a * b].rearrange("p (a b) -> p a b", a=a), src) \
                    .then_inc(weights_in[n % RING], 16)

            def rows_of(w):
                return w.rearrange("(k p) n -> p k n", p=P)

            def load_columns(w, count, width=256):
                v = rows_of(w)
                for i in range(count):
                    load(v[:, :, i * width:(i + 1) * width], v.shape[1], width)

            def load_ffn(n, l, f):
                gate_w, up_w, down_w = (rows_of(A[k][l, f]) for k in ("ffn_w_gate", "ffn_w_up", "ffn_w_down"))
                load(gate_w[:, :, 0:256], KB, 256)
                load(up_w[:, :, 0:256], KB, 256)
                load(gate_w[:, :, 256:512], KB, 256)
                load(up_w[:, :, 256:512], KB, 256)
                load(down_w[:, 0:2, :], 2, D)
                load(gate_w[:, :, 512:768], KB, 256)
                load(up_w[:, :, 512:768], KB, 256)
                load(down_w[:, 2:4, :], 2, D)
                name, layer, group, count, _, _ = ADA[n]
                ada = rows_of(A[name][layer])
                if n == 2:
                    sp.wait_ge(weights_consumed, consumed("ssd_out", 7))
                if n == 4:
                    sp.wait_ge(x_ready, 5)
                sp.wait_ge(ada_step, ADA_BASE[n])
                first = loaded[0]
                with sp.Fori(0, (FFN_ITERS - 3) // 2, 1) as it:
                    for j in range(6):
                        slot = (first + j) % RING
                        sp.wait_ge(weights_consumed, it * 6 + (first + j - RING + 1))
                        if j % 3 < 2:
                            src = (gate_w, up_w)[j % 3][:, :, bass.ds(it * 512 + 256 * (3 + j // 3), 256)]
                            dst = wring[:, slot, :].rearrange("p (a b) -> p a b", a=KB)
                        else:
                            src = down_w[:, bass.ds(it * 4 + 2 * (2 + j // 3), 2), :]
                            dst = wring[:, slot, :].rearrange("p (a b) -> p a b", a=2)
                        sp.dma_start(dst, src).then_inc(weights_in[slot], 16)
                        for a in {0: (0,), 1: (1,), 2: (2,), 5: (3, 4, 5)}.get(j, ()):
                            if a >= count:
                                continue
                            if a >= ADA_RING:
                                sp.wait_ge(ada_step, it * ADA_STEPS[n] + (ADA_BASE[n] + ada_last(n, a - ADA_RING)))
                            else:
                                before = a + ADA_RING if a + ADA_RING < count else a
                                sp.wait_ge(ada_step, it * ADA_STEPS[n] + (ADA_BASE[n] - ADA_STEPS[n] + ada_last(n, before)))
                            sp.dma_start(aring[:, a % ADA_RING], ada[:, bass.ds(it * 2, 2), (group + a) * D:(group + a + 1) * D]) \
                                .then_inc(ada_in[a], 16)
                loaded[0] += 6 * ((FFN_ITERS - 3) // 2)
                load(down_w[:, 2 * FFN_ITERS - 2:2 * FFN_ITERS, :], 2, D)

            sp.dma_start(cols[:], A["cols"]).then_inc(cols_in, 16)
            for group in range(3):
                for i in range(4):
                    load(rows_of(A["ada_w"][0])[:, 2 * i:2 * i + 2, group * D:(group + 1) * D], 2, D)
            load_ffn(0, 0, 0)
            load_ffn(1, 0, 0)
            w_ssd = rows_of(A["ssd_w_in"])
            for lat in range(2):
                load(w_ssd[:, :, 5120:5184], KB, 64)
                for i in range(12 if lat else 10):
                    load(w_ssd[:, :, 2048 + 256 * i:2304 + 256 * i], KB, 256)
                for i in range(8 if lat else 0):
                    load(w_ssd[:, :, 256 * i:256 * i + 256], KB, 256)
            load_columns(A["ssd_w_out"], 8, 128)
            load_ffn(2, 0, 1)
            load_ffn(3, 1, 0)
            load(A["pool_w"].rearrange("g (k p) n -> p (g k) n", p=P), 8, 256)
            load_ffn(4, 1, 1)
            for l in range(2):
                for i in W_IN_ORDER:
                    load(rows_of(A["w_in2"][l])[:, :, 256 * i:256 * i + 256], KB, 256)
                load_columns(A["w_out2"][l], 4)
                if l == 0:
                    sp.wait_ge(mods_ready, 7)
                else:
                    sp.wait_ge(ytok_ready, 2)
                sp.dma_start(keys, A[f"keys{l}"]).then_inc(keys_in, 16)
                load_columns(A["peer_wq"][l], 8)
            sp.wait_ge(x_ready, stop or 11)
            sp.dma_start(A["out"], xT[:]).then_inc(out_stored, 16)
            sp.wait_ge(out_stored, 16)

        @block.tensor
        def _(pe):
            taken = [0]

            def tile():
                n = taken[0]
                taken[0] += 1
                pe.wait_ge(weights_in[n % RING], 16 * (n // RING + 1))
                return wring[:, n % RING, :]

            def mm(out, lhsT, rhs, start, stop, shared=False):
                return nc.tensor.matmul(out, lhsT, rhs, start=start, stop=stop, skip_group_check=shared)

            def transpose(out, in_):
                return nc.tensor.transpose(out, in_, ident[0:in_.shape[0], 0:in_.shape[0]])

            def ada_rows(groups):
                for g in groups:
                    for i in range(4):
                        w = tile().rearrange("p (k n) -> p k n", k=2)
                        for k in range(2):
                            for half in range(2):
                                ins = mm(psum[0:2, 2 * g + half, :], silu_c[:, 2 * i + k, 0:2], w[:, k, half * 512:(half + 1) * 512],
                                         i == 0 and k == 0, i == 3 and k == 1)
                        ins.then_inc(weights_consumed, 1)
                pe.wait_ge(arow_ready, groups[-1] + 1)
                for g in groups:
                    for b in range(KB):
                        ins = transpose(bank(6, (KB * g + b) * 2, 2), arow[:, g, b * P:(b + 1) * P])
                ins.then_inc(arow_turned, 1)

            def ada_sums(n):
                count = ADA[n][3] + ADA[n][5]
                pe.wait_ge(ada_step, ADA_BASE[n + 1])
                for a in range(count):
                    for b in range(KB):
                        ins = mm(bank(ADA_BANK[n], KB * a + b, 1), (asum2 if n == 2 else asum)[:, a, b * P:(b + 1) * P], ones[:, 0:1], True, True)
                ins.then_inc(ada_summed, 1)

            def norm_sums(n):
                pe.wait_ge(sq_ready, n + 1)
                if n == 9:
                    pe.wait_ge(mods_ready, 7)
                for k in range(KB):
                    ins = mm(bank(7, 0, T), ones[:], sq[:, k, :], k == 0, k == KB - 1)
                ins.then_inc(ms_ready, 1)

            def ffn(n):
                base = n * FFN_ITERS

                def parts(t, it=0):
                    pe.wait_ge(w_low, it * 6 + (FFN_TILES * n + t + 1))
                    return whigh[:, t % HIGH_RING, :], wlow[:, (BASE[f"ffn{n}"] + t) % RING, :]

                def passes(w, x, start, stop, out, shared=False):
                    for a, b in ((0, 0), (0, 1), (1, 0)):
                        ins = mm(out, w[a], x[b], start and a + b == 0, stop and a == 1, shared)
                    return ins

                def half(t, out, it=0):
                    w = [v.rearrange("p (k n) -> p k n", k=KB) for v in parts(t, it)]
                    for b in range(2):
                        for k in range(KB):
                            ins = passes([v[:, k, b * P:(b + 1) * P] for v in w],
                                         [u_hi[:, k, :], u_lo[:, k, :]], k == 0, k == KB - 1,
                                         out[:, b * T:(b + 1) * T])
                    ins.then_inc(weights_consumed, 1)

                def down(t, s, first, last, it=0):
                    w = [v.rearrange("p (f n) -> p f n", f=2) for v in parts(t, it)]
                    for f in range(2):
                        for d in range(KB):
                            ins = passes([v[:, f, d * P:(d + 1) * P] for v in w],
                                         [v[:, s, f * T:(f + 1) * T] for v in (hid_hi, hid_lo)],
                                         first and f == 0 and d % 2 == 0, last and f == 1, bank(d // 2, (d % 2) * T, T), True)
                    ins.then_inc(weights_consumed, 1)

                pe.wait_ge(u_low, 4 * (n + 1))
                half(0, bank(4))
                half(1, bank(6))
                if n in (1, 4):
                    pe.wait_ge(mods_ready, {1: 3, 4: 6}[n])
                half(2, bank(5))
                half(3, bank(7))
                pe.wait_ge(hid_ready, base + 1)
                down(4, 0, True, False)
                half(5, bank(4))
                half(6, bank(6))
                pe.wait_ge(hid_ready, base + 2)
                down(7, 1, False, False)
                with pe.Fori(0, (FFN_ITERS - 3) // 2, 1) as it:
                    for j in range(2):
                        half(8 + 3 * j, bank(5 - j), it)
                        half(9 + 3 * j, bank(7 - j), it)
                        pe.wait_ge(hid_ready, it * 2 + (base + 3 + j))
                        down(10 + 3 * j, j, False, False, it)
                pe.wait_ge(hid_ready, base + FFN_ITERS)
                down(FFN_TILES - 1, 0, False, True)
                taken[0] += FFN_TILES

            def project(stage, i, count, evicted, before, src, kb, width):
                w = tile()[:, 0:kb * width].rearrange("p (k n) -> p k n", k=kb)
                if i >= 4:
                    pe.wait_ge(evicted, before + i - 3)
                for b in range((width + P - 1) // P):
                    m = min(P, width - b * P)
                    for k in range(kb):
                        ins = mm(psum[0:m, i % 4, b * T:(b + 1) * T], w[:, k, b * P:b * P + m], src[:, k, :],
                                 k == 0, k == kb - 1)
                ins.then_inc(weights_consumed, 1)

            pe.wait_ge(pool_step, 9)
            pe.wait_ge(bones_set, 1)
            pe.wait_ge(silu_c_ready, 3)
            ada_rows((0, 1))
            norm_sums(0)
            ada_rows((2,))
            pe.wait_ge(mods_ready, 2)
            ffn(0)
            norm_sums(1)
            ada_sums(0)
            ffn(1)

            def ssd_project(lat):
                stage = "proj_lat" if lat else "proj_ctx"
                pe.wait_ge(u_ready, u_done(4 if lat else 3))
                n = 21 if lat else 11
                for i in range(n):
                    if lat and i < 4:
                        pe.wait_ge(state_added, 4)
                    project(stage, i, n, proj_evicted, 11 * lat, u, KB, 64 if i == 0 else 256)

            def ssd_tokens(lat):
                pe.wait_ge(dt_ready, lat + 1)
                if lat:
                    pe.wait_ge(decay_ready, 2)
                for i in range(4):
                    ins = transpose(bank(6, 64 * i, 64), dt64[:, 1 + i // 2, (i % 2) * P:(i % 2) * P + P])
                ins.then_inc(da_done, 1)
                pe.wait_ge(da_evicted, lat + 1)
                for c in range(NCH):
                    for d, m in enumerate((tri, trisuf)):
                        mm(bank(6, 256 + 64 * c + 32 * d, 32), m[:], da_tok[:, 2 + c, 32 * d:32 * d + 32], True, True)
                ins = mm(bank(6, 384, 128), ones[:], da_tok[:, 2:4, :], True, True)
                ins.then_inc(cum_done, 1)
                for i in range(10):
                    g, c = i // 2, i % 2
                    pe.wait_ge(xbc_ready, (12 if lat else 0) * 1 - (2 if lat else 0) + 2 * g + 2)
                    if 10 * lat + i >= 2:
                        pe.wait_ge(tok_evicted, 10 * lat + i - 1)
                    for b in range(4):
                        ins = transpose(bank(4 + i % 2, b * P, P), xbc[:, 4 * g + b, c * P:c * P + P])
                    ins.then_inc(tok_done, 1)

            def ssd_states(k, c):
                pe.wait_ge(xw_ready, k + 1)
                if k == 0:
                    pe.wait_ge(proj_evicted, 11)
                elif k == 4:
                    pe.wait_ge(proj_evicted, 32)
                else:
                    pe.wait_ge(state_added, k)
                if k in (0, 4):
                    pe.wait_ge(tok_evicted, 10 if k == 0 else 20)
                for g in range(G):
                    ins = mm(bank(g), btok[:, c, g * N:(g + 1) * N], xw[:, k % 2, g * 512:(g + 1) * 512], True, True)
                ins.then_inc(state_done, 1)

            norm_sums(2)
            ada_sums(1)
            ssd_project(0)
            pe.wait_ge(mods_ready, 4)
            ssd_tokens(0)
            for k in range(4):
                d, i = k // 2, k % 2
                ssd_states(k, first_chunk(d) if i == 0 else 1 - first_chunk(d))
            norm_sums(3)
            ssd_project(1)
            ssd_tokens(1)
            for d in range(2):
                ssd_states(4 + d, first_chunk(d))
            pe.wait_ge(xbc_ready, 22)
            for c in range(NCH):
                for g in range(G):
                    ins = mm(bank(4 + c, g * P, P), xbc[:, 16 + g, c * P:c * P + P], xbc[:, 20 + g, c * P:c * P + P],
                             True, True)
            ins.then_inc(cb_done, 1)

            BATCHES = [(c, jb, d) for c in range(NCH) for jb in range(H // 4) for d in range(2)]

            def running_sums(b):
                c, jb, d = BATCHES[b]
                if b < 3:
                    pe.wait_ge(state_added, 6)
                    if b == 2:
                        pe.wait_ge(cbm_ready, 2)
                else:
                    pe.wait_ge(seg_ready, b - 2)
                    pe.wait_ge(expbc_ready, b - 2)
                for i in range(4):
                    h = 32 * d + 4 * jb + i
                    ins = mm(bank(BC_BANK[b % 3], i * P, P), da_tok[:, 2 + c, h:h + 1].to_broadcast([P, P]),
                             (tri, trisuf)[d][:], True, True)
                ins.then_inc(bc_done, 1)

            def outputs(b):
                c, jb, d = BATCHES[b]
                pe.wait_ge(m_ready, b + 1)
                pe.wait_ge(eoff_ready, b + 1)
                pe.wait_ge(xdt_ready, 2 * c + d + 1)
                t = c * 8 + jb
                if d == 0 and t >= 2:
                    pe.wait_ge(y_evicted, t - 1)
                state = h_state(d, c != first_chunk(d))
                for i in range(4):
                    h = 4 * jb + i
                    out = psum[64 * (h % 2):64 * (h % 2) + 64, 2 + t % 2, (i // 2) * P:(i // 2 + 1) * P]
                    mm(out, xdt(c, d)[:, h * HD:(h + 1) * HD], decay[:, b % 3, i * P:(i + 1) * P], d == 0 and i < 2, False, True)
                    ins = mm(out, state[:, h * HD:(h + 1) * HD], eoff[:, b % 3, i * P:(i + 1) * P], False, d == 1, True)
                ins.then_inc(y_done, 1)

            running_sums(0)
            running_sums(1)
            for b in range(len(BATCHES)):
                if b + 2 < len(BATCHES):
                    running_sums(b + 2)
                outputs(b)
            pe.wait_ge(y_evicted, 16)
            pe.wait_ge(gsq_ready, 1)
            for g in range(G):
                for k in range(4):
                    ins = mm(bank(g // 2, (g % 2) * T, T), ones[:], z[:, 4 * g + k, :], k == 0, k == 3)
            ins.then_inc(gms_ready, 1)
            pe.wait_ge(gnorm_ready, 1)
            pe.wait_ge(gstd_ready, 1)
            for i in range(8):
                project("ssd_out", i, 8, so_evicted, 0, xbc, 16, 128)
            norm_sums(4)
            ffn(2)
            norm_sums(5)
            ffn(3)

            norm_sums(6)
            ada_sums(2)
            ada_sums(3)
            w = tile().rearrange("p (g k n) -> p g k n", g=4, k=2)
            pe.wait_ge(pooled_ready, 4)
            for g in range(4):
                for b in range(2):
                    for k in range(2):
                        ins = mm(bank(g, b * T, T), w[:, g, k, b * P:(b + 1) * P], pooled[:, 2 * g + k, :], k == 0, k == 1)
            ins.then_inc(weights_consumed, 1)
            norm_sums(7)
            ffn(4)
            norm_sums(FINAL)
            pe.wait_ge(std_ready, FINAL + 1)
            ada_sums(4)

            pe.wait_ge(boh_in, 16)
            pe.wait_ge(relx_in, 16)
            mm(psum[0:HEADS, 6, 0:BSTEP], relx[0:BUCKETS + 1, :], boh[0:BUCKETS + 1, :], True, True) \
                .then_inc(brow_done, 1)

            for l in range(2):
                norm_sums(9 + 2 * l)
                pe.wait_ge(u_ready, u_done(10 + 2 * l))

                def w_in(i):
                    project("w_in", i, 8, win_evicted, 8 * l, u, KB, 256)

                for i in range(4):
                    w_in(i)
                pe.wait_ge(qksq_ready, l + 1)
                for b in range(5):
                    ins = mm(bank(4 + b // 2, (b % 2) * T, T), bones[:], sq[:, b, :], True, True)
                ins.then_inc(qkms_ready, 1)
                w_in(4)
                pe.wait_ge(win_evicted, 8 * l + 4)
                for b in range(2):
                    ins = mm(bank(7, b * T, T), bones[:], proj[:, 14 + b, :], True, True)
                ins.then_inc(vsum_done, 1)
                pe.wait_ge(qkstd_ready, l + 1)
                for t in range(TT):
                    ins = transpose(bank(5, t * P, P), proj[:, 5, t * P:(t + 1) * P])
                ins.then_inc(vt_done, 1)
                w_in(5)
                pe.wait_ge(vsq_ready, l + 1)
                for b in range(2):
                    ins = mm(bank(4, b * T, T), bones[:], vsq[:, b, :], True, True)
                ins.then_inc(vvar_done, 1)
                w_in(6)
                pe.wait_ge(vn_ready, l + 1)
                for t in range(TT):
                    for b in range(2):
                        ins = transpose(bank(7, t * T + b * P, P), vc[:, b, t * P:(t + 1) * P])
                ins.then_inc(vnt_done, 1)
                w_in(7)
                pe.wait_ge(vntok_ready, l + 1)
                pe.wait_ge(sgw_ready, 1)
                pe.wait_ge(rows_in, 32)
                pe.wait_ge(vstd_ready, l + 1)
                for t in range(TT):
                    for g in range(4):
                        out = psum[64 * (g % 2):64 * (g % 2) + 64, 6, t * T + (g // 2) * P:t * T + (g // 2 + 1) * P]
                        mm(out, vntok[:, t, g * DH:(g + 1) * DH], sgw[:, l, g, :], True, False)
                        ins = mm(out, ones[0:1, 0:DH], rowp[0:1, l, g, :], False, True)
                ins.then_inc(mix_done, 1)
                pe.wait_ge(qk_ready, l + 1)
                pe.wait_ge(bias_in, 16)
                pe.wait_ge(vtok_ready, l + 1)
                pe.wait_ge(win_evicted, 8 * l + 8)
                for n in range(TT):
                    r = 2 * l + n
                    if n:
                        pe.wait_ge(pexp_ready, r)
                    lo = P if n == 0 else 0
                    for h in range(HEADS):
                        out = bank(place(h) // 2, (place(h) % 2) * T + lo, T - lo)
                        part = slice(64 * (h % 2), 64 * (h % 2) + 64)
                        mm(out, flip[:], bias_t[:, h, lo:T], True, False)
                        ins = mm(out, proj[part, h // 2, n * P:(n + 1) * P],
                                 kd[part, h // 4, (n - 1) * P + lo:(n + 1) * P], False, True)
                    ins.then_inc(logits_done, 1)
                    pe.wait_ge(prob_ready, r + 1)
                    if n:
                        pe.wait_ge(pv_evicted, r)
                    else:
                        pe.wait_ge(heads_ready, 2 * l + 1)
                    for h in range(HEADS):
                        for s in range(lo // P, 2):
                            ins = transpose(bank(4 + h // 2, (h % 2) * T + s * P, P), prob[:, h, s * P:(s + 1) * P])
                    ins.then_inc(probT_done, 1)
                    pe.wait_ge(probT_ready, r + 1)
                    for h in range(HEADS):
                        out = psum[64 * (h % 2):64 * (h % 2) + 64, 4, (h // 2) * P:(h // 2 + 1) * P]
                        for s in range(lo // P, 2):
                            ins = mm(out, vtok[:, n - 1 + s, (h // 4) * DH:(h // 4 + 1) * DH], probT[:, place(h), s, :],
                                     s == lo // P, s == 1)
                    ins.then_inc(pv_done, 1)
                pe.wait_ge(osq_ready, l + 1)
                pe.wait_ge(pv_evicted, 2 * l + 2)
                for k in range(8):
                    g = 0 if k < 4 else 1 + (k - 4) // 2
                    ins = mm(bank(5 + g // 2, (g % 2) * T, T), ones[:], sq[:, k, :], k in (0, 4, 6), k in (3, 5, 7))
                ins.then_inc(oms_ready, 1)
                pe.wait_ge(merged_ready, l + 1)
                for i in range(4):
                    project("w_out", i, 4, None, 0, merged, KB, 256)
                norm_sums(10 + 2 * l)
                pe.wait_ge(u_ready, u_done(11 + 2 * l))
                for t in range(TT):
                    for k in range(KB):
                        ins = transpose(bank(4 + 2 * t + k // 4, (k % 4) * P, P), u[:, k, t * P:(t + 1) * P])
                ins.then_inc(h2t_done, 1)

                def key_products(m):
                    pe.wait_ge(wq_evicted, 8 * l + 2 * m + 2)
                    if m == 0:
                        pe.wait_ge(keys_in, 16 * (l + 1))
                        pe.wait_ge(h2t_ready, l + 1)
                    for a in range(4 * m, 4 * m + 4):
                        ins = mm(bank(4 + m, (a % 4) * P, P), qT[:, a, 0:P], keys[:, a, :], True, True)
                    ins.then_inc(keys_done, 1)

                for i in range(8):
                    project("wq", i, 8, wq_evicted, 8 * l, u, KB, 256)
                    if i in (3, 5, 7):
                        key_products((i - 3) // 2)
                key_products(3)
                for a in range(16):
                    ins = mm(bank(a // 4, (a % 4) * P, P), qT[:, a, P:T], keys[:, a, :], True, True)
                ins.then_inc(keys_done, 1)
                pe.wait_ge(score_ready, 5 * l + 5)
                for t in range(TT):
                    pe.wait_ge(ytok_ready, 2 * l + t + 1)
                    for k in range(KB):
                        ins = transpose(bank(2 * t + k // 4, (k % 4) * P, P), ytok[:, t, k * P:(k + 1) * P])
                    ins.then_inc(yt_done, 1)

        @block.scalar
        def _(act):
            def f(out, in_, fn, **kw):
                return nc.scalar.activation(out, in_, fn, **kw)

            act.dma_start(xT[:], A["xT"]).then_inc(x_in, 16)
            act.dma_start(hT[:], A["hT"]).then_inc(h_in_sem, 16)
            act.dma_start(rowp[:], A["sgu_b"]).then_inc(rows_in, 16)
            act.dma_start(sink[:], A["sink"].unsqueeze(0).to_broadcast([P, 2, HEADS])).then_inc(rows_in, 16)
            act.wait_ge(cols_in, 16)
            f(silu_c[:, :, 0], col("c", 0, 8), ACT.Silu).then_inc(silu_c_ready, 1)
            f(silu_c[:, :, 1], col("c_ctx", 0, 8), ACT.Silu).then_inc(silu_c_ready, 1)
            f(silu_c[:, :, 2], col("c2", 0, 8), ACT.Silu).then_inc(silu_c_ready, 1)
            f(exp_a[:], cols[0:64, COLS["a_log"][0]:COLS["a_log"][0] + 1], ACT.Exp).then_inc(act_step, 1)

            def norm(n):
                src, _, shift, _, (ready, value), _ = NORMS[n]
                act.wait_ge(ready, value)
                if n:
                    act.wait_ge(ms_ready, n)
                f(sq[:], src[:], ACT.Square).then_inc(sq_ready, 1)
                act.wait_ge(ms_ready, n + 1)
                f(std[:], bank(7, 0, T), ACT.Sqrt, scale=1.0 / D, bias=eps[:, 0:1]).then_inc(std_ready, 1)
                if n == FINAL:
                    return
                for k in range(KB):
                    act.wait_ge(un_ready, u_done(n) + k + 1)
                    f(u[:, k, :], u[:, k, :], ACT.Identity, bias=shift[:, k:k + 1]).then_inc(u_ready, 1)
                if n in FFN_NORM:
                    for k in range(0, KB, 2):
                        act.wait_ge(u_ready, u_done(n) + k + 2)
                        f(u_hi[:, k:k + 2, :], u[:, k:k + 2, :], ACT.Identity).then_inc(u_high, 1)

            def high(n, t, it=0):
                i = BASE[f"ffn{n}"] + t
                act.wait_ge(weights_in[i % RING], it * 16 + 16 * (i // RING + 1))
                if t >= HIGH_RING:
                    act.wait_ge(weights_consumed, it * 6 + consumed(f"ffn{n}", t - HIGH_RING))
                elif n:
                    act.wait_ge(weights_consumed, consumed("ssd_out", 7) if n == 2 else consumed(f"ffn{n - 1}", FFN_TILES - 1))
                f(whigh[:, t % HIGH_RING, :], wring[:, i % RING, :], ACT.Identity).then_inc(w_high, 1)

            def norm_ffn(m, n):
                base = n * FFN_ITERS
                if n == 0:
                    norm(m)
                for t in range(3):
                    high(n, t)
                if n:
                    norm(m)

                def silu(i, t, it=0):
                    act.wait_ge(weights_consumed, it * 6 + consumed(f"ffn{n}", t))
                    if i >= 2:
                        act.wait_ge(hid_full, it * 2 + (base + i - 1))
                    f(sg[:, i % 2, :], bank(4 + i % 2), ACT.Silu).then_inc(silu_ready, 1)

                def high_hidden(i, it=0):
                    act.wait_ge(hid_full, it * 2 + (base + i + 1))
                    f(hid_hi[:, i % 2, :], hid[:, i % 2, :], ACT.Identity).then_inc(hid_high, 1)

                silu(0, 0)
                high(n, 3)
                high(n, 4)
                high_hidden(0)
                silu(1, 2)
                high(n, 5)
                high(n, 6)
                high_hidden(1)
                high(n, 7)
                silu(2, 5)
                high(n, 8)
                high_hidden(2)
                with act.Fori(0, (FFN_ITERS - 3) // 2, 1) as it:
                    for j in range(2):
                        high(n, 9 + 3 * j, it)
                        high(n, 10 + 3 * j, it)
                        silu(3 + j, 8 + 3 * j, it)
                        high(n, 11 + 3 * j, it)
                        high_hidden(3 + j, it)

            act.wait_ge(eps_set, 1)
            norm_ffn(0, 0)
            norm_ffn(1, 1)

            def ssd_project(lat):
                name = "proj_lat" if lat else "proj_ctx"
                act.wait_ge(weights_consumed, consumed(name, 0))
                if lat:
                    act.wait_ge(da_evicted, 1)
                    act.wait_ge(da_done, 1)
                f(dt64[:, 0, :], psum[0:64, 0, 0:T], ACT.Identity, bias=cols[0:64, COLS["dt_bias"][0]:COLS["dt_bias"][0] + 1]) \
                    .then_inc(proj_evicted, 1)
                nconv = 12 if lat else 10

                def silu_conv(i):
                    act.wait_ge(conv_done, 10 * lat + i + 1)
                    f(xbc[:, 2 * i:2 * i + 2, :], xbc[:, 2 * i:2 * i + 2, :], ACT.Silu).then_inc(xbc_ready, 1)

                for i in range(nconv):
                    t = 10 * lat + i
                    act.wait_ge(weights_consumed, consumed(name, 1 + i))
                    if t >= 3:
                        act.wait_ge(conv_done, t - 2)
                    f(raw[:, t % 3, :, 2:2 + T], bank((1 + i) % 4).rearrange("p (a b) -> p a b", a=2), ACT.Identity) \
                        .then_inc(proj_evicted, 1)
                    if i == 0:
                        act.wait_ge(negabs_ready, lat + 1)
                        f(dtw[:, 0, :], dtw[:, 0, :], ACT.Exp).then_inc(expabs_ready, 1)
                    if i:
                        silu_conv(i - 1)
                silu_conv(nconv - 1)
                for i in range(8 if lat else 0):
                    act.wait_ge(weights_consumed, consumed(name, 13 + i))
                    f(z[:, 2 * i:2 * i + 2, :], bank((13 + i) % 4).rearrange("p (a b) -> p a b", a=2), ACT.Silu) \
                        .then_inc(proj_evicted, 1)
                act.wait_ge(diff_ready, lat + 1)
                f(diff[:], diff[:], ACT.Exp).then_inc(decay_ready, 1)
                f(eal[:], bank(6, 384, 128).rearrange("p (a b) -> p a b", a=NCH), ACT.Exp).then_inc(decay_ready, 1)

            norm(2)
            ssd_project(0)
            norm(3)
            ssd_project(1)
            for b in range(NCH * (H // 4) * 2):
                act.wait_ge(bc_done, b + 1)
                if b >= 3:
                    act.wait_ge(y_done, b - 2)
                act.wait_ge(seg_ready, b + 1)
                f(eoff[:, b % 3, :], bank(BC_BANK[b % 3]), ACT.Exp).then_inc(expbc_ready, 1)
                f(decay[:, b % 3, :], decay[:, b % 3, :], ACT.Exp).then_inc(expseg_ready, 1)
            act.wait_ge(gated_ready, 2)
            f(z[:], xbc[:, 0:XB, :], ACT.Square).then_inc(gsq_ready, 1)
            act.wait_ge(gms_ready, 1)
            f(grstd, psum[:, 0:2, :].rearrange("p a (b c) -> p (a b) c", b=2), ACT.Sqrt, scale=1.0 / 512, bias=eps[:, 0:1]) \
                .then_inc(gstd_ready, 1)
            norm_ffn(4, 2)
            norm_ffn(5, 3)
            norm(6)
            norm_ffn(7, 4)
            norm(FINAL)
            act.wait_ge(bias_in, 16)
            for l in range(2):
                norm(9 + 2 * l)
                for p, i in enumerate(W_IN_ORDER):
                    act.wait_ge(weights_consumed, consumed(f"w_in{l}", p))
                    f(proj[:, 2 * i:2 * i + 2, :], bank(p % 4).rearrange("p (a b) -> p a b", a=2), ACT.Identity) \
                        .then_inc(win_evicted, 1)
                    if p == 2:
                        act.wait_ge(win_evicted, 8 * l + 3)
                        f(sq[:, 0:5, :], proj[:, 0:5, :], ACT.Square).then_inc(qksq_ready, 1)
                    if p == 3:
                        act.wait_ge(qkms_ready, l + 1)
                        f(rs5.rearrange("p a b -> p (a b)"), psum[:, 4:7, :].rearrange("p a b -> p (a b)")[:, 0:5 * T], ACT.Sqrt,
                          scale=1.0 / DH, bias=eps[:, 0:1]).then_inc(qkstd_ready, 1)
                    if p == 4:
                        act.wait_ge(vc_ready, l + 1)
                        f(vsq, vc, ACT.Square).then_inc(vsq_ready, 1)
                    if p == 5:
                        act.wait_ge(vvar_done, l + 1)
                        f(vrs, bank(4).rearrange("p (a b) -> p a b", a=2), ACT.Sqrt, scale=1.0 / DH, bias=eps[:, 0:1]) \
                            .then_inc(vstd_ready, 1)
                for n in range(TT):
                    r = 2 * l + n
                    lo = P if n == 0 else 0
                    act.wait_ge(nmax_ready, r + 1)
                    if n:
                        act.wait_ge(probT_done, r)
                    for h in range(HEADS):
                        f(prob[:, h, lo:T], bank(h // 2, (h % 2) * T + lo, T - lo), ACT.Exp,
                          bias=small[:, 1, h:h + 1], accum_out=small[:, 2, h:h + 1])
                    f(small[:, 3, :], small[:, 3, :], ACT.Exp).then_inc(pexp_ready, 1)
                act.wait_ge(heads_ready, 2 * l + 2)
                act.wait_ge(pv_evicted, 2 * l + 2)
                f(sq[:], merged, ACT.Square).then_inc(osq_ready, 1)
                act.wait_ge(oms_ready, l + 1)
                f(ors[:, 0, :], bank(5, 0, T), ACT.Sqrt, scale=1.0 / 512, bias=eps[:, 0:1])
                f(ors[:, 1, :], bank(5, T, T), ACT.Sqrt, scale=1.0 / 256, bias=eps[:, 0:1])
                f(ors[:, 2, :], bank(6, 0, T), ACT.Sqrt, scale=1.0 / 256, bias=eps[:, 0:1]).then_inc(ostd_ready, 1)
                norm(10 + 2 * l)
                def scores(m):
                    act.wait_ge(keys_done, 5 * l + m + 1)
                    f(score[0][:, 4 * m:4 * m + 4, :], bank(4 + m).rearrange("p (a b) -> p a b", a=4), ACT.Identity).then_inc(score_ready, 1)

                for i in range(8):
                    act.wait_ge(weights_consumed, consumed(f"wq{l}", i))
                    f(qT[:, 2 * i:2 * i + 2, :], bank(i % 4).rearrange("p (a b) -> p a b", a=2), ACT.Identity) \
                        .then_inc(wq_evicted, 1)
                    if i in (3, 5, 7):
                        scores((i - 3) // 2)
                scores(3)
                act.wait_ge(keys_done, 5 * l + 5)
                f(score[1].rearrange("p a b -> p (a b)"), psum[:, 0:4, :].rearrange("p a b -> p (a b)"), ACT.Identity).then_inc(score_ready, 1)
                for t in range(TT):
                    act.wait_ge(gsub_ready, 2 * l + t + 1)
                    f(gsub, gsub, ACT.Exp).then_inc(gexp_ready, 1)
                for t in range(TT):
                    act.wait_ge(dots_ready, 2 * l + t + 1)
                    f(wexp[:, t, :], dots[:, t, :], ACT.Gelu).then_inc(gelu_ready, 1)

        @block.vector
        def _(dve):
            steps = [0]
            v = nc.vector

            def tick(ins):
                ins.then_inc(dve_step, 1)
                steps[0] += 1
                return ins

            def settle():
                dve.wait_ge(dve_step, steps[0])

            def tt(out, a, b, op):
                return v.tensor_tensor(out, a, b, op)

            def stt(out, a, s, b, op0, op1):
                return v.scalar_tensor_tensor(out=out, in0=a, scalar=s, in1=b, op0=op0, op1=op1)

            def ts(out, a, s1, s2=None, op0=ALU.mult, op1=None):
                return v.tensor_scalar(out, a, s1, s2, op0, op1) if op1 is not None else v.tensor_scalar(out, a, s1, None, op0)

            v.memset(eps[:], EPS).then_inc(eps_set, 1)
            tick(v.memset(bones[:], 0.0))
            settle()
            tick(v.memset(bones[0:64, 0:64], 1.0))
            v.memset(bones[64:P, 64:P], 1.0).then_inc(bones_set, 1)
            v.memset(gsum[0:1, 0, 0:1], 0.0).then_inc(rows_free, SLOTS)
            v.memset(gsum[0:1, 0, 1:2], 0.0).then_inc(ada_step, ADA_FREE)

            def mods_first(groups, n):
                for g in groups:
                    dve.wait_ge(weights_consumed, consumed("ada0", 4 * g + 3))
                    v.tensor_copy(arow[:, g, :], psum[0:2, 2 * g:2 * g + 2, :].rearrange("p a b -> p (a b)")).then_inc(arow_ready, 1)
                dve.wait_ge(arow_turned, n)
                lo, hi = KB * groups[0], KB * (groups[-1] + 1)
                ps = bank(6, 0, 48).rearrange("p (a b) -> p a b", b=2)
                tick(tt(mod0[:, lo:hi], ps[:, lo:hi, 0], col("ada_b0", lo, hi - lo), ALU.add))
                tt(mod0c[:, lo:hi], ps[:, lo:hi, 1], col("ada_b0", lo, hi - lo), ALU.add).then_inc(mods_ready, 1)

            def mods(n):
                name, layer, group, count, _, also = ADA[n]
                out, b = {"ada_w": ((mod0, mod1)[layer][:], f"ada_b{layer}"), "w_ada2": (mod2[:, layer, :], f"ada_b2_{layer}")}[name]
                dve.wait_ge(ada_summed, n + 1)
                if also:
                    tick(tt(mod0c[:, KB * group:KB * (group + also)], bank(ADA_BANK[n], KB * count, KB * also), col(b, KB * group, KB * also), ALU.add))
                tt(out[:, KB * group:KB * (group + count)], bank(ADA_BANK[n], 0, KB * count), col(b, KB * group, KB * count), ALU.add) \
                    .then_inc(mods_ready, 1)

            def norm(n):
                src, g, _, scale, (ready, value), mods_count = NORMS[n]
                dve.wait_ge(ready, value)
                if n == FINAL:
                    dve.wait_ge(std_ready, n + 1)
                    dve.wait_ge(ms_ready, n + 1)
                    tick(v.reciprocal(rstd[:], std[:]))
                    settle()
                    for k in range(KB):
                        ins = stt(xT[:, k, :], xT[:, k, :], col("final_g", k), rstd[:], ALU.mult, ALU.mult)
                    ins.then_inc(x_ready, 1)
                    return
                dve.wait_ge(mods_ready, mods_count)
                tick(stt(gscale[:, n, :], scale, 1.0, g, ALU.add, ALU.mult))
                dve.wait_ge(std_ready, n + 1)
                tick(v.reciprocal(rstd[:], std[:]))
                settle()
                if n == 3:
                    dve.wait_ge(weights_consumed, consumed("proj_ctx", 10))
                for k in range(KB):
                    stt(u[:, k, :], src[:, k, :], gscale[:, n, k:k + 1], rstd[:], ALU.mult, ALU.mult).then_inc(un_ready, 1)
                if n in FFN_NORM:
                    for k in range(0, KB, 2):
                        dve.wait_ge(u_high, 4 * FFN_NORM.index(n) + k // 2 + 1)
                        tt(u_lo[:, k:k + 2, :], u[:, k:k + 2, :], u_hi[:, k:k + 2, :].bitcast(F32), ALU.subtract).then_inc(u_low, 1)

            def low(n, t, it=0):
                dve.wait_ge(w_high, it * 6 + (FFN_TILES * n + t + 1))
                slot = (BASE[f"ffn{n}"] + t) % RING
                tt(wlow[:, slot, :], wring[:, slot, :], whigh[:, t % HIGH_RING, :].bitcast(F32), ALU.subtract).then_inc(w_low, 1)

            def low_first(n):
                for t in range(3):
                    low(n, t)

            def ffn(n):
                base = n * FFN_ITERS
                name = f"ffn{n}"

                def product(i, t, it=0):
                    dve.wait_ge(weights_consumed, it * 6 + consumed(name, t))
                    dve.wait_ge(silu_ready, it * 2 + (base + i + 1))
                    tt(hid[:, i % 2, :], sg[:, i % 2, :], bank(6 + i % 2), ALU.mult).then_inc(hid_full, 1)

                def low_hidden(i, it=0):
                    dve.wait_ge(hid_high, it * 2 + (base + i + 1))
                    tt(hid_lo[:, i % 2, :], hid[:, i % 2, :], hid_hi[:, i % 2, :].bitcast(F32), ALU.subtract).then_inc(hid_ready, 1)

                if n == 0:
                    dve.wait_ge(mods_ready, 2)
                tick(ts(hgate[:, n, :], FFN_GATE[n], 0.5))
                _, _, _, count, vec, also = ADA[n]
                sums = asum2 if n == 2 else asum
                tick(v.memset(sums[:, 0:count + also, :], 0.0))
                low(n, 3)
                low(n, 4)
                product(0, 1)
                low_hidden(0)
                low(n, 5)
                product(1, 3)
                low(n, 6)
                low_hidden(1)
                low(n, 7)
                low(n, 8)
                product(2, 6)
                low_hidden(2)
                settle()
                if n == 0:
                    dve.wait_ge(silu_c_ready, 3)
                slot_uses = [ADA_TURNS * sum(ADA[m][3] > j for m in range(n)) for j in range(6)]

                def condition(t, it):
                    dve.wait_ge(ada_in[t], it * 16 + 16 * (slot_uses[t] + 1))
                    for k in range(2):
                        for which in range(1 + (t < also)):
                            if k and not which:
                                dve.wait_ge(ada_step, it * ADA_STEPS[n] + (ADA_BASE[n] + ada_last(n, t) - 1 - (t < also)))
                            dst = sums[:, count + t if which else t, :]
                            stt(dst, aring[:, t % ADA_RING, k, :], cpair[:, k, (1 if which else vec):(1 if which else vec) + 1], dst,
                                ALU.mult, ALU.add).then_inc(ada_step, 1)

                with dve.Fori(0, ADA_TURNS, 1) as it:
                    dve.wait_ge(ada_step, it * ADA_STEPS[n] + ADA_BASE[n])
                    v.tensor_copy(cpair[:], silu_c[:, bass.ds(it * 2, 2), :]).then_inc(cpair_set, 1)
                    dve.wait_ge(cpair_set, it + (ADA_TURNS * n + 1))
                    for j in range(2):
                        for t in range(3):
                            low(n, 9 + 3 * j + t, it)
                            if t == 2:
                                product(3 + j, 9 + 3 * j, it)
                                low_hidden(3 + j, it)
                            if 3 * j + t < count:
                                condition(3 * j + t, it)
                dve.wait_ge(weights_consumed, consumed(name, 32))
                settle()
                dst = FFN_DST[n]
                for d in range(KB):
                    ins = stt(dst[:, d, :], bank(d // 2, (d % 2) * T, T), hgate[:, n, d:d + 1], dst[:, d, :], ALU.mult, ALU.add)
                ins.then_inc(h_ready if n == 1 else x_ready, 1)

            dve.wait_ge(cols_in, 16)
            mods_first((0, 1), 1)
            norm(0)
            mods_first((2,), 2)
            low_first(0)
            ffn(0)
            low_first(1)
            norm(1)
            mods(0)
            ffn(1)
            norm(2)
            mods(1)

            tick(v.memset(raw[:, :, :, 0:2], 0.0))
            tick(v.memset(raw[:, :, :, 2 + T:], 0.0))
            settle()

            def softplus(lat):
                val, dt, a = dt64[:, 0, :], dt64[:, 1, :], dt64[:, 2, :]
                e, r, s2 = dtw[:, 0, :], dtw[:, 1, :], dtw[:, 2, :]
                dve.wait_ge(proj_evicted, 11 * lat + 1)
                if lat:
                    dve.wait_ge(da_done, 1)
                stt(e, val, -1.0, val, ALU.mult, ALU.min).then_inc(negabs_ready, 1)
                yield
                dve.wait_ge(expabs_ready, lat + 1)
                tick(ts(r, e, 2.0, op0=ALU.add))
                settle()
                tick(v.reciprocal(r, r))
                settle()
                tick(tt(r, r, e, ALU.mult))
                settle()
                tick(tt(s2, r, r, ALU.mult))
                settle()
                tick(ts(e, s2, 1.0 / 15))
                settle()
                for odd in (13, 11, 9, 7, 5, 3):
                    tick(stt(e, e, 1.0 / odd, s2, ALU.add, ALU.mult))
                    settle()
                tick(stt(e, e, 1.0, r, ALU.add, ALU.mult))
                tick(ts(val, val, 0.0, op0=ALU.max))
                settle()
                tick(stt(dt, e, 2.0, val, ALU.mult, ALU.add))
                settle()
                dve.wait_ge(act_step, 1)
                ts(a, dt, exp_a[:, 0:1], -1.0, ALU.mult, ALU.mult).then_inc(dt_ready, 1)
                yield

            def ssd_conv(lat):
                name = "proj_lat" if lat else "proj_ctx"
                sp_steps = softplus(lat)
                next(sp_steps)
                for i in range(12 if lat else 10):
                    t = 10 * lat + i
                    dve.wait_ge(proj_evicted, 11 * lat + 2 + i)
                    if lat and i == 0:
                        dve.wait_ge(tok_done, 10)
                    for k in range(CONV_W):
                        for b in range(2):
                            blk = 2 * i + b
                            src = raw[:, t % 3, b, k:k + T]
                            w = col("conv_w", 24 * k + blk)
                            if k == 0:
                                ins = ts(xbc[:, blk, :], src, w, col("conv_b", blk), ALU.mult, ALU.add)
                            else:
                                ins = stt(xbc[:, blk, :], src, w, xbc[:, blk, :], ALU.mult, ALU.add)
                        if k < CONV_W - 1:
                            tick(ins)
                            settle()
                        else:
                            ins.then_inc(conv_done, 1)
                    if i == 1:
                        next(sp_steps)

            def sums(lat):
                dve.wait_ge(da_done, lat + 1)
                if lat:
                    settle()
                v.tensor_copy(da_tok.rearrange("p a b -> p (a b)"), bank(6, 0, 256)).then_inc(da_evicted, 1)
                dve.wait_ge(cum_done, lat + 1)
                cum = bank(6, 256, 128).rearrange("p (a b) -> p a b", a=NCH)
                tot = bank(6, 384, 128).rearrange("p (a b) -> p a b", a=NCH)
                tick(v.tensor_copy(acum, cum))
                settle()
                tt(diff, tot, acum, ALU.subtract).then_inc(diff_ready, 1)

            def tokens(lat):
                sums(lat)
                for i in range(10):
                    g, c = i // 2, i % 2
                    dve.wait_ge(tok_done, 10 * lat + i + 1)
                    dst = xtok[:, c, 512 * g:512 * g + 512] if g < 4 else btok[:, c, :]
                    v.tensor_copy(dst, bank(4 + i % 2)).then_inc(tok_evicted, 1)
                dve.wait_ge(decay_ready, 2 * lat + 2)
                dve.wait_ge(tok_evicted, 10 * lat + 10)
                dve.wait_ge(da_evicted, lat + 1)
                tick(tt(wdt, diff, da_tok[:, 0:2, :], ALU.mult))
                settle()

            def weigh(out, c, w):
                return tt(out.rearrange("p (h q) -> p h q", h=H), xtok[:, c, :].rearrange("p (h q) -> p h q", h=H),
                          w.unsqueeze(2).to_broadcast([P, H, HD]), ALU.mult)

            def heads3(a):
                return a.rearrange("p (h q) -> p h q", h=H)

            psum_state = psum[:, 0:4, :].rearrange("p a b -> p (a b)")

            def states(k, d, c, dst, src, first):
                if k >= 2:
                    dve.wait_ge(state_done, k - 1)
                weigh(xw[:, k % 2, :], c, wdt[:, c, 32 * d:32 * d + 32]).then_inc(xw_ready, 1)
                if not first:
                    tick(tt(heads3(dst), heads3(src), eal[:, c, 32 * d:32 * d + 32].unsqueeze(2).to_broadcast([P, H, HD]), ALU.mult))
                    settle()
                dve.wait_ge(state_done, k + 1)
                if first:
                    v.tensor_copy(dst, psum_state).then_inc(state_added, 1)
                else:
                    tt(dst, dst, psum_state, ALU.add).then_inc(state_added, 1)
                dve.wait_ge(state_added, k + 1)

            ssd_conv(0)
            tokens(0)
            for d in range(2):
                c0 = first_chunk(d)
                states(2 * d, d, c0, h_first[:, d, :], None, True)
                states(2 * d + 1, d, 1 - c0, h_first[:, d, :], h_first[:, d, :], False)
            norm(3)
            ssd_conv(1)
            tokens(1)
            for d in range(2):
                if d == 1:
                    dve.wait_ge(ms_ready, 4)
                states(4 + d, d, first_chunk(d), h_state(d, True), h_first[:, d, :], False)
            dve.wait_ge(cb_done, 1)
            for c in range(NCH):
                for d, m in enumerate((tri, trisuf)):
                    tt(cbm[:, c, d, :].rearrange("p (g l) -> p g l", g=G), bank(4 + c).rearrange("p (g l) -> p g l", g=G),
                       m[:, :].unsqueeze(1).to_broadcast([P, G, P]), ALU.mult).then_inc(cbm_ready, 1)
            dve.wait_ge(cbm_ready, 4)
            BATCHES = [(c, jb, d) for c in range(NCH) for jb in range(H // 4) for d in range(2)]

            def segments(b):
                c, jb, d = BATCHES[b]
                dve.wait_ge(bc_done, b + 1)
                if b >= 3:
                    dve.wait_ge(y_done, b - 2)
                for i in range(4):
                    h = 32 * d + 4 * jb + i
                    ins = ts(decay[:, b % 3, i * P:(i + 1) * P], bank(BC_BANK[b % 3], i * P, P), acum[:, c, h:h + 1], 0.0,
                             ALU.subtract, ALU.min)
                ins.then_inc(seg_ready, 1)

            def weights(b):
                c, jb, d = BATCHES[b]
                dve.wait_ge(expseg_ready, b + 1)
                g = jb // 2
                tt(decay[:, b % 3, :].rearrange("p (i l) -> p i l", i=4), decay[:, b % 3, :].rearrange("p (i l) -> p i l", i=4),
                   cbm[:, c, d, g * P:(g + 1) * P].unsqueeze(1).to_broadcast([P, 4, P]), ALU.mult).then_inc(m_ready, 1)

            def skip(b):
                c, jb, d = BATCHES[b]
                dve.wait_ge(y_done, b + 1)
                for j in range(2):
                    blk = 2 * jb + j
                    y = xbc[:, blk, c * P:(c + 1) * P]
                    ins = stt(y, y, col("ssd_d", blk), bank(2 + (c * 8 + jb) % 2, j * P, P), ALU.mult, ALU.add)
                ins.then_inc(y_evicted, 1)

            dve.wait_ge(state_done, 6)
            for c in range(NCH):
                for d in range(2):
                    if c:
                        dve.wait_ge(xdt_ready, 2 * c + d)
                    weigh(xdt(c, d), c, da_tok[:, c, 32 * d:32 * d + 32]).then_inc(xdt_ready, 1)
            for b in range(len(BATCHES)):
                segments(b)
                if b >= 3 and BATCHES[b - 3][2] == 1:
                    skip(b - 3)
                if b >= 1:
                    weights(b - 1)
            weights(31)
            skip(29)
            skip(31)
            dve.wait_ge(y_evicted, 16)
            tt(xbc[:, 0:8, :], xbc[:, 0:8, :], z[:, 0:8, :], ALU.mult).then_inc(gated_ready, 1)
            tt(xbc[:, 8:16, :], xbc[:, 8:16, :], z[:, 8:16, :], ALU.mult).then_inc(gated_ready, 1)
            dve.wait_ge(gstd_ready, 1)
            tick(v.reciprocal(grstd, grstd))
            settle()
            for k in range(XB):
                ins = stt(xbc[:, k, :], xbc[:, k, :], col("ssd_ng", k), grstd[:, k // 4, :], ALU.mult, ALU.mult)
            ins.then_inc(gnorm_ready, 1)
            for i in range(8):
                dve.wait_ge(weights_consumed, consumed("ssd_out", i))
                ins = stt(xT[:, i, :], bank(i % 4, 0, T), mod0[:, 40 + i:41 + i], xT[:, i, :], ALU.mult, ALU.add)
                if i < 7:
                    ins.then_inc(so_evicted, 1)
            ins.then_inc(x_ready, 1)
            low_first(2)
            norm(4)
            ffn(2)
            low_first(3)
            norm(5)
            ffn(3)
            norm(6)

            dve.wait_ge(u_ready, u_done(7))
            dve.wait_ge(rcnt_in, 16)
            tick(v.memset(vpad, 0.0))
            settle()
            for g in range(4):
                ug = u[:, 2 * g:2 * g + 2, :].rearrange("p a (r c) -> p (a r) c", r=4)
                tick(v.tensor_copy(vpad[:, :, 8:72], ug))
                settle()
                tick(tt(pa[:, :, 1:80], vpad[:, :, 0:79], vpad[:, :, 1:80], ALU.add))
                settle()
                cur, oth, lo, hi = pa, pb, 1, 80
                for s in (1, 2, 4)[:g]:
                    lo, hi = lo + s, hi - s
                    tick(tt(oth[:, :, lo:hi], cur[:, :, lo - s:hi - s], cur[:, :, lo + s:hi + s], ALU.add))
                    settle()
                    cur, oth = oth, cur
                cs = cur[:, :, 8:72].rearrange("p (a r) c -> p a r c", a=2)
                o = psum2
                if g == 0:
                    tick(v.tensor_copy(o[:, :, 0:1, :], cs[:, :, 0:1, :]))
                    for a in range(2):
                        tick(tt(o[:, a, 1:4, :], cs[:, a, 0:3, :], cs[:, a, 1:4, :], ALU.add))
                else:
                    for a in range(2):
                        tick(tt(prow[:, a, 0:3, :], cs[:, a, 0:3, :], cs[:, a, 1:4, :], ALU.add))
                    settle()
                    if g == 1:
                        tick(v.tensor_copy(o[:, :, 0, :], prow[:, :, 0, :]))
                        tick(tt(o[:, :, 1, :], prow[:, :, 0, :], cs[:, :, 2, :], ALU.add))
                        tick(tt(o[:, :, 2, :], prow[:, :, 0, :], prow[:, :, 2, :], ALU.add))
                        tick(tt(o[:, :, 3, :], prow[:, :, 2, :], cs[:, :, 1, :], ALU.add))
                    else:
                        for r in range(4):
                            tick(tt(o[:, :, r, :], prow[:, :, 0, :], prow[:, :, 2, :], ALU.add))
                settle()
                of = o.rearrange("p a r c -> p a (r c)")
                tick(tt(of, of, rcnt[:, g:g + 1, :].to_broadcast([P, 2, T]), ALU.mult))
                settle()
                tt(pooled[:, 2 * g:2 * g + 2, :], of, u[:, 2 * g:2 * g + 2, :], ALU.subtract).then_inc(pooled_ready, 1)
                dve.wait_ge(pooled_ready, g + 1)
            mods(2)
            mods(3)
            dve.wait_ge(weights_consumed, consumed("pool", 0))
            for k in range(KB):
                tick(ts(pooled[:, k, :], bank(k // 2, (k % 2) * T, T), col("pool_b", k), col("pool_scale", k), ALU.add, ALU.mult))
            settle()
            for k in range(KB):
                ins = stt(xT[:, k, :], pooled[:, k, :], mod1[:, 40 + k:41 + k], xT[:, k, :], ALU.mult, ALU.add)
            ins.then_inc(x_ready, 1)
            low_first(4)
            norm(7)
            ffn(4)
            norm(FINAL)
            mods(4)

            dve.wait_ge(brow_done, 1)
            v.tensor_copy(brow[0:HEADS, :], psum[0:HEADS, 6, 0:BSTEP]).then_inc(brow_ready, 1)
            dve.wait_ge(sgw_in, 16)
            tt(sgw.rearrange("p a g t -> p (a g) t"), sgw.rearrange("p a g t -> p (a g) t"),
               tri[:, :].unsqueeze(1).to_broadcast([P, 8, P]), ALU.mult).then_inc(sgw_ready, 1)

            def top16(vals, idx, src, spare, lo, hi):
                for i in range(lo, hi):
                    ins = v.max(out=vals[:, i, 0:8], in_=src[:, i, :])
                tick(ins)
                settle()
                for i in range(lo, hi):
                    v.max_index(out=idx[:, i, 0:8], in_max=vals[:, i, 0:8], in_values=src[:, i, :])
                    ins = v.match_replace(out=spare[:, i, :], in_to_replace=vals[:, i, 0:8], in_values=src[:, i, :], imm_value=-3.0e38)
                tick(ins)
                settle()
                for i in range(lo, hi):
                    ins = v.max(out=vals[:, i, 8:16], in_=spare[:, i, :])
                tick(ins)
                settle()
                for i in range(lo, hi):
                    ins = v.max_index(out=idx[:, i, 8:16], in_max=vals[:, i, 8:16], in_values=spare[:, i, :])
                tick(ins)
                settle()

            def attend(l):
                def short_conv():
                    dve.wait_ge(win_evicted, 8 * l + 8)
                    tick(v.memset(zpad[:, :, 0:2], 0.0))
                    tick(tt(zpad[:, :, 2:], proj[:, 8:10, :], proj[:, 10:12, :], ALU.mult))
                    settle()
                    for k in range(3):
                        for b in range(2):
                            w = col("conv_w2", 6 * l + 2 * k + b)
                            if k == 0:
                                ins = ts(cacc[:, b, :], zpad[:, b, 0:T], w)
                            else:
                                ins = stt(cacc[:, b, :], zpad[:, b, k:k + T], w, cacc[:, b, :], ALU.mult, ALU.add)
                        tick(ins)
                        settle()
                    tick(tt(merged[:, 4:6, :], proj[:, 6:8, :], cacc, ALU.mult))

                dve.wait_ge(cols_in, 16)
                tick(ts(gq8, col("qg", l), DH ** -0.5))
                dve.wait_ge(qkstd_ready, l + 1)
                tick(v.reciprocal(rs5, rs5))
                settle()
                dve.wait_ge(win_evicted, 8 * l + 3)
                for b in range(5):
                    ins = stt(proj[:, b, :], proj[:, b, :], gq8 if b < 4 else col("kg", l), rs5[:, b, :], ALU.mult, ALU.mult)
                tick(ins)
                settle()
                for kv in range(KV):
                    for half in range(2):
                        ins = v.tensor_copy(kd[64 * half:64 * half + 64, kv, :], proj[64 * kv:64 * kv + 64, 4, :])
                ins.then_inc(qk_ready, 1)
                dve.wait_ge(vt_done, l + 1)
                v.tensor_copy(vtok.rearrange("p a b -> p (a b)"), bank(5, 0, T)).then_inc(vtok_ready, 1)
                dve.wait_ge(vsum_done, l + 1)
                stt(vc, bank(7).rearrange("p (a b) -> p a b", a=2), -1.0 / DH, proj[:, 14:16, :], ALU.mult, ALU.add) \
                    .then_inc(vc_ready, 1)
                dve.wait_ge(vstd_ready, l + 1)
                tick(v.reciprocal(vrs, vrs))
                settle()
                tt(vc, vc, vrs, ALU.mult).then_inc(vn_ready, 1)
                dve.wait_ge(vnt_done, l + 1)
                v.tensor_copy(vntok.rearrange("p a b -> p (a b)"), bank(7)).then_inc(vntok_ready, 1)
                dve.wait_ge(mix_done, l + 1)
                for t in range(TT):
                    ins = tt(merged[:, 6:8, t * P:(t + 1) * P], proj[:, 12:14, t * P:(t + 1) * P],
                             bank(6, t * T, T).rearrange("p (a b) -> p a b", a=2), ALU.mult)
                ins.then_inc(heads_ready, 1)
                dve.wait_ge(rows_in, 32)
                mx, nm, rsum, es, den = (small[:, i, :] for i in range(5))
                for n in range(TT):
                    r = 2 * l + n
                    lo = P if n == 0 else 0
                    dve.wait_ge(logits_done, r + 1)
                    logits = psum[:, 0:4, :].rearrange("p a (b s) -> p (a b) s", b=2)[:, :, lo:T]
                    tick(v.tensor_reduce(mx, logits, AX_X, ALU.max))
                    settle()
                    tick(tt(mx, mx, sink[:, l, :], ALU.max))
                    settle()
                    tick(ts(nm, mx, -1.0))
                    settle()
                    tt(es, sink[:, l, :], nm, ALU.add).then_inc(nmax_ready, 1)
                    if n == 0:
                        short_conv()
                    dve.wait_ge(pexp_ready, r + 1)
                    tick(tt(den, rsum, es, ALU.add))
                    settle()
                    tick(v.reciprocal(den, den))
                    settle()
                    tt(prob[:, :, lo:T], prob[:, :, lo:T], den.unsqueeze(2).to_broadcast([P, HEADS, T - lo]), ALU.mult) \
                        .then_inc(prob_ready, 1)
                    dve.wait_ge(probT_done, r + 1)
                    s0 = lo // P
                    v.tensor_copy(probT[:, :, s0:2, :].rearrange("p h s q -> p h (s q)"),
                                  psum[:, 4:8, :].rearrange("p a (b s) -> p (a b) s", b=2)[:, :, lo:T]).then_inc(probT_ready, 1)
                    dve.wait_ge(pv_done, r + 1)
                    v.tensor_copy(merged[:, 0:4, n * P:(n + 1) * P], bank(4).rearrange("p (a b) -> p a b", a=4)).then_inc(pv_evicted, 1)
                v.memset(gsum[:, 0, :], 0.0).then_inc(heads_ready, 1)
                dve.wait_ge(ostd_ready, l + 1)
                tick(v.reciprocal(ors, ors))
                settle()
                dve.wait_ge(pv_evicted, 2 * l + 2)
                for k in range(8):
                    g = 0 if k < 4 else 1 + (k - 4) // 2
                    ins = stt(merged[:, k, :], merged[:, k, :], col("out_g", 8 * l + k), ors[:, g, :], ALU.mult, ALU.mult)
                ins.then_inc(merged_ready, 1)
                for i in range(4):
                    dve.wait_ge(weights_consumed, consumed(f"w_out{l}", i))
                    for b in range(2):
                        k = 2 * i + b
                        ins = stt(xT[:, k, :], bank(i, b * T, T), mod2[:, l, 16 + k:17 + k], xT[:, k, :], ALU.mult, ALU.add)
                ins.then_inc(x_ready, 1)

            def candidates(t, lo, hi):
                top16(topv, topi, score[t], rep, lo, hi)
                tick(v.tensor_copy(topf[:, lo:hi, :], topi[:, lo:hi, :]))
                heads = slice(lo // 2, hi // 2)
                tv = topv.rearrange("p (h two) k -> p h two k", two=2)[:, heads]
                shape = [P, (hi - lo) // 2, TOPK, TOPK]
                tick(tt(cand[:, heads], tv[:, :, 0, :].unsqueeze(3).to_broadcast(shape),
                        tv[:, :, 1, :].unsqueeze(2).to_broadcast(shape), ALU.add))
                settle()
                tick(v.tensor_copy(dtop[:, lo:hi, 0:1], topf[:, lo:hi, 0:1]))
                tick(tt(dtop[:, lo:hi, 1:], topf[:, lo:hi, 1:], topf[:, lo:hi, 0:TOPK - 1], ALU.subtract))
                settle()

            def best_pairs(lo, hi):
                top16(bestv, posi[:].rearrange("p (h k) -> p h k", h=PH), cand.rearrange("p h a b -> p h (a b)"), rep2, lo, hi)

            def choose(l, t):
                tt(gsub, bestv, bestv[:, :, 0:1].to_broadcast([P, PH, TOPK]), ALU.subtract).then_inc(gsub_ready, 1)
                tick(v.tensor_copy(posf, posi[:]))
                settle()
                geb = ge.rearrange("p (a m) -> p a m", m=TOPK)
                ge4 = ge.rearrange("p (h k m) -> p h k m", h=PH, k=TOPK)
                tmpb = tmp.rearrange("p (a m) -> p a m", m=TOPK)
                tmp4 = tmp.rearrange("p (h k m) -> p h k m", h=PH, k=TOPK)
                dt4 = dtop.rearrange("p (h two) m -> p h two m", two=2)
                for half, (where, found) in enumerate(((posf, e1), (jrem, e2))):
                    tick(tt(geb, where.unsqueeze(2).to_broadcast([P, PICKS, TOPK]),
                            thr[:, half:half + 1, :].to_broadcast([P, PICKS, TOPK]), ALU.is_ge))
                    settle()
                    if half == 0:
                        tick(v.tensor_reduce(isum, geb, AX_X, ALU.add))
                    tick(tt(tmp4, ge4, dt4[:, :, half, :].unsqueeze(2).to_broadcast([P, PH, TOPK, TOPK]), ALU.mult))
                    settle()
                    tick(v.tensor_reduce(found, tmpb, AX_X, ALU.add))
                    if half == 0:
                        tick(stt(jrem, isum, -float(TOPK), posf, ALU.mult, ALU.add))
                    settle()
                tick(stt(e1, e1, float(KEYS), e2, ALU.mult, ALU.add))
                settle()
                v.tensor_copy(eidx[:, t, :], e1).then_inc(eidx_ready, 1)
                dve.wait_ge(gexp_ready, 2 * l + t + 1)
                tick(v.tensor_reduce(gsum[:, 0, :], gsub, AX_X, ALU.add))
                settle()
                tick(v.reciprocal(gsum[:, 1, :], gsum[:, 0, :]))
                settle()
                tick(tt(gate[:, t, :].rearrange("p (h k) -> p h k", h=PH), gsub,
                        gsum[:, 1, :].unsqueeze(2).to_broadcast([P, PH, TOPK]), ALU.mult))
                settle()

            def expert_dots(l, t, first, last):
                head0 = 32 * l + 8 * t + first
                with dve.Fori(0, last - first, 1) as it:
                    for j in range(TOPK):
                        dve.wait_ge(row_in[j], it * 16 + 16 * (head0 + 1))
                        v.tensor_tensor_reduce(out=rows[:, j, :], in0=rows[:, j, :], in1=h2tok[:, t, :], scale=1.0, scalar=0.0,
                                               op0=ALU.mult, op1=ALU.add, accum_out=dots16[:, j:j + 1]).then_inc(rows_free, 1)
                    dve.wait_ge(rows_free, it * TOPK + (SLOTS + TOPK * (head0 + 1)))
                    v.tensor_copy(dots[:, t, bass.ds(it * TOPK + first * TOPK, TOPK)], dots16).then_inc(dots_saved, 1)
                    dve.wait_ge(dots_saved, it + (head0 + 1))
                if last == PH:
                    v.memset(gsum[:, 0, :], 0.0).then_inc(dots_ready, 1)

            def expert_sum(l, t):
                head0 = 32 * l + 16 + 8 * t
                dve.wait_ge(gelu_ready, 2 * l + t + 1)
                tick(tt(wexp[:, t, :], wexp[:, t, :], gate[:, t, :], ALU.mult))
                tick(v.memset(yacc, 0.0))
                settle()
                with dve.Fori(0, PH, 1) as it:
                    v.tensor_copy(w16, wexp[:, t, bass.ds(it * TOPK, TOPK)]).then_inc(dots_saved, 1)
                    dve.wait_ge(dots_saved, it + (32 * l + 16 + 8 * t + 1))
                    for j in range(TOPK):
                        dve.wait_ge(row_in[j], it * 16 + 16 * (head0 + 1))
                        dve.wait_ge(rows_free, it * TOPK + (SLOTS + TOPK * head0 + j - 1))
                        stt(yacc[:, j % 2, :], rows[:, j, :], w16[:, j:j + 1], yacc[:, j % 2, :], ALU.mult, ALU.add) \
                            .then_inc(rows_free, 1)
                    dve.wait_ge(rows_free, it * TOPK + (SLOTS + TOPK * (head0 + 1)))
                tt(ytok[:, t, :], yacc[:, 0, :], yacc[:, 1, :], ALU.add).then_inc(ytok_ready, 1)
                dve.wait_ge(ytok_ready, 2 * l + t + 1)

            for l in range(2):
                norm(9 + 2 * l)
                attend(l)
                norm(10 + 2 * l)
                dve.wait_ge(h2t_done, l + 1)
                v.tensor_copy(h2tok.rearrange("p a b -> p (a b)"), psum[:, 4:8, :].rearrange("p a b -> p (a b)")).then_inc(h2t_ready, 1)
                for m in range(4):
                    dve.wait_ge(score_ready, 5 * l + m + 1)
                    candidates(0, 4 * m, 4 * m + 4)
                    best_pairs(2 * m, 2 * m + 2)
                choose(l, 0)
                dve.wait_ge(score_ready, 5 * l + 5)
                candidates(1, 0, 16)
                expert_dots(l, 0, 0, PH // 2)
                best_pairs(0, PH)
                choose(l, 1)
                expert_dots(l, 0, PH // 2, PH)
                expert_dots(l, 1, 0, PH)
                for t in range(TT):
                    expert_sum(l, t)
                for t in range(TT):
                    dve.wait_ge(yt_done, 2 * l + t + 1)
                    for k in range(KB):
                        ins = stt(xT[:, k, t * P:(t + 1) * P], bank(2 * t + k // 4, (k % 4) * P, P), mod2[:, l, 40 + k:41 + k],
                                  xT[:, k, t * P:(t + 1) * P], ALU.mult, ALU.add)
                ins.then_inc(x_ready, 1)

        @block.gpsimd
        def _(pool):
            g = nc.gpsimd
            done = [0]

            def each(ins):
                ins.then_inc(pool_step, 1)
                done[0] += 1
                pool.wait_ge(pool_step, done[0])

            each(g.memset(ones[:], 1.0))
            for m, start, op, base, step, mult in ((ident, 0.0, ALU.not_equal, 0, -1, 1), (flip, 0.0, ALU.not_equal, 1 - P, 1, 1),
                                                   (tri, 1.0, ALU.is_ge, 0, 1, -1), (trisuf, 1.0, ALU.is_ge, 0, -1, 1)):
                each(g.memset(m[:], start))
                each(g.affine_select(out=m[:], in_=m[:], compare_op=op, fill=1.0 - start, base=base, pattern=[[step, P]],
                                     channel_multiplier=mult))
            for i, (step, base) in enumerate(((TOPK, 0), (1, -TOPK))):
                each(g.iota(thr[:, i, :], pattern=[[step, TOPK]], base=base, channel_multiplier=0,
                            allow_small_or_imprecise_dtypes=True))
            each(g.memset(gate_in[:], 0.0))

            for b in range(NCH * (H // 4) * 2):
                c, jb = b // 16, (b // 2) % 8
                pool.wait_ge(expbc_ready, b + 1)
                e = eoff[:, b % 3, :].rearrange("p (i l) -> p i l", i=4)
                g.tensor_tensor(e, e, xbc[:, 20 + jb // 2, c * P:(c + 1) * P].unsqueeze(1).to_broadcast([P, 4, P]), ALU.mult) \
                    .then_inc(eoff_ready, 1)

            pool.wait_ge(x_ready, 4)
            pool.dma_start(rcnt, A["rcnt"].unsqueeze(0).to_broadcast([P, 4, T])).then_inc(rcnt_in, 16)
            pool.wait_ge(x_ready, 7)
            pool.dma_start(sgw, A["sgu_w"]).then_inc(sgw_in, 16)
            pool.dma_start(boh[0:BUCKETS + 1, :], A["bias_onehot"]).then_inc(boh_in, 16)
            pool.dma_start(relx[0:BUCKETS + 1, :], A["rel_bias"]).then_inc(relx_in, 16)
            pool.wait_ge(brow_ready, 1)
            pool.dma_start(A["bias_scratch"], brow[0:HEADS, :]).then_inc(brow_out, 16)
            pool.wait_ge(brow_out, 16)
            pool.dma_start(bias_t, bass.AP(A["bias_scratch"].tensor, 0, [[1, P], [BSTEP, HEADS], [1, T]])).then_inc(bias_in, 16)

            def gather(l, table, t, phase):
                head0 = 32 * l + 8 * phase
                pool.wait_ge(eidx_ready, 2 * l + t + 1)
                pool.wait_ge(keys_done, 5 * l + 5)
                with pool.Fori(0, PH // 2, 1) as it:
                    for hh in range(2):
                        g.tensor_copy(istage[:, hh, :], eidx[:, t, bass.ds(it * (2 * TOPK) + hh * TOPK, TOPK)]).then_inc(stage_set, 1)
                        for q in range(4):
                            n = head0 * 4 + hh * 4 + q
                            pool.wait_ge(gate_passed, it * 8 + (n + 1)) 
                            pool.wait_ge(stage_set, it * 2 + (head0 + hh + 1))
                            pool.wait_ge(rows_free, it * (2 * TOPK) + ((head0 + hh) * TOPK + 4 * q + 4))
                            g.tensor_tensor(gate_out[:], gate_in[:], gate_in[:], ALU.add).then_inc(gate_passed, 1)
                            for j in range(4 * q, 4 * q + 4):
                                pool.indirect_dma_start(out=rows[:, j, :], out_offset=None, in_=A[table],
                                                        in_offset=bass.IndirectOffsetOnAxis(ap=istage[:, hh, j:j + 1], axis=0)) \
                                    .then_inc(row_in[j], 16)

            g.tensor_tensor(gate_out[:], gate_in[:], gate_in[:], ALU.add).then_inc(gate_passed, 1)
            for l in range(2):
                for phase in range(4):
                    gather(l, f"peer_{'down' if phase < 2 else 'up'}{l}", phase % 2, phase)


def kernel(**inputs):
    import numpy as np
    import concourse.bacc as bacc
    from concourse.bass_utils import run_bass_kernel_spmd as run

    I = {k: np.asarray(v) for k, v in inputs.items()}

    def column(a):
        return np.ascontiguousarray(a).reshape(-1, P).T

    def pad64(a):
        return np.concatenate([a.reshape(64, 1), np.zeros((64, 1), np.float32)])

    parts = {
        "c": column(I["c"]), "c_ctx": column(I["c_ctx"]), "c2": column(I["c_2"]),
        "ada_b0": column(I["ada_b"][0]), "ada_b1": column(I["ada_b"][1]), "norm_g": column(I["norm_g"]),
        "conv_w": column(I["ssd_conv_w"][0]), "conv_b": column(I["ssd_conv_b"][0]), "ssd_ng": column(I["ssd_norm_g"][0]),
        "ssd_d": column(np.repeat(I["ssd_d"][0], HD)), "dt_bias": pad64(I["ssd_dt_bias"][0]), "a_log": pad64(I["ssd_a_log"][0]),
        "pool_b": column(I["pool_b"][0]), "pool_scale": column(I["pool_scale"][0]), "final_g": column(I["final_g"]),
        "ada_b2_0": column(I["b_ada_2"][0]), "ada_b2_1": column(I["b_ada_2"][1]),
        "n1g": column(I["norm1_g_2"]), "n2g": column(I["norm2_g_2"]),
        "qg": np.tile(I["q_norm_g_2"], (1, 2)).T, "kg": np.tile(I["k_norm_g_2"], (1, 2)).T,
        "conv_w2": column(I["conv_w_2"]), "out_g": column(I["out_norm_g_2"]),
    }
    cols = np.concatenate([parts[k] for k in COLS], axis=1)
    assert cols.shape == (P, N_COLS)

    def counts(n, w):
        pos = np.arange(n)
        return np.minimum(pos + (w - w // 2), n) - np.maximum(pos - w // 2, 0)

    rcnt = np.stack([1.0 / np.outer(counts(4, w), counts(64, w)).reshape(-1) for w in (2, 4, 8, 16)]).astype(np.float32)
    dist = 255 - np.arange(BSTEP)
    half = BUCKETS // 2
    dd = np.maximum(dist, 0)
    ratio = np.log(np.maximum(dd, 1).astype(np.float32) / np.float32(half)) / np.float32(np.log(MAX_DIST / half))
    large = np.minimum(half + (ratio * np.float32(BUCKETS - half)).astype(np.int32), BUCKETS - 1)
    bucket = np.where(dd < half, dd, large)
    ok = (dist >= 0) & (dist < WINDOW)
    onehot = np.zeros((BUCKETS + 1, BSTEP), np.float32)
    onehot[bucket[ok], np.arange(BSTEP)[ok]] = 1.0
    onehot[BUCKETS, ~ok] = NEG
    rel = np.concatenate([I["rel_bias_2"], np.ones((1, HEADS), np.float32)])

    def blocks(a):
        return np.ascontiguousarray(a[0].T.reshape(KB, P, T).transpose(1, 0, 2))

    arrays = {
        "xT": blocks(I["x"]), "hT": blocks(I["ctx"]), "cols": np.ascontiguousarray(cols),
        "ada_w": I["ada_w"], "ffn_w_gate": I["ffn_w_gate"], "ffn_w_up": I["ffn_w_up"], "ffn_w_down": I["ffn_w_down"],
        "ssd_w_in": I["ssd_w_in"][0], "ssd_w_out": I["ssd_w_out"][0], "pool_w": I["pool_w"][0],
        "w_ada2": I["w_ada_2"], "w_in2": I["w_in_2"], "w_out2": I["w_out_2"], "peer_wq": I["peer_wq_2"],
        "rcnt": rcnt, "bias_onehot": onehot, "rel_bias": rel, "sink": np.ascontiguousarray(I["attn_sink_2"].reshape(2, HEADS // 2, 2).transpose(0, 2, 1).reshape(2, HEADS)),
        "sgu_b": I["sgu_b_2"][None], "sgu_w": np.ascontiguousarray(I["sgu_w_2"].transpose(3, 0, 1, 2)),
    }
    for l in range(2):
        arrays[f"keys{l}"] = np.ascontiguousarray(I["peer_sub_keys_2"][l].reshape(16, KEYS, P).transpose(2, 0, 1))
        arrays[f"peer_down{l}"] = I["peer_down_2"][l]
        arrays[f"peer_up{l}"] = I["peer_up_2"][l]
    arrays = {k: np.ascontiguousarray(a) for k, a in arrays.items()}

    nc = bacc.Bacc("TRN2", target_bir_lowering=False, num_devices=1)
    A = {k: nc.dram_tensor(f"in_{k}", a.shape, F32, kind="ExternalInput").ap() for k, a in arrays.items()}
    A["bias_scratch"] = nc.dram_tensor("bias_scratch", (HEADS, BSTEP), F32, kind="Internal").ap()
    A["out"] = nc.dram_tensor("out", (P, KB, T), F32, kind="ExternalOutput").ap()
    program(nc, A)
    r = run(nc, [{f"in_{k}": a for k, a in arrays.items()}], core_ids=[0])
    out = np.asarray(r.results[0]["out"])
    return np.ascontiguousarray(out.transpose(1, 0, 2).reshape(D, T).T)[None]
```
